# Optimizing a Trainium2 kernel written in Bass

```python
import math
import jax, jax.numpy as jnp
from jax import lax
import numpy as np

D_MODEL = 1024
BATCH = 1
SEQ = 512
DEPTH = 2

CTX_LEN = 256
GRID_W = 64
MIX_WIDTH = D_MODEL

GLA_HEADS = 4
GLA_DV = MIX_WIDTH // 2 // GLA_HEADS
GLA_DK = GLA_DV // 2
GLA_RANK = 16
GLA_TAU = 16.0
GLA_CHUNK = 64
GLA_K_W = GLA_HEADS * GLA_DK
GLA_V_W = GLA_HEADS * GLA_DV

FOURIER_GROUPS = 4
FOURIER_WIDTH = MIX_WIDTH // 4

CONV_GROUPS = 4
CONV_WIDTH = MIX_WIDTH - GLA_V_W - FOURIER_WIDTH
CONV_K = 3

FFN_HIDDEN = -(-8 * D_MODEL // (3 * 256)) * 256
RMS_EPS = 1e-6
N_MOD = 6

STATE_COLS = GLA_K_W + GLA_V_W + 2 * GLA_RANK
IN_COLS = STATE_COLS + GLA_K_W + GLA_V_W + FOURIER_WIDTH + 3 * CONV_WIDTH
STATE_SPLITS = [GLA_K_W, GLA_K_W + GLA_V_W, GLA_K_W + GLA_V_W + GLA_RANK]
MAIN_SPLITS = [
    STATE_COLS,
    STATE_COLS + GLA_K_W,
    STATE_COLS + GLA_K_W + GLA_V_W,
    STATE_COLS + GLA_K_W + GLA_V_W + FOURIER_WIDTH,
    STATE_COLS + GLA_K_W + GLA_V_W + FOURIER_WIDTH + CONV_WIDTH,
    STATE_COLS + GLA_K_W + GLA_V_W + FOURIER_WIDTH + 2 * CONV_WIDTH,
]

kernel_name = "hybrid_gla_fourier_conv_dit_block"

def rmsnorm(x, g):
    xf = x.astype(jnp.float32)
    y = xf * lax.rsqrt(jnp.mean(xf * xf, axis=-1, keepdims=True) + RMS_EPS)
    return (y * g.astype(jnp.float32)).astype(x.dtype)

def modulate(h, shift, scale):
    return h * (1 + scale) + shift

def flip(t):
    return jnp.flip(t, axis=1)

def grid_pos_embed(n_tokens, dim, dtype):
    rows = n_tokens // GRID_W
    row = jnp.repeat(jnp.arange(rows, dtype=jnp.float32), GRID_W)
    col = jnp.tile(jnp.arange(GRID_W, dtype=jnp.float32), rows)
    quarter = dim // 4
    freqs = 1.0 / (10000.0 ** (jnp.arange(quarter, dtype=jnp.float32) / quarter))

    def enc(p):
        ang = p[:, None] * freqs[None, :]
        return jnp.concatenate([jnp.sin(ang), jnp.cos(ang)], axis=-1)

    return jnp.concatenate([enc(row), enc(col)], axis=-1).astype(dtype)

def gla_chunked(q, k, v, logg, s0, with_output=True):
    f32 = jnp.float32
    b, l, h, dk = k.shape
    dv = v.shape[-1]
    n = l // GLA_CHUNK
    k = k.astype(f32).reshape(b, n, GLA_CHUNK, h, dk)
    v = v.astype(f32).reshape(b, n, GLA_CHUNK, h, dv)
    g = jnp.cumsum(logg.astype(f32).reshape(b, n, GLA_CHUNK, h, dk), axis=2)
    g_last = g[:, :, -1]
    k_upd = k * jnp.exp(g_last[:, :, None] - g)
    ds = jnp.einsum('bnjhd,bnjhv->nbhdv', k_upd, v)
    decay = jnp.moveaxis(jnp.exp(g_last), 1, 0)

    def step(s, inp):
        dec, d = inp
        return dec[..., None] * s + d, s

    s_final, s_start = lax.scan(step, s0.astype(f32), (decay, ds))
    if not with_output:
        return None, s_final
    q = q.astype(f32).reshape(b, n, GLA_CHUNK, h, dk)
    g_mid = g[:, :, GLA_CHUNK // 2 - 1][:, :, None]
    scores = jnp.einsum('bnihd,bnjhd->bnhij', q * jnp.exp(g - g_mid), k * jnp.exp(g_mid - g))
    mask = jnp.tril(jnp.ones((GLA_CHUNK, GLA_CHUNK), dtype=bool))
    scores = jnp.where(mask, scores, 0.0)
    o_intra = jnp.einsum('bnhij,bnjhv->bnihv', scores, v)
    o_inter = jnp.einsum('bnihd,nbhdv->bnihv', q * jnp.exp(g), s_start)
    return (o_intra + o_inter).reshape(b, l, h, dv), s_final

def gla_state_inputs(p_state, w_dec_f, b_dec_f, w_dec_b, b_dec_b):
    k, v, lr_f, lr_b = jnp.split(p_state, STATE_SPLITS, axis=-1)
    b, l = k.shape[:2]
    k = k.reshape(b, l, GLA_HEADS, GLA_DK)
    v = v.reshape(b, l, GLA_HEADS, GLA_DV)
    logg_f = jax.nn.log_sigmoid((lr_f @ w_dec_f + b_dec_f).astype(jnp.float32)) / GLA_TAU
    logg_b = jax.nn.log_sigmoid((lr_b @ w_dec_b + b_dec_b).astype(jnp.float32)) / GLA_TAU
    return (k, v, logg_f.reshape(b, l, GLA_HEADS, GLA_DK), logg_b.reshape(b, l, GLA_HEADS, GLA_DK))

def zero_state(b):
    return jnp.zeros((b, GLA_HEADS, GLA_DK, GLA_DV), jnp.float32)

def fourier_mix(u):
    b, l, w = u.shape
    uf = u.astype(jnp.float32).reshape(b, l, FOURIER_GROUPS, w // FOURIER_GROUPS)
    y = jnp.fft.fft2(uf, axes=(1, 3), norm="ortho").real
    return y.reshape(b, l, w).astype(u.dtype)

def short_conv(b_gate, c_gate, u, conv_w, conv_b):
    z = c_gate * u
    zp = jnp.pad(z, ((0, 0), (1, 1), (0, 0)))
    y = conv_w[0] * zp[:, :-2] + conv_w[1] * zp[:, 1:-1] + conv_w[2] * zp[:, 2:] + conv_b
    return b_gate * y

def context_states(h, w_in, w_dec_f, b_dec_f, w_dec_b, b_dec_b):
    p_state = h @ w_in[:, :STATE_COLS]
    k, v, gf, gb = gla_state_inputs(p_state, w_dec_f, b_dec_f, w_dec_b, b_dec_b)
    s0 = zero_state(h.shape[0])
    _, s_f = gla_chunked(None, k, v, gf, s0, with_output=False)
    _, s_b = gla_chunked(None, flip(k), flip(v), flip(gb), s0, with_output=False)
    return s_f, s_b

def token_mixer(h, w_in, w_dec_f, b_dec_f, w_dec_b, b_dec_b, gla_norm_w, conv_w, conv_b, w_out, s_f0, s_b0):
    b, l, _ = h.shape
    p = h @ w_in
    p_state, q, r, u_four, b_gate, c_gate, u_conv = jnp.split(p, MAIN_SPLITS, axis=-1)
    k, v, gf, gb = gla_state_inputs(p_state, w_dec_f, b_dec_f, w_dec_b, b_dec_b)
    q = q.reshape(b, l, GLA_HEADS, GLA_DK) * (GLA_DK ** -0.5)
    o_f, s_f = gla_chunked(q, k, v, gf, s_f0)
    o_b, s_b = gla_chunked(flip(q), flip(k), flip(v), flip(gb), s_b0)
    o = o_f + flip(o_b)
    o = o * lax.rsqrt(jnp.mean(o * o, axis=-1, keepdims=True) + RMS_EPS)
    o = o * gla_norm_w.astype(jnp.float32).reshape(GLA_HEADS, GLA_DV)
    y_gla = o.reshape(b, l, GLA_V_W).astype(h.dtype) * jax.nn.silu(r)
    y_four = fourier_mix(u_four)
    y_conv = short_conv(b_gate, c_gate, u_conv, conv_w, conv_b)
    y = jnp.concatenate([y_gla, y_four, y_conv], axis=-1) @ w_out
    return y, s_f, s_b

def ffn_sublayer(x, shift, scale, gate, g_pre, g_post, w_ffn_in, w_ffn_out):
    h = modulate(rmsnorm(x, g_pre), shift, scale)
    a, u = jnp.split(h @ w_ffn_in, 2, axis=-1)
    y = (jax.nn.silu(a) * u) @ w_ffn_out
    return x + gate * rmsnorm(y, g_post)

def setup_inputs(seed: int = 0) -> dict:
    key = jax.random.key(seed)
    ks = jax.random.split(key, 24)
    f32 = jnp.float32
    D = D_MODEL

    def nrm(k, shape, scale):
        return jax.random.normal(k, shape, f32) * scale

    def gain(k, shape):
        return 1.0 + 0.05 * jax.random.normal(k, shape, f32)

    return {
        "x": nrm(ks[0], (BATCH, SEQ, D), 1.0),
        "c": nrm(ks[1], (BATCH, D), 1.0),
        "ctx": nrm(ks[2], (BATCH, CTX_LEN, D), 1.0),
        "c_ctx": nrm(ks[3], (D,), 1.0),
        "w_mod": nrm(ks[4], (DEPTH, D, N_MOD * D), 0.5 * D ** -0.5),
        "b_mod": nrm(ks[5], (DEPTH, N_MOD * D), 0.02),
        "g_mix_pre": gain(ks[6], (DEPTH, D)),
        "g_mix_post": gain(ks[7], (DEPTH, D)),
        "g_ffn_pre": gain(ks[8], (DEPTH, D)),
        "g_ffn_post": gain(ks[9], (DEPTH, D)),
        "w_in": nrm(ks[10], (DEPTH, D, IN_COLS), D ** -0.5),
        "w_dec_f": nrm(ks[11], (DEPTH, GLA_RANK, GLA_K_W), GLA_RANK ** -0.5),
        "b_dec_f": nrm(ks[12], (DEPTH, GLA_K_W), 0.1),
        "w_dec_b": nrm(ks[13], (DEPTH, GLA_RANK, GLA_K_W), GLA_RANK ** -0.5),
        "b_dec_b": nrm(ks[14], (DEPTH, GLA_K_W), 0.1),
        "gla_norm_w": gain(ks[15], (DEPTH, GLA_V_W)),
        "conv_w": nrm(ks[16], (DEPTH, CONV_K, CONV_WIDTH), CONV_K ** -0.5),
        "conv_b": nrm(ks[17], (DEPTH, CONV_WIDTH), 0.02),
        "w_out": nrm(ks[18], (DEPTH, MIX_WIDTH, D), MIX_WIDTH ** -0.5),
        "w_ffn_in": nrm(ks[19], (DEPTH, D, 2 * FFN_HIDDEN), D ** -0.5),
        "w_ffn_out": nrm(ks[20], (DEPTH, FFN_HIDDEN, D), FFN_HIDDEN ** -0.5),
    }

def reference(x, c, ctx, c_ctx, w_mod, b_mod, g_mix_pre, g_mix_post, g_ffn_pre, g_ffn_post,
              w_in, w_dec_f, b_dec_f, w_dec_b, b_dec_b, gla_norm_w, conv_w, conv_b, w_out,
              w_ffn_in, w_ffn_out):
    n_lat = x.shape[1]
    x = x + grid_pos_embed(n_lat, x.shape[-1], x.dtype)[None]
    xc = ctx
    for i in range(DEPTH):
        last = i == DEPTH - 1
        mod_lat = jnp.split((jax.nn.silu(c) @ w_mod[i] + b_mod[i])[:, None, :], N_MOD, axis=-1)
        mod_ctx = jnp.split((jax.nn.silu(c_ctx) @ w_mod[i] + b_mod[i])[None, None, :], N_MOD, axis=-1)
        mix_w = (w_in[i], w_dec_f[i], b_dec_f[i], w_dec_b[i], b_dec_b[i], gla_norm_w[i], conv_w[i], conv_b[i], w_out[i])

        h_lat = modulate(rmsnorm(x, g_mix_pre[i]), mod_lat[0], mod_lat[1])
        h_ctx = modulate(rmsnorm(xc, g_mix_pre[i]), mod_ctx[0], mod_ctx[1])
        if last:
            s_f, s_b = context_states(h_ctx, w_in[i], w_dec_f[i], b_dec_f[i], w_dec_b[i], b_dec_b[i])
        else:
            s0 = zero_state(xc.shape[0])
            y_ctx, s_f, s_b = token_mixer(h_ctx, *mix_w, s0, s0)
            xc = xc + mod_ctx[2] * rmsnorm(y_ctx, g_mix_post[i])
            xc = ffn_sublayer(xc, mod_ctx[3], mod_ctx[4], mod_ctx[5], g_ffn_pre[i], g_ffn_post[i], w_ffn_in[i], w_ffn_out[i])

        y_lat, _, _ = token_mixer(h_lat, *mix_w, s_f, s_b)
        x = x + mod_lat[2] * rmsnorm(y_lat, g_mix_post[i])
        x = ffn_sublayer(x, mod_lat[3], mod_lat[4], mod_lat[5], g_ffn_pre[i], g_ffn_post[i], w_ffn_in[i], w_ffn_out[i])
    return x


_drawn_inputs = setup_inputs


def setup_inputs(seed=0):
    import zlib

    import numpy as np

    out = dict(_drawn_inputs(seed))
    spreads = {}
    factors = {'ctx': 2.79,
     'c_ctx': 4.06,
     'g_mix_post': 3.214,
     'g_ffn_post': 3.18,
     'b_dec_f': 4.914,
     'b_dec_b': 4.862,
     'gla_norm_w': 5.357,
     'conv_b': 8.0}
    for name, (base, spread) in spreads.items():
        noise = np.random.default_rng([zlib.crc32(name.encode()), seed]).standard_normal(out[name].shape)
        drawn = base * np.exp(spread * noise) if base else spread * noise
        out[name] = __import__('jax').numpy.asarray(drawn.astype(out[name].dtype))
    for name, factor in factors.items():
        out[name] = (out[name] * factor).astype(out[name].dtype)
    return out
```

```python
from contextlib import ExitStack, nullcontext

import numpy as np

import concourse.bass as bass
from concourse import mybir
from concourse.alu_op_type import AluOpType as ALU

F32 = mybir.dt.float32
F32R = mybir.dt.float32r
I32 = mybir.dt.int32
ACT = mybir.ActivationFunctionType

P = 128
DEPTH, D, SEQ, CTX = 2, 1024, 512, 256
TOK = SEQ + CTX
KT = D // P
TT_ALL, TT_LAT = TOK // P, SEQ // P
HEADS, DK, DV, RANK, CHUNK = 4, 64, 128, 16, 64
HID = 2816 // P
BLOCKS = (8, 8, 6)
EPS = 1e-6
LN_SET = "natural_log_exp_and_others"

KW, VW, FW = HEADS * DK, HEADS * DV, 256
C_LR = KW + VW
C_Q = C_LR + 2 * RANK
C_R = C_Q + KW
C_F = C_R + VW
C_B, C_C, C_U = C_F + FW, C_F + 2 * FW, C_F + 3 * FW
W_IN = ([("lr", 0, C_LR)] + [("k", j, j * P) for j in range(2)] + [("v", j, KW + j * P) for j in range(4)]
        + [("r", j, C_R + j * P) for j in range(4)] + [("q", j, C_Q + j * P) for j in range(2)]
        + [("f", j, C_F + j * P) for j in range(2)] + [("c", j, C_C + j * P) for j in range(2)]
        + [("u", j, C_U + j * P) for j in range(2)] + [("b", j, C_B + j * P) for j in range(2)])
STATE_NAMES = ("lr", "k", "v")
STEPS = [(0, 4), (1, 5), (0, 5), (1, 4), (0, 0), (1, 3), (0, 1), (1, 2), (0, 2), (1, 1), (0, 3), (1, 0)]
PB, PG, PCW, PCB, PGN, PCOLS = 0, 48, 80, 86, 88, 92


def build_order():
    order = []
    order.append(("mods", 0, 0, 16))
    order.append(("prenorm", 0, 0))
    mod = [16]

    def mod_one():
        if mod[0] < 48:
            order.append(("mod", 0, mod[0]))
            mod[0] += 1

    for L in range(DEPTH):
        z, t, s, d = list(range(TT_ALL)), list(range(6)), list(range(12)), list(range(12))
        for x, (name, j, _) in enumerate(W_IN):
            order.append(("proj", L, x))
            if L == 0:
                mod_one()
            if 1 <= x <= 3:
                order.append(("z", L, z.pop(0)))
                order.append(("z", L, z.pop(0)))
            if 3 <= x <= 8:
                order.append(("turn", L, t.pop(0)))
            if x >= 10:
                if s:
                    order.append(("suffix", L, s.pop(0)))
                if x >= 11 and d:
                    order.append(("dstate", L, d.pop(0)))
        while d:
            if s:
                order.append(("suffix", L, s.pop(0)))
            order.append(("dstate", L, d.pop(0)))
        tiles = (4, 5, 0, 1, 2, 3) if L == 0 else (0, 1, 2, 3)
        for tt in tiles:
            order.append(("four", L, tt))
            if L == 0:
                mod_one()
        for g in (0, 1):
            order.append(("gate", L, tiles[0], g))
        for s4 in range(4):
            order.append(("dft", L, s4))
            if L == 0:
                mod_one()
        if L == 0:
            order.append(("dft", L, 4))
            mod_one()
            order.append(("modend", 0))
        for a, tt in enumerate(tiles):
            order.append(("score", L, tt))
            if a + 1 < len(tiles):
                for g in (0, 1):
                    order.append(("gate", L, tiles[a + 1], g))
            order.append(("o", L, tt))
            if a:
                order.append(("msq", L, tiles[a - 1]))
        order.append(("msq", L, tiles[-1]))
        order.append(("wout", L))
        order.append(("postnorm", L, 0))
        order.append(("prenorm", L, 1))
        first = 0
        for b, nb in enumerate(BLOCKS):
            order.append(("ffn_in", L, b, first))
            order.append(("ffn_out", L, b))
            first += nb
        if L == 0:
            order.append(("mods", 1, 44, 4))
        order.append(("postnorm", L, 1))
        if L == 0:
            order.append(("prenorm", 1, 0))
    return order


ORDER = build_order()


def chunks_of(e):
    kind, L = e[0], e[1]
    if kind == "mods":
        return [("mod", L, m) for m in range(e[2], e[2] + e[3])]
    if kind == "mod":
        return [("mod", L, e[2])]
    if kind == "proj":
        return [("in", L, W_IN[e[2]][2])]
    if kind == "dft":
        return [("dft", e[2])]
    if kind == "wout":
        return [("out", L, m) for m in range(KT)]
    if kind == "ffn_in":
        out = []
        for p in range(e[3], e[3] + BLOCKS[e[2]]):
            out += [("fin", L, p), ("fin", L, HID + p)]
            if L == 0:
                out += [("mod", 1, 2 * p), ("mod", 1, 2 * p + 1)]
        return out
    if kind == "ffn_out":
        first = sum(BLOCKS[:e[2]])
        return [("fout", L, m, first, BLOCKS[e[2]]) for m in range(KT)]
    return []


def tokens(L, name=None):
    return TOK if L == 0 or name in STATE_NAMES else SEQ


def segments(T):
    return [(0, SEQ, 0)] + ([(SEQ, TOK, 1)] if T > SEQ else [])


class Plan:

    def __init__(self):
        self.n0, self.full, self.before, self.evac, self.acc = {}, {}, {}, {}, {}
        n, used, kinds, copies, acc = 0, dict.fromkeys(("A0", "A1", "N0", "N1", "G0", "G1"), 0), {}, {}, 0
        g = 0
        for e in ORDER:
            kind, L = e[0], e[1]
            self.n0[e] = n
            n += len(chunks_of(e))
            units = []
            if kind == "mods" and e[2] == 0:
                units = ["G0"]
            elif kind == "proj":
                units = [f"A{acc % 2}"]
                self.acc[e] = acc % 2
                acc += 1
            elif kind in ("z", "turn", "four"):
                if kind == "turn":
                    units = ["G0", "G1"]
                else:
                    units = [f"G{g % 2}"]
                    g += 1
            elif kind == "mod" and e[2] == 16:
                units = ["N0"]
            elif kind == "suffix":
                units = ["N1"]
            elif kind == "dstate":
                units = ["G0", "G1"]
            elif kind == "gate":
                units = [f"G{e[3]}"]
            elif kind == "dft" and e[2] == 0:
                units = ["A0", "A1"]
            elif kind == "score":
                units = ["N0", "N1"]
            elif kind == "o":
                units = [f"A{self.tile_turn(L, e[2])}"]
            elif kind == "wout":
                units = []
                self.acc[e] = (used["A0"], used["A1"])
                used["A0"] += KT // 2
                used["A1"] += KT // 2
            elif kind == "ffn_in":
                self.acc[e] = (used["A0"], used["A1"])
                used["A0"] += BLOCKS[e[2]]
                used["A1"] += BLOCKS[e[2]]
                if L == 0 and e[2] == 0:
                    units = ["G0"]
            elif kind == "ffn_out":
                self.acc[e] = (used["A0"], used["A1"])
                used["A0"] += KT // 2
                used["A1"] += KT // 2
            elif kind in ("postnorm", "prenorm"):
                units = ["N0"] + (["N1"] if L == 0 or (kind == "prenorm" and e[2] == 0) else [])
            self.before[e] = [(u, used[u]) for u in units]
            for u in units:
                used[u] += 1
            fk = kind
            if kind in ("mods", "mod", "modend", "proj", "dft", "prenorm", "wout", "ffn_in", "ffn_out"):
                fk = None
            if fk:
                kinds[fk] = kinds.get(fk, 0) + 1
                self.full[e] = kinds[fk]
        self.total = n

    @staticmethod
    def tile_turn(L, tt):
        tiles = (4, 5, 0, 1, 2, 3) if L == 0 else (0, 1, 2, 3)
        return tiles.index(tt) % 2


PLAN = Plan()
N_MOD0 = 16
N_CHUNKS = PLAN.total


def norm_tokens(e):
    return TOK if e[1] == 0 or (e[0] == "prenorm" and e[2] == 0) else SEQ


def bass_hybrid_block(nc: bass.Bass, stream, xT, posT, cols, wdec, masks, mats, wide, x_keep, out):
    with ExitStack() as ctx:
        def sb(name, shape, dt=F32, stack=None):
            return (stack or ctx).enter_context(nc.sbuf_tensor(name, shape, dt))

        def sem(name):
            return ctx.enter_context(nc.semaphore(name))

        h_hi = sb("h_hi", [P, KT, TOK], F32R)
        h_lo = sb("h_lo", [P, KT, TOK], F32R)
        raw = sb("raw", [P, 4, 1024])
        w_hi = sb("w_hi", [P, 2, 1024], F32R)
        w_lo = sb("w_lo", [P, 2, 1024], F32R)
        par = sb("par", [P, DEPTH * PCOLS + 16])
        wd = sb("wd", [33, DEPTH, 512])
        mask = sb("mask", [P, 2, P], I32)
        mat = sb("mat", [P, 4 * P + 2 * P + 2])
        chan = sb("chan", [P, 2 * P])
        one_d = sb("one_d", [P, P])
        one_v = sb("one_v", [P, P])
        ident = sb("ident", [P, P])
        eps = sb("eps", [P, 1])
        csil = sb("csil", [P, 2, KT])
        c4 = sb("c4", [P, KT, 4], F32R)
        mraw = sb("mraw", [P, 48, 4])
        modT = sb("modT", [P, 48, 2])
        coef = sb("coef", [P, DEPTH, 6, KT, 2])
        dec = sb("dec", [P, 12, 4])

        mix, ffn = ExitStack(), ExitStack()
        with ffn:
            y = sb("y", [P, KT, TOK], stack=ffn)
            g_hi = sb("g_hi", [P, 8, TOK], F32R, stack=ffn)
            g_lo = sb("g_lo", [P, 8, TOK], F32R, stack=ffn)
            sil = sb("sil", [P, 2, TOK], stack=ffn)
            rstd = sb("rstd", [P, TOK], stack=ffn)
            ssq = sb("ssq", [P, TOK], stack=ffn)
            sqb = sb("sqb", [P, 2, TOK], stack=ffn)
            x = sb("x", [P, KT, TOK], stack=ffn)
        with mix:
            kT = sb("kT", [P, 2, TOK], stack=mix)
            qT = sb("qT", [P, 2, TOK], stack=mix)
            ktok = sb("ktok", [P, TT_ALL, KW], stack=mix)
            vtok = sb("vtok", [P, TT_ALL, VW], stack=mix)
            ls = sb("ls", [P, TT_ALL, 2 * KW], stack=mix)
            S = sb("S", [P, 2, 12, 2, DV], stack=mix)
            r_s = sb("r_s", [P, 4, TOK], stack=mix)
            early, late = ExitStack(), ExitStack()
            with early:
                lrT = sb("lrT", [33, TOK], stack=early)
                vst = sb("vst", [P, 2, TOK], stack=early)
                eu = sb("eu", [P, 2, KW], stack=early)
                zs = sb("zs", [P, 2, 2 * KW], stack=early)
                cgz = sb("cgz", [P, 2, TOK], stack=early)
                bg = sb("bg", [P, 2, TOK], stack=early)
                cv = sb("cv", [P, TOK], stack=early)
                uF = sb("uF", [P, 2, TOK], stack=early)
            with late:
                E = sb("E", [P, 2, 2, 3, 2, P], stack=late)
                Pm = sb("Pm", [P, 2, 2, 2, 2, P], stack=late)
                osq = sb("osq", [P, 2, 4 * P], stack=late)
                rb = sb("rb", [P, 2, 4, P], stack=late)

        def ps(name, n):
            return ctx.enter_context(nc.psum_tensor(name, [P, n], F32))

        A = [ps("A0", 1024), ps("A1", 1024)]
        N = ps("N", 1024)
        G = [ps("G0", 512), ps("G1", 512)]

        raw_in = [sem(f"raw_in{j}") for j in range(4)]
        hi_done, lo_first, lo_done, chunk_used = sem("hi_done"), sem("lo_first"), sem("lo_done"), sem("chunk_used")
        free = {u: sem(f"free_{u}") for u in ("A0", "A1", "N0", "N1", "G0", "G1")}
        full = {k: sem(f"full_{k}") for k in
                ("z", "turn", "suffix", "dstate", "four", "gate", "score", "o", "msq", "postnorm")}
        consts_in, x_in, pos_in = sem("consts_in"), sem("x_in"), sem("pos_in")
        x_kept, x_back, out_sent = sem("x_kept"), sem("x_back"), sem("out_sent")
        consts_set = sem("consts_set")
        c_ready, csil_ready, c4hi_ready = sem("c_ready"), sem("csil_ready"), sem("c4hi_ready")
        lr_ones = sem("lr_ones")
        zneg_ready, zln_ready, ku_ready = sem("zneg_ready"), sem("zln_ready"), sem("ku_ready")
        ab_hi, four_hi = sem("ab_hi"), sem("four_hi")
        conv_f, conv_hi, conv_ready = sem("conv_f"), sem("conv_hi"), sem("conv_ready")
        qk_ready = sem("qk_ready")
        osq_ready, orstd_ready, yg_ready, yhi_ready, ylo_ready = (
            sem("osq_ready"), sem("orstd_ready"), sem("yg_ready"), sem("yhi_ready"), sem("ylo_ready"))
        ssq_ready, rstd_ready, xnew_ready, sq_ready, sq_used = (
            sem("ssq_ready"), sem("rstd_ready"), sem("xnew_ready"), sem("sq_ready"), sem("sq_used"))
        haff_ready, hhi_ready, hlo_ready = sem("haff_ready"), sem("hhi_ready"), sem("hlo_ready")
        ghi_ready, g_ready = sem("ghi_ready"), sem("g_ready")
        dve_step, act_step = sem("dve_step"), sem("act_step")

        def col(L, at, n=1):
            return par[:, L * PCOLS + at:L * PCOLS + at + n]

        def tiles_of(L):
            return (4, 5, 0, 1, 2, 3) if L == 0 else (0, 1, 2, 3)

        def turn(L, tt):
            return tiles_of(L).index(tt) % 2

        def nth(L, tt):
            return 6 * L + tiles_of(L).index(tt)

        def lo_wait(eng, n, plus=0):
            if n < N_MOD0:
                eng.wait_ge(lo_first, n + 1)
            else:
                eng.wait_ge(lo_done, n - N_MOD0 + 1 + plus)

        def read_out(eng, e):
            for u, before in PLAN.before[e]:
                eng.wait_ge(free[u], before + 1)

        def proj(L, name, j):
            return ("proj", L, [w[:2] for w in W_IN].index((name, j)))

        def pre_no(L, which):
            return 2 * L + which

        def unit_of(e):
            u = PLAN.before[e][0][0]
            return G[int(u[1])][:, :]

        def o_at(b, h):
            pr, hp = divmod(h, 2)
            return A[b][:, hp * 512 + pr * P:hp * 512 + (pr + 1) * P]

        def o_all(b, mean):
            return A[b][:, :].rearrange("p (q m r) -> p q m r", q=2, m=2)[:, :, mean, :]

        def y_all(h, tt):
            return h[:, 0:4, tt * P:(tt + 1) * P].rearrange("p (r q) t -> p q r t", q=2)

        block = ctx.enter_context(nc.Block())

        @block.sync
        def _(sp):
            for n in range(4 + N_MOD0):
                if n >= 4:
                    lo_wait(sp, n - 4)
                sp.dma_start(raw[:, n % 4, :], stream[n]).then_inc(raw_in[n % 4], 16)
            first = 4 + N_MOD0
            rounds = (N_CHUNKS - first) // 4
            with sp.Fori(0, rounds, 1) as i:
                for j in range(4):
                    sp.wait_ge(lo_done, 4 * i + (j + 1))
                    sp.dma_start(raw[:, (first + j) % 4, :], stream[4 * i + (first + j)]).then_inc(raw_in[(first + j) % 4], 16)
            for n in range(first + 4 * rounds, N_CHUNKS):
                lo_wait(sp, n - 4)
                sp.dma_start(raw[:, n % 4, :], stream[n]).then_inc(raw_in[n % 4], 16)

        @block.gpsimd
        def _(pool):
            def low(n, i=None):
                pool.wait_ge(hi_done, n + 1 if i is None else 4 * i + (n + 1))
                pool.tensor_tensor(w_lo[:, n % 2, :], raw[:, n % 4, :], w_hi[:, n % 2, :].bitcast(F32),
                                   ALU.subtract).then_inc(lo_done, 1)

            rounds = (N_CHUNKS - N_MOD0) // 4
            with pool.Fori(0, rounds, 1) as i:
                for j in range(4):
                    low(N_MOD0 + j, i)
            for n in range(N_MOD0 + 4 * rounds, N_CHUNKS):
                low(n)

        @block.tensor
        def _(pe):
            def unit_free(e):
                for u, before in PLAN.before[e]:
                    if before:
                        pe.wait_ge(free[u], before)

            def split_matmul(dst, n, T, k, src, first, last):
                s, (hi, lo) = n % 2, src
                wh, wl = w_hi[:, s, k * P:(k + 1) * P], w_lo[:, s, k * P:(k + 1) * P]
                for a, b, p in ((wh, hi, 0), (wh, lo, 1), (wl, hi, 2)):
                    for t0, t1, _ in segments(T):
                        m = pe.matmul(dst[:, t0:t1], a, b[:, k, t0:t1], start=(first and p == 0), stop=(last and p == 2))
                return m

            def project(dst, n, T, src, K=KT):
                for k in range(K):
                    m = split_matmul(dst, n, T, k, src, k == 0, k == K - 1)
                m.then_inc(chunk_used, 1)

            def mod_matmul(dst, n):
                for k in range(KT):
                    for w in (w_hi, w_lo):
                        m = pe.matmul(dst, w[:, n % 2, k * P:(k + 1) * P], c4[:, k, :],
                                      start=(k == 0 and w is w_hi), stop=(k == KT - 1 and w is w_lo))
                m.then_inc(chunk_used, 1)
                return m

            H = (h_hi, h_lo)
            pe.wait_ge(consts_set, 1)
            pe.wait_ge(consts_in, 16 * 8)
            for e in ORDER:
                kind, L = e[0], e[1]
                n0 = PLAN.n0[e]
                if kind == "mods":
                    unit_free(e)
                    pe.wait_ge(c_ready, 1)
                    for m in range(e[3]):
                        lo_wait(pe, n0 + m)
                        mod_matmul(G[0][:, 4 * (e[2] + m):4 * (e[2] + m) + 4], n0 + m)
                elif kind == "mod":
                    unit_free(e)
                    lo_wait(pe, n0)
                    mod_matmul(N[:, 4 * e[2]:4 * e[2] + 4], n0)
                elif kind == "proj":
                    name, j, _ = W_IN[e[2]]
                    unit_free(e)
                    lo_wait(pe, n0)
                    if e[2] == 0:
                        for k in range(KT):
                            pe.wait_ge(hlo_ready, KT * pre_no(L, 0) + k + 1)
                            m = split_matmul(A[PLAN.acc[e]], n0, tokens(L, name), k, H, k == 0, k == KT - 1)
                        m.then_inc(chunk_used, 1)
                    else:
                        project(A[PLAN.acc[e]], n0, tokens(L, name), H)
                elif kind == "z":
                    tt = e[2]
                    unit_free(e)
                    read_out(pe, proj(L, "lr", 0))
                    pe.wait_ge(lr_ones, L + 1)
                    pe.matmul(unit_of(e), lrT[0:33, tt * P:(tt + 1) * P], wd[0:33, L, :],
                              start=True, stop=True).then_inc(full["z"], 1)
                elif kind == "turn":
                    unit_free(e)
                    j = e[2]
                    src = kT[:, j, :] if j < 2 else vst[:, j % 2, :]
                    read_out(pe, proj(L, *(("k", j) if j < 2 else ("v", j - 2))))
                    for tt in range(TT_ALL):
                        m = pe.transpose(G[tt // 4][:, (tt % 4) * P:(tt % 4 + 1) * P], src[:, tt * P:(tt + 1) * P], ident[:, :])
                    m.then_inc(full["turn"], 1)
                elif kind == "suffix":
                    g, tt = STEPS[e[2]]
                    unit_free(e)
                    read_out(pe, ("z", L, tt))
                    pe.matmul(N[:, 512:512 + KW], mat[:, 512 + g * P:512 + (g + 1) * P], ls[:, tt, g * KW:(g + 1) * KW],
                              start=True, stop=True)
                    for pr in range(2):
                        m = pe.matmul(N[:, 768 + 2 * pr:770 + 2 * pr], ls[:, tt, g * KW + pr * P:g * KW + (pr + 1) * P],
                                      mat[:, 768:770], start=True, stop=True)
                    m.then_inc(full["suffix"], 1)
                elif kind == "dstate":
                    g, tt = STEPS[e[2]]
                    unit_free(e)
                    pe.wait_ge(ku_ready, 12 * L + e[2] + 1)
                    if e[2] == 0:
                        read_out(pe, ("turn", L, 5))
                    for c in range(2):
                        for pr in range(2):
                            for hp in range(2):
                                h, row = 2 * pr + hp, slice(c * 64, c * 64 + 64)
                                m = pe.matmul(G[c][hp * 64:hp * 64 + 64, pr * DV:(pr + 1) * DV],
                                              eu[row, g, h * DK:(h + 1) * DK], vtok[row, tt, h * DV:(h + 1) * DV],
                                              start=True, stop=True)
                    m.then_inc(full["dstate"], 1)
                elif kind == "four":
                    tt = e[2]
                    unit_free(e)
                    read_out(pe, proj(L, "f", 0))
                    read_out(pe, proj(L, "f", 1))
                    for ch in range(2):
                        m = pe.matmul(unit_of(e)[:, ch * 256:(ch + 1) * 256], uF[:, ch, tt * P:(tt + 1) * P], chan[:, :],
                                      start=True, stop=True)
                    m.then_inc(full["four"], 1)
                elif kind == "dft":
                    unit_free(e)
                    lo_wait(pe, n0)
                    if e[2] == 0:
                        for tt in tiles_of(L)[-2:]:
                            read_out(pe, ("four", L, tt))
                    s = n0 % 2
                    ab = [t[:, 0:4, :].rearrange("p a b -> p (a b)") for t in H]
                    ctx_part = e[2] == 4
                    tts = (4, 5) if ctx_part else (e[2],)
                    w = CTX if ctx_part else SEQ
                    for ch in range(2):
                        dst = A[ch][:, SEQ:TOK] if ctx_part else A[ch][:, 0:SEQ]
                        for a, tt in enumerate(tts):
                            for part in range(2):
                                lhs = [t[:, tt * 512 + ch * 256 + part * P:tt * 512 + ch * 256 + (part + 1) * P] for t in ab]
                                o = (2 * a + part) * w
                                first = part == 0 and (a == 0 if ctx_part else e[2] == 0)
                                last = part == 1 and (a == 1 if ctx_part else e[2] == 3)
                                for p, (l, r) in enumerate(((lhs[0], w_hi), (lhs[0], w_lo), (lhs[1], w_hi))):
                                    m = pe.matmul(dst, l, r[:, s, o:o + w], start=(first and p == 0), stop=(last and p == 2))
                    m.then_inc(chunk_used, 1)
                elif kind == "gate":
                    tt, g = e[2], e[3]
                    unit_free(e)
                    read_out(pe, ("z", L, tt))
                    for pr in range(2):
                        m = pe.matmul(G[g][:, pr * 256:(pr + 1) * 256], ls[:, tt, g * KW + pr * P:g * KW + (pr + 1) * P],
                                      mat[:, g * 256:(g + 1) * 256], start=True, stop=True)
                    m.then_inc(full["gate"], 1)
                elif kind == "score":
                    tt = e[2]
                    b = turn(L, tt)
                    unit_free(e)
                    pe.wait_ge(qk_ready, 2 * (nth(L, tt) + 1))
                    for g in range(2):
                        for pr in range(2):
                            for hp in range(2):
                                row = slice(hp * 64, hp * 64 + 64)
                                o = hp * 512 + (g * 2 + pr) * P
                                m = pe.matmul(N[:, o:o + P], E[row, b, g, 1, pr, :], E[row, b, g, 0, pr, :], start=True, stop=True)
                    m.then_inc(full["score"], 1)
                elif kind == "o":
                    tt = e[2]
                    b = turn(L, tt)
                    unit_free(e)
                    read_out(pe, ("score", L, tt))
                    read_out(pe, ("dstate", L, 11))
                    for h in range(HEADS):
                        pr, hp = divmod(h, 2)
                        row = slice(hp * 64, hp * 64 + 64)
                        for g in range(2):
                            pe.matmul(o_at(b, h), vtok[:, tt, h * DV:(h + 1) * DV], Pm[:, b, hp, g, pr, :],
                                      start=(g == 0), stop=False)
                        for g in range(2):
                            for c in range(2):
                                m = pe.matmul(o_at(b, h)[:, c * 64:c * 64 + 64], S[row, g, 2 * tt + c, pr, :],
                                              E[row, b, g, 2, pr, c * 64:c * 64 + 64], start=False, stop=(g == 1 and c == 1))
                    m.then_inc(full["o"], 1)
                elif kind == "msq":
                    b = turn(L, e[2])
                    pe.wait_ge(osq_ready, nth(L, e[2]) + 1)
                    for hp in range(2):
                        m = pe.matmul(A[b][:, hp * 512 + 256:hp * 512 + 512], one_v[:, :], osq[:, b, hp * 256:(hp + 1) * 256],
                                      start=True, stop=True)
                    m.then_inc(full["msq"], 1)
                elif kind == "wout":
                    T = tokens(L)
                    pe.wait_ge(ylo_ready, 6 * L + len(tiles_of(L)))
                    read_out(pe, ("dft", L, 0))
                    pe.wait_ge(conv_ready, 2 * (L + 1))
                    with pe.Fori(0, KT // 4, 1) as i:
                        for j in range(4):
                            pe.wait_ge(lo_done, 4 * i + (n0 + j - N_MOD0 + 1))
                            pe.wait_ge(free[f"A{j % 2}"], 2 * i + (PLAN.acc[e][j % 2] + j // 2))
                            project(A[j % 2], n0 + j, T, H)
                elif kind == "ffn_in":
                    T, per = tokens(L), 4 if L == 0 else 2
                    nb = BLOCKS[e[2]]
                    unit_free(e)
                    if e[2] == 0:
                        pe.wait_ge(hlo_ready, KT * (pre_no(L, 1) + 1))
                    pairs = 4 // per
                    with pe.Fori(0, nb // pairs, 1) as i:
                        for q in range(pairs):
                            for j in range(2):
                                c = q * per + j
                                pe.wait_ge(lo_done, 4 * i + (n0 + c - N_MOD0 + 1))
                                pe.wait_ge(free[f"A{j}"], pairs * i + (PLAN.acc[e][j] + q))
                                project(A[j], n0 + c, T, H)
                        if L == 0:
                            for j in range(2):
                                pe.wait_ge(lo_done, 4 * i + (n0 + 2 + j - N_MOD0 + 1))
                                o = 8 * i + (8 * e[3] + 4 * j)
                                mod_matmul(G[0][:, bass.ds(o, 4)], n0 + 2 + j)
                elif kind == "ffn_out":
                    T = tokens(L)
                    pe.wait_ge(g_ready, 2 + HID * L + sum(BLOCKS[:e[2] + 1]))
                    with pe.Fori(0, KT // 4, 1) as i:
                        for j in range(4):
                            pe.wait_ge(lo_done, 4 * i + (n0 + j - N_MOD0 + 1))
                            pe.wait_ge(free[f"A{j % 2}"], 2 * i + (PLAN.acc[e][j % 2] + j // 2))
                            project(A[j % 2], n0 + j, T, (g_hi, g_lo), K=BLOCKS[e[2]])
                elif kind == "postnorm":
                    unit_free(e)
                    pe.wait_ge(ssq_ready, KT * (2 * L + e[2] + 1))
                    for t0, t1, _ in segments(norm_tokens(e)):
                        m = pe.matmul(N[:, t0:t1], one_d[:, :], ssq[:, t0:t1], start=True, stop=True)
                    m.then_inc(full["postnorm"], 1)
                elif kind == "prenorm":
                    unit_free(e)
                    base = KT * pre_no(L, e[2])
                    for k in range(KT):
                        pe.wait_ge(sq_ready, base + k + 1)
                        for t0, t1, _ in segments(norm_tokens(e)):
                            m = pe.matmul(N[:, t0:t1], one_d[:, :], sqb[:, k % 2, t0:t1], start=(k == 0), stop=(k == KT - 1))
                        m.then_inc(sq_used, 1)

        @block.scalar
        def _(act):
            steps = [0]

            def link(ins):
                steps[0] += 1
                ins.then_inc(act_step, 1)
                act.wait_ge(act_step, steps[0])

            def high(n, i=None):
                if n >= N_CHUNKS:
                    return
                r, u = 16 * (n // 4 + 1), n - 1
                act.wait_ge(raw_in[n % 4], r if i is None else 16 * i + r)
                if n >= 2:
                    act.wait_ge(chunk_used, u if i is None else 4 * i + u)
                act.activation(w_hi[:, n % 2, :], raw[:, n % 4, :], ACT.Copy).then_inc(hi_done, 1)

            def normalise(e, T, dst, parts, eps_col):
                for (a, b, u) in parts:
                    act.activation(dst[:, a:b], N[:, a:b], ACT.Ln, bias=eps_col).then_inc(free[u], 1)
                read_out(act, e)
                return act.activation(dst[:, 0:T], dst[:, 0:T], ACT.Exp, scale=-0.5)

            act.dma_start(par[:, :], cols).then_inc(consts_in, 16)
            for k in range(0, KT, 4):
                act.dma_start(x[:, k:k + 4, :], xT[:, k:k + 4, :]).then_inc(x_in, 16)
            for k in range(0, KT, 4):
                act.dma_start(y[:, k:k + 4, 0:SEQ], posT[:, k:k + 4, :]).then_inc(pos_in, 16)
            for dst, src in ((wd, wdec), (mask, masks), (mat, mats), (chan, wide[:, 0:256]), (one_d, wide[:, 256:384]),
                             (one_v, wide[:, 384:512]), (ident, wide[:, 512:640])):
                act.dma_start(dst[:], src).then_inc(consts_in, 16)
            high(0)
            high(1)
            act.wait_ge(consts_in, 16 * 8)
            act.activation(csil[:, :, :].rearrange("p v k -> p (v k)"), par[:, DEPTH * PCOLS:DEPTH * PCOLS + 16],
                           ACT.Silu).then_inc(csil_ready, 1)
            act.wait_ge(csil_ready, 1)
            act.activation(c4[:, :, 0:2], csil[:, :, :].rearrange("p v k -> p k v"), ACT.Copy).then_inc(c4hi_ready, 1)

            act.wait_ge(consts_set, 1)
            for e in ORDER:
                kind, L = e[0], e[1]
                n0, nc_ = PLAN.n0[e], len(chunks_of(e))
                if kind in ("mods", "mod"):
                    for m in range(nc_):
                        high(n0 + m + 2)
                    if kind == "mods":
                        act.wait_ge(chunk_used, n0 + nc_)
                        a, b = (0, 48) if L else (0, 16)
                        act.activation(mraw[:, a:b, :].rearrange("p a b -> p (a b)"), G[0][:, 4 * a:4 * b],
                                       ACT.Copy).then_inc(free["G0"], 1)
                elif kind == "modend":
                    act.wait_ge(chunk_used, n0)
                    act.activation(mraw[:, 16:48, :].rearrange("p a b -> p (a b)"), N[:, 64:192], ACT.Copy).then_inc(free["N0"], 1)
                elif kind == "proj":
                    name, j, _ = W_IN[e[2]]
                    T = tokens(L, name)
                    high(n0 + 2)
                    if e[2] == 0:
                        act.wait_ge(x_kept, 32 * (L + 1))
                    if name == "u":
                        continue
                    src = A[PLAN.acc[e]]
                    act.wait_ge(chunk_used, n0 + 1)
                    if name == "v" and j >= 2:
                        act.wait_ge(full["turn"], 6 * L + j + 1)
                    dst = {"lr": lrT[0:32, 0:T], "k": kT[:, j % 2, 0:T], "v": vst[:, j % 2, 0:T], "q": qT[:, j % 2, 0:T],
                           "f": uF[:, j % 2, 0:T], "c": cgz[:, j % 2, 0:T], "b": bg[:, j % 2, 0:T], "r": r_s[:, j, 0:T]}[name]
                    rows = 32 if name == "lr" else P
                    if name == "r":
                        m = act.activation(dst, src[0:rows, 0:T], ACT.Silu)
                    else:
                        m = act.activation(dst, src[0:rows, 0:T], ACT.Copy, scale=DK ** -0.5 if name == "q" else 1.0)
                    m.then_inc(free[f"A{PLAN.acc[e]}"], 1)
                    if name == "lr" or (name, j) == ("r", 3):
                        act.preload_act_table_set(LN_SET)
                elif kind == "z":
                    q = TT_ALL * L + e[2]
                    b = e[2] % 2
                    act.wait_ge(zneg_ready, q + 1)
                    link(act.activation(zs[:, b, :], zs[:, b, :], ACT.Exp))
                    act.activation(zs[:, b, :], zs[:, b, :], ACT.Ln, bias=1.0).then_inc(zln_ready, 1)
                elif kind == "turn":
                    j = e[2]
                    act.wait_ge(full["turn"], PLAN.full[e])
                    dst = ktok[:, :, j * P:(j + 1) * P] if j < 2 else vtok[:, :, (j - 2) * P:(j - 1) * P]
                    for half, (a, b) in enumerate(((0, 4), (4, 6))):
                        m = act.activation(dst[:, a:b, :], G[half][:, 0:(b - a) * P].rearrange("p (a b) -> p a b", b=P), ACT.Copy)
                        m.then_inc(free[f"G{half}"], 1)
                elif kind == "suffix":
                    g, tt = STEPS[e[2]]
                    act.wait_ge(full["suffix"], PLAN.full[e])
                    act.activation(eu[:, g, :], N[:, 512:512 + KW], ACT.Exp)
                    m = act.activation(dec[:, e[2], :], N[:, 768:772], ACT.Exp)
                    m.then_inc(free["N1"], 1)
                elif kind == "four":
                    tt = e[2]
                    act.wait_ge(full["four"], PLAN.full[e])
                    ab = h_hi[:, 0:4, :].rearrange("p a b -> p (a b)")
                    act.activation(ab[:, tt * 512:(tt + 1) * 512], unit_of(e), ACT.Copy).then_inc(ab_hi, 1)
                elif kind == "dft":
                    high(n0 + 2)
                    if e[2] == 0:
                        for j in range(2):
                            act.wait_ge(conv_f, 2 * L + j + 1)
                            act.activation(h_hi[:, 6 + j, 0:tokens(L)], bg[:, j, 0:tokens(L)], ACT.Copy).then_inc(conv_hi, 1)
                    if e[2] == (3 if L else 4):
                        act.wait_ge(chunk_used, n0 + 1)
                        for ch in range(2):
                            act.activation(h_hi[:, 4 + ch, 0:tokens(L)], A[ch][:, 0:tokens(L)], ACT.Copy).then_inc(four_hi, 1)
                elif kind == "gate":
                    tt, g = e[2], e[3]
                    b = turn(L, tt)
                    act.wait_ge(full["gate"], PLAN.full[e])
                    src = G[g][:, :].rearrange("p (r w t) -> p r w t", r=2, w=2)
                    if nth(L, tt) - 6 * L >= 2:
                        act.wait_ge(full["o"], 6 * L + tiles_of(L).index(tt) - 1)
                    elif tiles_of(L).index(tt) == 0:
                        read_out(act, ("dstate", L, 11))
                        act.wait_ge(conv_f, 2 * (L + 1))
                    act.activation(E[:, b, g, 0, :, :], src[:, :, 1, :], ACT.Exp)
                    act.activation(E[:, b, g, 1, :, :], src[:, :, 1, :], ACT.Exp, scale=-1.0)
                    m = act.activation(E[:, b, g, 2, :, :], src[:, :, 0, :], ACT.Exp)
                    m.then_inc(free[f"G{g}"], 1)
                elif kind == "o":
                    b = turn(L, e[2])
                    act.wait_ge(full["o"], PLAN.full[e])
                    if tiles_of(L).index(e[2]) >= 2:
                        act.wait_ge(full["msq"], nth(L, e[2]) - 1)
                    act.activation(osq[:, b, :].rearrange("p (q r) -> p q r", q=2), o_all(b, 0), ACT.Square).then_inc(osq_ready, 1)
                elif kind == "msq":
                    b = turn(L, e[2])
                    q = nth(L, e[2])
                    act.wait_ge(full["msq"], PLAN.full[e])
                    if tiles_of(L).index(e[2]) >= 2:
                        act.wait_ge(ylo_ready, q - 1)
                    flat = rb[:, b, :, :].rearrange("p (q r) t -> p q (r t)", q=2)
                    link(act.activation(flat, o_all(b, 1), ACT.Ln, bias=eps[:, 0:1]))
                    act.activation(flat, flat, ACT.Exp, scale=-0.5).then_inc(orstd_ready, 1)
                    act.wait_ge(yg_ready, q + 1)
                    act.activation(y_all(h_hi, e[2]), rb[:, b, :, :].rearrange("p (q r) t -> p q r t", q=2), ACT.Copy).then_inc(yhi_ready, 1)
                elif kind == "wout":
                    act.wait_ge(ylo_ready, 6 * L + len(tiles_of(L)))
                    for k in range(0, KT, 4):
                        act.dma_start(x[:, k:k + 4, :], x_keep[:, k:k + 4, :]).then_inc(x_back, 16)
                    with act.Fori(0, KT // 4, 1) as i:
                        for j in range(4):
                            high(n0 + j + 2, i)
                elif kind == "ffn_in":
                    T, per = tokens(L), 4 if L == 0 else 2
                    nb, pairs = BLOCKS[e[2]], 2 if L else 1
                    p0 = HID * L + e[3]
                    if e[2] == 0:
                        act.preload_act_table_set("silu_and_others")
                    with act.Fori(0, nb // 2, 1) as i:
                        for q in range(2):
                            ci, co = (4, n0 + q * per) if per == 2 else (8, n0 + q * per)

                            def high_at(c):
                                act.wait_ge(raw_in[c % 4], (4 * ci) * i + 16 * (c // 4 + 1))
                                act.wait_ge(chunk_used, ci * i + (c - 1))
                                act.activation(w_hi[:, c % 2, :], raw[:, c % 4, :], ACT.Copy).then_inc(hi_done, 1)

                            high_at(co + 2)
                            act.wait_ge(chunk_used, ci * i + (co + 1))
                            act.wait_ge(g_ready, 2 * i + (p0 + q + 1))
                            act.activation(sil[:, q, 0:T], A[0][:, 0:T], ACT.Silu).then_inc(free["A0"], 1)
                            high_at(co + 3)
                            act.wait_ge(free["A1"], 2 * i + (PLAN.acc[e][1] + q + 1))
                            act.activation(g_hi[:, bass.ds(2 * i + q, 1), 0:T], sil[:, q:q + 1, 0:T], ACT.Copy).then_inc(ghi_ready, 1)
                            if per == 4:
                                high_at(co + 4)
                                high_at(co + 5)
                elif kind == "ffn_out":
                    lastn = e[2] == 2 and L == 1
                    if lastn:
                        for j in range(KT):
                            high(n0 + j + 2)
                    else:
                        with act.Fori(0, KT // 4, 1) as i:
                            for j in range(4):
                                high(n0 + j + 2, i)
                elif kind == "postnorm":
                    T = norm_tokens(e)
                    act.preload_act_table_set(LN_SET)
                    act.wait_ge(full["postnorm"], PLAN.full[e])
                    parts = [(t0, t1, f"N{v}") for t0, t1, v in segments(T)]
                    normalise(e, T, rstd, parts, eps[:, 0:1]).then_inc(rstd_ready, 1)
                    if L == 1 and e[2] == 1:
                        for k in range(KT):
                            act.wait_ge(xnew_ready, KT * (pre_no(L, 1) + 1) + k + 1)
                            act.dma_start(out[:, k, :], x[:, k, 0:SEQ]).then_inc(out_sent, 16)
                        act.wait_ge(out_sent, 16 * KT)
                elif kind == "prenorm":
                    T = norm_tokens(e)
                    q = pre_no(L, e[2])
                    if q == 0:
                        act.preload_act_table_set(LN_SET)
                    for k in range(KT):
                        act.wait_ge(xnew_ready, KT * q + k + 1)
                        if KT * q + k >= 2:
                            act.wait_ge(sq_used, KT * q + k - 1)
                        act.activation(sqb[:, k % 2, 0:T], x[:, k, 0:T], ACT.Square).then_inc(sq_ready, 1)
                    if e[2] == 0:
                        for k in range(0, KT, 4):
                            act.dma_start(x_keep[:, k:k + 4, :], x[:, k:k + 4, :]).then_inc(x_kept, 16)
                    act.wait_ge(sq_used, KT * (q + 1))
                    parts = [(t0, t1, f"N{v}") for t0, t1, v in segments(T)]
                    normalise(e, T, rstd, parts, eps[:, 0:1]).then_inc(rstd_ready, 1)
                    for k in range(KT):
                        act.wait_ge(haff_ready, KT * q + k + 1)
                        act.activation(h_hi[:, k, 0:T], y[:, k, 0:T], ACT.Copy).then_inc(hhi_ready, 1)

        @block.vector
        def _(dve):
            steps = [0]

            def link(ins):
                steps[0] += 1
                ins.then_inc(dve_step, 1)
                dve.wait_ge(dve_step, steps[0])

            dve.memset(eps[:, :], EPS).then_inc(consts_set, 1)
            dve.memset(coef[:, 0, 0, 0, :], 0.0).then_inc(g_ready, 2)
            dve.wait_ge(c4hi_ready, 1)
            dve.tensor_tensor(c4[:, :, 2:4], csil[:, :, :].rearrange("p v k -> p k v"), c4[:, :, 0:2].bitcast(F32),
                              ALU.subtract).then_inc(c_ready, 1)
            for n in range(N_MOD0):
                dve.wait_ge(hi_done, n + 1)
                dve.tensor_tensor(w_lo[:, n % 2, :], raw[:, n % 4, :], w_hi[:, n % 2, :].bitcast(F32),
                                  ALU.subtract).then_inc(lo_first, 1)

            def modulation(L, a, b, unit, before):
                dve.wait_ge(free[unit], before + 1)
                link(dve.tensor_tensor(modT[:, a:b, :], mraw[:, a:b, 0:2], mraw[:, a:b, 2:4], ALU.add))
                for v in range(2):
                    m = dve.tensor_tensor(modT[:, a:b, v], modT[:, a:b, v], col(L, PB + a, b - a), ALU.add)
                link(m)
                for w in range(a // KT, b // KT):
                    src = modT[:, w * KT:(w + 1) * KT, :]
                    for v in range(2):
                        if w % 3 == 0:
                            m = dve.tensor_copy(coef[:, L, w, :, v], src[:, :, v])
                        else:
                            gain = col(L, PG + KT * {1: 0, 2: 1, 4: 2, 5: 3}[w], KT)
                            m = dve.scalar_tensor_tensor(coef[:, L, w, :, v], src[:, :, v], 1.0 if w % 3 == 1 else 0.0,
                                                         gain, ALU.add, ALU.mult)
                link(m)

            for e in ORDER:
                kind, L = e[0], e[1]
                n0 = PLAN.n0[e]
                if kind == "mods":
                    if L == 0:
                        dve.wait_ge(x_in, 32)
                        dve.wait_ge(pos_in, 32)
                        for k in range(KT):
                            dve.tensor_tensor(x[:, k, 0:SEQ], x[:, k, 0:SEQ], y[:, k, 0:SEQ], ALU.add).then_inc(xnew_ready, 1)
                    entry = ("ffn_in", 0, 0, 0) if L else e
                    modulation(L, 0, 48 if L else 16, *PLAN.before[entry][0])
                elif kind == "modend":
                    modulation(0, 16, 48, *PLAN.before[("mod", 0, 16)][0])
                elif kind == "proj":
                    name, j, _ = W_IN[e[2]]
                    T = tokens(L, name)
                    if e[2] == 0:
                        dve.wait_ge(x_kept, 32 * (L + 1))
                        dve.memset(lrT[32:33, :], 1.0).then_inc(lr_ones, 1)
                        dve.memset(S[:, 0, 8, :, :], 0.0)
                        link(dve.memset(S[:, 1, 11, :, :], 0.0))
                    if name == "u":
                        read_out(dve, proj(L, "c", j))
                        dve.wait_ge(chunk_used, n0 + 1)
                        m = dve.tensor_tensor(cgz[:, j, 0:T], cgz[:, j, 0:T], A[PLAN.acc[e]][:, 0:T], ALU.mult)
                        m.then_inc(free[f"A{PLAN.acc[e]}"], 1)
                    if name == "b":
                        read_out(dve, proj(L, "u", j))
                        for t0, t1, _ in segments(T):
                            tap = [col(L, PCW + 2 * w + j) for w in range(3)]
                            link(dve.tensor_scalar(cv[:, t0:t1], cgz[:, j, t0:t1], tap[1], col(L, PCB + j), ALU.mult, ALU.add))
                            link(dve.scalar_tensor_tensor(cv[:, t0 + 1:t1], cgz[:, j, t0:t1 - 1], tap[0], cv[:, t0 + 1:t1],
                                                          ALU.mult, ALU.add))
                            link(dve.scalar_tensor_tensor(cv[:, t0:t1 - 1], cgz[:, j, t0 + 1:t1], tap[2], cv[:, t0:t1 - 1],
                                                          ALU.mult, ALU.add))
                        read_out(dve, proj(L, "b", j))
                        dve.tensor_tensor(bg[:, j, 0:T], bg[:, j, 0:T], cv[:, 0:T], ALU.mult).then_inc(conv_f, 1)
                elif kind == "z":
                    tt = e[2]
                    b, q = tt % 2, TT_ALL * L + tt
                    dve.wait_ge(full["z"], PLAN.full[e])
                    link(dve.tensor_scalar(zs[:, b, :], unit_of(e), -1.0, None, ALU.mult))
                    dve.tensor_tensor(zs[:, b, :], zs[:, b, :], unit_of(e), ALU.min).then_inc(zneg_ready, 1)
                    dve.wait_ge(zln_ready, q + 1)
                    m = dve.scalar_tensor_tensor(ls[:, tt, :], unit_of(e), 0.0, zs[:, b, :], ALU.min, ALU.subtract)
                    m.then_inc(free[PLAN.before[e][0][0]], 1)
                elif kind == "suffix":
                    g, tt = STEPS[e[2]]
                    if e[2] == 0:
                        read_out(dve, ("turn", L, 1))
                    read_out(dve, e)
                    dve.tensor_tensor(eu[:, g, :], eu[:, g, :], ktok[:, tt, :], ALU.mult).then_inc(ku_ready, 1)
                elif kind == "dstate":
                    g, tt = STEPS[e[2]]
                    dve.wait_ge(full["dstate"], PLAN.full[e])
                    order = (0, 1) if g == 0 else (1, 0)
                    for c in order:
                        at = 2 * tt + c
                        after = {11: 0, 7: None}.get(at, at + 1) if g == 0 else {8: 7, 0: None}.get(at, at - 1)
                        if after is None:
                            continue
                        final = (g, at) in ((0, 6), (1, 1))
                        for pr in range(2):
                            m = dve.scalar_tensor_tensor(S[:, g, after, pr, :], S[:, g, at, pr, :],
                                                         dec[:, e[2], 2 * pr + c:2 * pr + c + 1],
                                                         G[c][:, pr * DV:(pr + 1) * DV], ALU.mult, ALU.add)
                            if pr == 1:
                                m.then_inc(free[f"G{c}"], 1)
                            elif final:
                                m.then_inc(free[f"G{1 - c}"], 1)
                        dve.wait_ge(free[f"G{c}"], PLAN.before[e][c][1] + 1)
                elif kind == "four":
                    tt = e[2]
                    q = 6 * L + tiles_of(L).index(tt)
                    ab = [t[:, 0:4, :].rearrange("p a b -> p (a b)")[:, tt * 512:(tt + 1) * 512] for t in (h_hi, h_lo)]
                    dve.wait_ge(ab_hi, q + 1)
                    m = dve.tensor_tensor(ab[1], unit_of(e), ab[0].bitcast(F32), ALU.subtract)
                    m.then_inc(free[PLAN.before[e][0][0]], 1)
                elif kind == "dft":
                    T = tokens(L)
                    if e[2] == 0:
                        for j in range(2):
                            dve.wait_ge(conv_hi, 2 * L + j + 1)
                            dve.tensor_tensor(h_lo[:, 6 + j, 0:T], bg[:, j, 0:T], h_hi[:, 6 + j, 0:T].bitcast(F32),
                                              ALU.subtract).then_inc(conv_ready, 1)
                    if e[2] == (3 if L else 4):
                        for ch in range(2):
                            dve.wait_ge(four_hi, 2 * L + ch + 1)
                            m = dve.tensor_tensor(h_lo[:, 4 + ch, 0:T], A[ch][:, 0:T], h_hi[:, 4 + ch, 0:T].bitcast(F32),
                                                  ALU.subtract)
                            m.then_inc(free[f"A{ch}"], 1)
                elif kind == "gate":
                    tt, g = e[2], e[3]
                    b = turn(L, tt)
                    if tiles_of(L).index(tt) == 0 and g == 0:
                        link(dve.memset(Pm[:, :, :, :, :, :], 0.0))
                    read_out(dve, e)
                    q_, k_ = qT[:, :, tt * P:(tt + 1) * P], kT[:, :, tt * P:(tt + 1) * P]
                    dve.tensor_tensor(E[:, b, g, 0, :, :], E[:, b, g, 0, :, :], q_, ALU.mult)
                    dve.tensor_tensor(E[:, b, g, 1, :, :], E[:, b, g, 1, :, :], k_, ALU.mult)
                    dve.tensor_tensor(E[:, b, g, 2, :, :], E[:, b, g, 2, :, :], q_, ALU.mult).then_inc(qk_ready, 1)
                elif kind == "score":
                    b = turn(L, e[2])
                    dve.wait_ge(full["score"], PLAN.full[e])
                    if tiles_of(L).index(e[2]) >= 2:
                        dve.wait_ge(full["o"], nth(L, e[2]) - 1)
                    for hp in range(2):
                        for g in range(2):
                            m = dve.copy_predicated(Pm[:, b, hp, g, :, :],
                                                    mask[:, g:g + 1, :].to_broadcast([P, 2, P]),
                                                    N[:, hp * 512 + g * 256:hp * 512 + (g + 1) * 256].rearrange("p (r t) -> p r t", r=2))
                        m.then_inc(free[f"N{hp}"], 1)
                elif kind == "msq":
                    tt = e[2]
                    b, q = turn(L, tt), nth(L, tt)
                    dve.wait_ge(orstd_ready, q + 1)
                    flat = rb[:, b, :, :].rearrange("p (q r) t -> p q (r t)", q=2)
                    m = dve.tensor_tensor(flat, o_all(b, 0), flat, ALU.mult)
                    m.then_inc(free[f"A{b}"], 1)
                    read_out(dve, ("o", L, tt))
                    for h in range(HEADS):
                        at = (h % 2) * 2 + h // 2
                        m = dve.scalar_tensor_tensor(rb[:, b, at, :], rb[:, b, at, :], col(L, PGN + h),
                                                     r_s[:, h, tt * P:(tt + 1) * P], ALU.mult, ALU.mult)
                    m.then_inc(yg_ready, 1)
                    dve.wait_ge(yhi_ready, q + 1)
                    dve.tensor_tensor(y_all(h_lo, tt), rb[:, b, :, :].rearrange("p (q r) t -> p q r t", q=2),
                                      y_all(h_hi, tt).bitcast(F32), ALU.subtract).then_inc(ylo_ready, 1)
                elif kind in ("wout", "ffn_out"):
                    T = tokens(L)
                    last = kind == "wout" or e[2] == 2
                    add = kind == "ffn_out" and e[2] > 0
                    if last:
                        link(dve.memset(ssq[:, 0:T], 0.0))
                    for j in range(2):
                        dve.wait_ge(free[f"A{j}"], PLAN.acc[e][j])
                    base = steps[0]
                    sums = KT * (2 * L + (kind == "ffn_out"))
                    with dve.Fori(0, KT // 4, 1) as i:
                        for j in range(4):
                            ym = y[:, bass.ds(4 * i + j, 1), 0:T]
                            src = A[j % 2][:, 0:T].rearrange("p (a t) -> p a t", a=1)
                            dve.wait_ge(chunk_used, 4 * i + (n0 + j + 1))
                            m = dve.tensor_tensor(ym, src, ym, ALU.add) if add else dve.tensor_copy(ym, src)
                            m.then_inc(free[f"A{j % 2}"], 1)
                            if last:
                                dve.wait_ge(free[f"A{j % 2}"], 2 * i + (PLAN.acc[e][j % 2] + j // 2 + 1))
                                s3 = sqb[:, 0:1, 0:T]
                                dve.tensor_tensor(s3, ym, ym, ALU.mult).then_inc(dve_step, 1)
                                dve.wait_ge(dve_step, 4 * i + (base + j + 1))
                                q3 = ssq[:, 0:T].rearrange("p (a t) -> p a t", a=1)
                                dve.tensor_tensor(q3, q3, s3, ALU.add).then_inc(ssq_ready, 1)
                                dve.wait_ge(ssq_ready, 4 * i + (sums + j + 1))
                    steps[0] += KT if last else 0
                elif kind == "ffn_in":
                    T, per = tokens(L), 4 if L == 0 else 2
                    nb = BLOCKS[e[2]]
                    p0 = HID * L + e[3]
                    ci = 2 * per
                    with dve.Fori(0, nb // 2, 1) as i:
                        for q in range(2):
                            dve.wait_ge(free["A0"], 2 * i + (PLAN.acc[e][0] + q + 1))
                            dve.wait_ge(chunk_used, ci * i + (n0 + q * per + 2))
                            dve.tensor_tensor(sil[:, q, 0:T], sil[:, q, 0:T], A[1][:, 0:T], ALU.mult).then_inc(free["A1"], 1)
                            dve.wait_ge(ghi_ready, 2 * i + (p0 + q + 1))
                            gp = bass.ds(2 * i + q, 1)
                            dve.tensor_tensor(g_lo[:, gp, 0:T], sil[:, q:q + 1, 0:T], g_hi[:, gp, 0:T].bitcast(F32),
                                              ALU.subtract).then_inc(g_ready, 1)
                elif kind == "postnorm":
                    T = norm_tokens(e)
                    no = 2 * L + e[2]
                    if e[2] == 0:
                        dve.wait_ge(x_back, 32 * (L + 1))
                    dve.wait_ge(rstd_ready, 1 + 2 * no + 1)
                    for k in range(KT):
                        link(dve.tensor_tensor(y[:, k, 0:T], y[:, k, 0:T], rstd[:, 0:T], ALU.mult))
                        for t0, t1, v in segments(T):
                            m = dve.scalar_tensor_tensor(x[:, k, t0:t1], y[:, k, t0:t1], coef[:, L, 3 * e[2] + 2, k, v:v + 1],
                                                         x[:, k, t0:t1], ALU.mult, ALU.add)
                        m.then_inc(xnew_ready, 1)
                elif kind == "prenorm":
                    T = norm_tokens(e)
                    q = pre_no(L, e[2])
                    dve.wait_ge(rstd_ready, 2 * q + 1)

                    def low(k):
                        dve.wait_ge(hhi_ready, KT * q + k + 1)
                        dve.tensor_tensor(h_lo[:, k, 0:T], y[:, k, 0:T], h_hi[:, k, 0:T].bitcast(F32),
                                          ALU.subtract).then_inc(hlo_ready, 1)

                    for k in range(KT):
                        link(dve.tensor_tensor(y[:, k, 0:T], x[:, k, 0:T], rstd[:, 0:T], ALU.mult))
                        for t0, t1, v in segments(T):
                            c = [coef[:, L, 3 * e[2] + w, k, v:v + 1] for w in range(2)]
                            m = dve.tensor_scalar(y[:, k, t0:t1], y[:, k, t0:t1], c[1], c[0], ALU.mult, ALU.add)
                        m.then_inc(haff_ready, 1)
                        if k:
                            low(k - 1)
                    low(KT - 1)


def stream_layout(a):
    out = np.zeros((N_CHUNKS, P, 1024), np.float32)
    ang = lambda n: 2 * np.pi * (np.outer(np.arange(n), np.arange(n)) % n) / n
    dft = {}
    for n in (SEQ, CTX):
        s = 1.0 / np.sqrt(n * 64.0)
        dft[n] = (np.cos(ang(n)) * s, -np.sin(ang(n)) * s)

    def tile(w, k0, K, m):
        return w[k0 * P:(k0 + K) * P, m:m + P].reshape(K, P, -1).transpose(1, 0, 2)

    for e in ORDER:
        for i, c in enumerate(chunks_of(e)):
            dst = out[PLAN.n0[e] + i]
            if c[0] == "dft":
                if c[1] < 4:
                    dst[:, 0:512], dst[:, 512:] = (t[c[1] * P:(c[1] + 1) * P] for t in dft[SEQ])
                else:
                    for s in range(2):
                        for q in range(2):
                            dst[:, (2 * s + q) * CTX:(2 * s + q + 1) * CTX] = dft[CTX][q][s * P:(s + 1) * P]
                continue
            name = {"mod": "w_mod", "in": "w_in", "out": "w_out", "fin": "w_ffn_in", "fout": "w_ffn_out"}[c[0]]
            w = a[name][c[1]]
            k0, K = (c[3], c[4]) if c[0] == "fout" else (0, KT)
            m = c[2] if c[0] == "in" else c[2] * P
            dst[:, 0:K * P] = tile(w, k0, K, m).reshape(P, K * P)
    return out


def constants():
    t = np.arange(P)
    same = (t[:, None] // CHUNK) == (t[None, :] // CHUNK)
    s_, t_ = t[:, None] % CHUNK, t[None, :] % CHUNK
    half = CHUNK // 2
    before, after = same & (s_ <= t_), same & (s_ >= t_)
    mats = [before, before * 1.0 - (same & (s_ < half)), after, after * 1.0 - (same & (s_ >= half)),
            same & (s_ > t_), same & (s_ < t_), np.stack([t < CHUNK, t >= CHUNK], 1)]
    mats = np.concatenate([m.astype(np.float32) for m in mats], 1) / 16.0
    masks = np.stack([before, after], 1).astype(np.int32)
    a = 2 * np.pi * (np.outer(np.arange(64), np.arange(64)) % 64) / 64
    chan = np.zeros((P, 2 * P))
    for g in range(2):
        r = slice(g * 64, g * 64 + 64)
        chan[r, g * 64:g * 64 + 64] = np.cos(a)
        chan[r, P + g * 64:P + g * 64 + 64] = np.sin(a)
    wide = np.concatenate([chan, np.full((P, P), 1.0 / D), np.full((P, P), 1.0 / DV), np.eye(P)], 1)
    rows = SEQ // 64
    row, c = np.repeat(np.arange(rows, dtype=np.float32), 64), np.tile(np.arange(64, dtype=np.float32), rows)
    quarter = D // 4
    f = (1.0 / (np.float32(10000.0) ** (np.arange(quarter, dtype=np.float32) / np.float32(quarter)))).astype(np.float32)
    enc = lambda p: np.concatenate([np.sin(p[:, None] * f[None]), np.cos(p[:, None] * f[None])], -1)
    pos = np.concatenate([enc(row), enc(c)], -1).astype(np.float32)
    return masks, mats.astype(np.float32), wide.astype(np.float32), pos


def feature_major(a):
    return np.ascontiguousarray(a.T.reshape(-1, P, a.shape[0]).transpose(1, 0, 2))


def kernel(**inputs):
    import numpy as _np
    import concourse.bacc as _bacc
    from concourse import mybir as _mybir
    from concourse.bass_utils import run_bass_kernel_spmd as _run

    a = {k: _np.asarray(v) for k, v in inputs.items()}
    masks, mats, wide, pos = constants()
    column = lambda v: v.reshape(-1, P).T
    cols = []
    for L in range(DEPTH):
        cols += [column(a[k][L]) for k in ("b_mod", "g_mix_pre", "g_mix_post", "g_ffn_pre", "g_ffn_post", "conv_w",
                                           "conv_b", "gla_norm_w")]
    cols += [column(a["c"][0]), column(a["c_ctx"])]
    wdec = _np.zeros((33, DEPTH, 512), _np.float32)
    for L in range(DEPTH):
        wdec[0:16, L, 0:256], wdec[32, L, 0:256] = a["w_dec_f"][L], a["b_dec_f"][L]
        wdec[16:32, L, 256:512], wdec[32, L, 256:512] = a["w_dec_b"][L], a["b_dec_b"][L]
    arrays = {
        "stream": stream_layout(a),
        "xT": _np.concatenate([feature_major(a["x"][0]), feature_major(a["ctx"][0])], 2),
        "posT": feature_major(pos),
        "cols": _np.concatenate(cols, 1),
        "wdec": wdec,
        "masks": masks,
        "mats": mats,
        "wide": wide,
    }
    arrays = {k: _np.ascontiguousarray(v) for k, v in arrays.items()}
    nc = _bacc.Bacc("TRN2", target_bir_lowering=False, num_devices=1)
    args = [nc.dram_tensor(k, v.shape, _mybir.dt.from_np(v.dtype), kind="ExternalInput").ap() for k, v in arrays.items()]
    args.append(nc.dram_tensor("x_keep", (P, KT, TOK), F32, kind="Internal").ap())
    args.append(nc.dram_tensor("out_0_dram", (P, KT, SEQ), F32, kind="ExternalOutput").ap())
    bass_hybrid_block(nc, *args)
    r = _run(nc, [arrays], core_ids=[0])
    got = r.results[0]["out_0_dram"]
    return _np.ascontiguousarray(got.transpose(1, 0, 2).reshape(D, SEQ).T)[None]
```

```python
from contextlib import ExitStack, nullcontext

import numpy as np

import concourse.bass as bass
from concourse import mybir
from concourse.alu_op_type import AluOpType as ALU

F32 = mybir.dt.float32
F32R = mybir.dt.float32r
I32 = mybir.dt.int32
ACT = mybir.ActivationFunctionType

P = 128
DEPTH, D, SEQ, CTX = 2, 1024, 512, 256
TOK = SEQ + CTX
KT = D // P
TT_ALL, TT_LAT = TOK // P, SEQ // P
HEADS, DK, DV, RANK, CHUNK = 4, 64, 128, 16, 64
HID = 2816 // P
BLOCKS = (8, 8, 6)
EPS = 1e-6
LN_SET = "natural_log_exp_and_others"

KW, VW, FW = HEADS * DK, HEADS * DV, 256
C_LR = KW + VW
C_Q = C_LR + 2 * RANK
C_R = C_Q + KW
C_F = C_R + VW
C_B, C_C, C_U = C_F + FW, C_F + 2 * FW, C_F + 3 * FW
W_IN = ([("lr", 0, C_LR)] + [("k", j, j * P) for j in range(2)] + [("v", j, KW + j * P) for j in range(4)]
        + [("r", j, C_R + j * P) for j in range(4)] + [("q", j, C_Q + j * P) for j in range(2)]
        + [("f", j, C_F + j * P) for j in range(2)] + [("c", j, C_C + j * P) for j in range(2)]
        + [("u", j, C_U + j * P) for j in range(2)] + [("b", j, C_B + j * P) for j in range(2)])
STATE_NAMES = ("lr", "k", "v")
STEPS = [(0, 4), (1, 5), (0, 5), (1, 4), (0, 0), (1, 3), (0, 1), (1, 2), (0, 2), (1, 1), (0, 3), (1, 0)]
MC = 66
PB, PG, PCW, PCB, PGN, PCOLS = 0, 48, 80, 86, 88, 92


def build_order():
    order = []
    order.append(("mods", 0, 0, 16))
    order.append(("prenorm", 0, 0))
    mod = [16]

    def mod_one():
        if mod[0] > 16:
            order.append(("mturn", 0, mod[0] - 1))
        if mod[0] < 48:
            order.append(("mod", 0, mod[0]))
            mod[0] += 1

    for L in range(DEPTH):
        z, t, s, d = list(range(TT_ALL)), list(range(6)), list(range(12)), list(range(12))
        for x, (name, j, _) in enumerate(W_IN):
            order.append(("proj", L, x))
            if L == 0:
                mod_one()
            if 1 <= x <= 3:
                order.append(("z", L, z.pop(0)))
                order.append(("z", L, z.pop(0)))
            if 3 <= x <= 8:
                order.append(("turn", L, t.pop(0)))
            if x >= 10:
                if s:
                    order.append(("suffix", L, s.pop(0)))
                if x >= 11 and d:
                    order.append(("dstate", L, d.pop(0)))
        while d:
            if s:
                order.append(("suffix", L, s.pop(0)))
            order.append(("dstate", L, d.pop(0)))
        tiles = (4, 5, 0, 1, 2, 3) if L == 0 else (0, 1, 2, 3)
        for tt in tiles:
            order.append(("four", L, tt))
            if L == 0:
                mod_one()
        for g in (0, 1):
            order.append(("gate", L, tiles[0], g))
        for s4 in range(4):
            order.append(("dft", L, s4))
            if L == 0:
                mod_one()
        if L == 0:
            order.append(("dft", L, 4))
            mod_one()
            order.append(("mturn", 0, 47))
            order.append(("modend", 0))
        for a, tt in enumerate(tiles):
            order.append(("score", L, tt))
            if a + 1 < len(tiles):
                for g in (0, 1):
                    order.append(("gate", L, tiles[a + 1], g))
            order.append(("o", L, tt))
            if a:
                order.append(("msq", L, tiles[a - 1]))
        order.append(("msq", L, tiles[-1]))
        order.append(("wout", L))
        order.append(("postnorm", L, 0))
        order.append(("prenorm", L, 1))
        first = 0
        for b, nb in enumerate(BLOCKS):
            order.append(("ffn_in", L, b, first))
            order.append(("ffn_out", L, b))
            first += nb
        if L == 0:
            order.append(("mods", 1, 44, 4))
        order.append(("postnorm", L, 1))
        if L == 0:
            order.append(("prenorm", 1, 0))
    return order


ORDER = build_order()


def chunks_of(e):
    kind, L = e[0], e[1]
    if kind == "mods":
        return [("mod", L, m) for m in range(e[2], e[2] + e[3])]
    if kind == "mod":
        return [("mod", L, e[2])]
    if kind == "proj":
        return [("in", L, W_IN[e[2]][2])]
    if kind == "dft":
        return [("dft", e[2])]
    if kind == "wout":
        return [("out", L, m) for m in range(KT)]
    if kind == "ffn_in":
        out = []
        for p in range(e[3], e[3] + BLOCKS[e[2]]):
            if L == 0:
                out += [("mod", 1, 2 * p), ("mod", 1, 2 * p + 1)]
            out += [("fin", L, p), ("fin", L, HID + p)]
        return out
    if kind == "ffn_out":
        first = sum(BLOCKS[:e[2]])
        return [("fout", L, m, first, BLOCKS[e[2]]) for m in range(KT)]
    return []


def tokens(L, name=None):
    return TOK if L == 0 or name in STATE_NAMES else SEQ


def segments(T):
    return [(0, SEQ, 0)] + ([(SEQ, TOK, 1)] if T > SEQ else [])


class Plan:

    def __init__(self):
        self.n0, self.full, self.before, self.evac, self.acc = {}, {}, {}, {}, {}
        n, used, kinds, copies, acc = 0, dict.fromkeys(("A0", "A1", "N0", "N1", "G0", "G1"), 0), {}, {}, 0
        g = 0
        for e in ORDER:
            kind, L = e[0], e[1]
            self.n0[e] = n
            n += len(chunks_of(e))
            units = []
            if kind == "mods" and e[2] == 0:
                units = ["G0", "A0", "A1"]
            elif kind == "proj":
                units = [f"A{acc % 2}"]
                self.acc[e] = acc % 2
                acc += 1
            elif kind in ("z", "turn", "four"):
                if kind == "turn":
                    units = ["G0", "G1"]
                else:
                    units = [f"G{g % 2}"]
                    g += 1
            elif kind == "mod" and e[2] == 16:
                units = ["N0"]
            elif kind == "suffix":
                units = ["N1"]
            elif kind == "dstate":
                units = ["G0", "G1"]
            elif kind == "gate":
                units = [f"G{e[3]}"]
            elif kind == "dft" and e[2] == 0:
                units = ["A0", "A1"]
            elif kind == "score":
                units = ["N0", "N1"]
            elif kind == "o":
                units = [f"A{self.tile_turn(L, e[2])}"]
            elif kind == "wout":
                units = []
                self.acc[e] = (used["A0"], used["A1"])
                used["A0"] += KT // 2
                used["A1"] += KT // 2
            elif kind == "ffn_in":
                self.acc[e] = (used["A0"], used["A1"])
                used["A0"] += BLOCKS[e[2]]
                used["A1"] += BLOCKS[e[2]]
                if L == 0 and e[2] == 0:
                    units = ["G0"]
            elif kind == "ffn_out":
                self.acc[e] = (used["A0"], used["A1"])
                used["A0"] += KT // 2
                used["A1"] += KT // 2
            elif kind in ("postnorm", "prenorm"):
                units = ["N0"] + (["N1"] if L == 0 or (kind == "prenorm" and e[2] == 0) else [])
            self.before[e] = [(u, used[u]) for u in units]
            for u in units:
                used[u] += 1
            fk = kind
            if kind in ("mods", "mod", "mturn", "modend", "proj", "dft", "prenorm", "wout", "ffn_in", "ffn_out"):
                fk = None
            if fk:
                kinds[fk] = kinds.get(fk, 0) + 1
                self.full[e] = kinds[fk]
        self.total = n

    @staticmethod
    def tile_turn(L, tt):
        tiles = (4, 5, 0, 1, 2, 3) if L == 0 else (0, 1, 2, 3)
        return tiles.index(tt) % 2


PLAN = Plan()
N_MOD0 = 16
RAW, RING = 2, 4
N_CHUNKS = PLAN.total


def norm_tokens(e):
    return TOK if e[1] == 0 or (e[0] == "prenorm" and e[2] == 0) else SEQ


def bass_hybrid_block(nc: bass.Bass, stream, xT, pos_row, pos_col, cols, wdec, masks, mats, wide, x_keep, out):
    with ExitStack() as ctx:
        def sb(name, shape, dt=F32, stack=None):
            return (stack or ctx).enter_context(nc.sbuf_tensor(name, shape, dt))

        def sem(name):
            return ctx.enter_context(nc.semaphore(name))

        h_hi = sb("h_hi", [P, KT, TOK], F32R)
        h_lo = sb("h_lo", [P, KT, TOK], F32R)
        raw = sb("raw", [P, RAW, 1024])
        w_hi = sb("w_hi", [P, RING, 1024], F32R)
        w_lo = sb("w_lo", [P, RING, 1024], F32R)
        par = sb("par", [P, DEPTH * PCOLS + 16])
        wd = sb("wd", [33, 512])
        mask = sb("mask", [P, 2, P], I32)
        mat = sb("mat", [P, 4 * P + 2 * P + 2])
        chan = sb("chan", [P, 2 * P])
        one_d = sb("one_d", [P, P])
        one_v = sb("one_v", [P, P])
        ident = sb("ident", [P, P])
        eps = sb("eps", [P, 1])
        csil = sb("csil", [P, 2, KT])
        c4 = sb("c4", [P, KT, MC], F32R)
        sel = sb("sel", [4, 2])
        mrow = sb("mrow", [4, 2 * P])
        modT = sb("modT", [P, 48, 2])
        coef = sb("coef", [P, DEPTH, 6, KT, 2])
        dec = sb("dec", [P, 12, 4])

        start, mix, ffn = ExitStack(), ExitStack(), ExitStack()
        with start:
            raw0 = sb("raw0", [P, N_MOD0, 1024], stack=start)
            mrow0 = sb("mrow0", [4, N_MOD0 * P], stack=start)
        with ffn:
            y = sb("y", [P, KT, TOK], stack=ffn)
            hidden, norm = ExitStack(), ExitStack()
            with hidden:
                g_hi = sb("g_hi", [P, 8, TOK], F32R, stack=hidden)
            with norm:
                rstd = sb("rstd", [P, TOK], stack=norm)
            g_hold = sb("g_hold", [P, 8, TOK], F32R, stack=ffn)
            g_lo = sb("g_lo", [P, 8, TOK], F32R, stack=ffn)
            sqb = sb("sqb", [P, 2, TOK], stack=ffn)
            x = sb("x", [P, KT, TOK], stack=ffn)
            posr = sb("posr", [P, 4, 8], stack=ffn)
            posc = sb("posc", [P, 4, 64], stack=ffn)
        ssq, sil = sqb[:, 1, :], sqb[:, 0, :]
        with mix:
            kT = sb("kT", [P, 2, TOK], stack=mix)
            qT = sb("qT", [P, 2, TOK], stack=mix)
            ktok = sb("ktok", [P, TT_ALL, KW], stack=mix)
            vtok = sb("vtok", [P, TT_ALL, VW], stack=mix)
            ls = sb("ls", [P, TT_ALL, 2 * KW], stack=mix)
            S = sb("S", [P, 2, 12, 2, DV], stack=mix)
            r_s = sb("r_s", [P, 4, TOK], stack=mix)
            early, late = ExitStack(), ExitStack()
            with early:
                lrT = sb("lrT", [33, TOK], stack=early)
                eu = sb("eu", [P, 2, KW], stack=early)
                vst = sb("vst", [P, 2, TOK], stack=early)
                zs = sb("zs", [P, 2, 2 * KW], stack=early)
                cgz = sb("cgz", [P, 2, TOK], stack=early)
                bg = sb("bg", [P, 2, TOK], stack=early)
            uF = vst
            cv = zs[:, :, :].rearrange("p a b -> p (a b)")[:, 0:TOK]
            with late:
                E = sb("E", [P, 2, 2, 3, 2, P], stack=late)
                Pm = sb("Pm", [P, 2, 2, 2, 2, P], stack=late)
                osq = sb("osq", [P, 4 * P], stack=late)
                rb = sb("rb", [P, 2, 4, P], stack=late)

        def ps(name, n):
            return ctx.enter_context(nc.psum_tensor(name, [P, n], F32))

        A = [ps("A0", 1024), ps("A1", 1024)]
        N = ps("N", 1024)
        G = [ps("G0", 512), ps("G1", 512)]

        first_in = [sem(f"first_in{j}") for j in range(N_MOD0)]
        raw_in = [sem(f"raw_in{j}") for j in range(RAW)]
        hi_done, lo_first, lo_done, chunk_used = sem("hi_done"), sem("lo_first"), sem("lo_done"), sem("chunk_used")
        free = {u: sem(f"free_{u}") for u in ("A0", "A1", "N0", "N1", "G0", "G1")}
        full = {k: sem(f"full_{k}") for k in
                ("mturn", "z", "turn", "suffix", "dstate", "four", "gate", "score", "o", "msq", "postnorm")}
        par_in, consts_in, x_in, wd_in = sem("par_in"), sem("consts_in"), sem("x_in"), sem("wd_in")
        sel_in, mrow_ready = sem("sel_in"), sem("mrow_ready")
        x_kept, x_back, out_sent = sem("x_kept"), sem("x_back"), sem("out_sent")
        consts_set = sem("consts_set")
        c_ready, csil_ready, c4hi_ready = sem("c_ready"), sem("csil_ready"), sem("c4hi_ready")
        lr_ones = sem("lr_ones")
        zneg_ready, zln_ready, ku_ready = sem("zneg_ready"), sem("zln_ready"), sem("ku_ready")
        ab_hi, four_hi = sem("ab_hi"), sem("four_hi")
        conv_f, conv_hi, conv_ready = sem("conv_f"), sem("conv_hi"), sem("conv_ready")
        qk_ready = sem("qk_ready")
        osq_ready, orstd_ready, yg_ready, yhi_ready, ylo_ready = (
            sem("osq_ready"), sem("orstd_ready"), sem("yg_ready"), sem("yhi_ready"), sem("ylo_ready"))
        ssq_ready, rstd_ready, xnew_ready, sq_ready, sq_used = (
            sem("ssq_ready"), sem("rstd_ready"), sem("xnew_ready"), sem("sq_ready"), sem("sq_used"))
        haff_ready, hhi_ready = sem("haff_ready"), sem("hhi_ready")
        hlo_ready_p, hlo_ready_v, yn_ready = sem("hlo_ready_p"), sem("hlo_ready_v"), sem("yn_ready")
        ghi_ready, g_ready = sem("ghi_ready"), sem("g_ready")
        dve_step, act_step = sem("dve_step"), sem("act_step")

        def col(L, at, n=1):
            return par[:, L * PCOLS + at:L * PCOLS + at + n]

        def tiles_of(L):
            return (4, 5, 0, 1, 2, 3) if L == 0 else (0, 1, 2, 3)

        def turn(L, tt):
            return tiles_of(L).index(tt) % 2

        def nth(L, tt):
            return 6 * L + tiles_of(L).index(tt)

        def lo_wait(eng, n, plus=0):
            if n < N_MOD0:
                eng.wait_ge(lo_first, n + 1)
            else:
                eng.wait_ge(lo_done, n - N_MOD0 + 1 + plus)

        def read_out(eng, e):
            for u, before in PLAN.before[e]:
                eng.wait_ge(free[u], before + 1)

        def proj(L, name, j):
            return ("proj", L, [w[:2] for w in W_IN].index((name, j)))

        def pre_no(L, which):
            return 2 * L + which

        def h_wait(eng, q, k):
            if k % 4 == 3:
                eng.wait_ge(hlo_ready_v, 2 * q + k // 4 + 1)
            else:
                eng.wait_ge(hlo_ready_p, 6 * q + k + 1 - k // 4)

        def unit_of(e):
            u = PLAN.before[e][0][0]
            return G[int(u[1])][:, :]

        def o_at(b, h):
            pr, hp = divmod(h, 2)
            return A[b][:, hp * 512 + pr * P:hp * 512 + (pr + 1) * P]

        def o_all(b, mean):
            return A[b][:, :].rearrange("p (q m r) -> p q m r", q=2, m=2)[:, :, mean, :]

        def y_all(h, tt):
            return h[:, 0:4, tt * P:(tt + 1) * P].rearrange("p (r q) t -> p q r t", q=2)

        block = ctx.enter_context(nc.Block())

        @block.sync
        def _(sp):
            for n in range(N_MOD0 + RAW):
                if n < N_MOD0:
                    sp.dma_start(raw0[:, n, :], stream[n]).then_inc(first_in[n], 16)
                else:
                    sp.dma_start(raw[:, n % RAW, :], stream[n]).then_inc(raw_in[n % RAW], 16)
            first = N_MOD0 + RAW
            with sp.Fori(0, (N_CHUNKS - first) // RAW, 1) as i:
                for j in range(RAW):
                    sp.wait_ge(lo_done, RAW * i + (j + 1))
                    sp.dma_start(raw[:, j, :], stream[RAW * i + (first + j)]).then_inc(raw_in[j], 16)
            for n in range(N_CHUNKS - (N_CHUNKS - first) % RAW, N_CHUNKS):
                lo_wait(sp, n - RAW)
                sp.dma_start(raw[:, n % RAW, :], stream[n]).then_inc(raw_in[n % RAW], 16)

        @block.gpsimd
        def _(pool):
            done = [N_MOD0]

            def low(n, i=None):
                pool.wait_ge(hi_done, n + 1 if i is None else 4 * i + (n + 1))
                pool.tensor_tensor(w_lo[:, n % RING, :], raw[:, n % RAW, :], w_hi[:, n % RING, :].bitcast(F32),
                                   ALU.subtract).then_inc(lo_done, 1)

            def low_until(end):
                n, rounds = done[0], (end - done[0]) // 4
                if rounds > 1:
                    with pool.Fori(0, rounds, 1) as i:
                        for j in range(4):
                            low(n + j, i)
                    n += 4 * rounds
                for m in range(n, end):
                    low(m)
                done[0] = end

            for e in ORDER:
                if e[0] == "postnorm":
                    low_until(min(N_CHUNKS, PLAN.n0[e] + RING))
                    T, no = norm_tokens(e), 2 * e[1] + e[2]
                    pool.wait_ge(rstd_ready, 2 * no + 2)
                    for k in range(1, KT, 2):
                        pool.tensor_tensor(y[:, k, 0:T], y[:, k, 0:T], rstd[:, 0:T], ALU.mult).then_inc(yn_ready, 1)
                elif e[0] == "prenorm":
                    low_until(PLAN.n0[e] + RING)
                    T, q = norm_tokens(e), pre_no(e[1], e[2])
                    for k in range(KT):
                        if k % 4 != 3:
                            pool.wait_ge(hhi_ready, KT * q + k + 1)
                            pool.tensor_tensor(h_lo[:, k, 0:T], y[:, k, 0:T], h_hi[:, k, 0:T].bitcast(F32),
                                               ALU.subtract).then_inc(hlo_ready_p, 1)
            low_until(N_CHUNKS)

        @block.tensor
        def _(pe):
            def unit_free(e):
                for u, before in PLAN.before[e]:
                    if before:
                        pe.wait_ge(free[u], before)

            def split_matmul(dst, n, T, k, src, first, last):
                s, (hi, lo) = n % RING, src
                wh, wl = w_hi[:, s, k * P:(k + 1) * P], w_lo[:, s, k * P:(k + 1) * P]
                for a, b, p in ((wh, hi, 0), (wh, lo, 1), (wl, hi, 2)):
                    for t0, t1, _ in segments(T):
                        m = pe.matmul(dst[:, t0:t1], a, b[:, k, t0:t1], start=(first and p == 0), stop=(last and p == 2))
                return m

            def project(dst, n, T, src, K=KT, ready=None):
                for k in range(K):
                    if ready:
                        ready(k)
                    m = split_matmul(dst, n, T, k, src, k == 0, k == K - 1)
                m.then_inc(chunk_used, 1)

            def mod_matmul(dst, n):
                for k in range(KT):
                    for w in (w_hi, w_lo):
                        m = pe.matmul(dst, c4[:, k, :], w[:, n % RING, k * P:(k + 1) * P],
                                      start=(k == 0 and w is w_hi), stop=(k == KT - 1 and w is w_lo))
                m.then_inc(chunk_used, 1)

            def mod_turn(dst, row):
                return pe.matmul(dst, row, sel[:, :], start=True, stop=True)

            mrows = [0]
            H = (h_hi, h_lo)
            for e in ORDER:
                kind, L = e[0], e[1]
                n0 = PLAN.n0[e]
                if kind == "mods" and L == 0:
                    pe.wait_ge(c_ready, 1)
                    for m in range(e[3]):
                        pe.wait_ge(lo_first, n0 + m + 1)
                        mod_matmul(A[m // 8][0:MC, (m % 8) * P:(m % 8 + 1) * P], n0 + m)
                    pe.wait_ge(sel_in, 16)
                    for m in range(e[3]):
                        pe.wait_ge(free[f"A{m // 8}"], 1)
                        mm = mod_turn(G[0][:, 2 * m:2 * m + 2], mrow0[:, m * P:(m + 1) * P])
                    mm.then_inc(full["mturn"], 1)
                elif kind == "mods":
                    for m in range(0, e[3], 2):
                        for j in range(2):
                            lo_wait(pe, n0 + m + j)
                            mod_matmul(G[0][0:MC, 256 + j * P:256 + (j + 1) * P], n0 + m + j)
                        mrows[0] += 1
                        pe.wait_ge(mrow_ready, mrows[0])
                        for j in range(2):
                            o = 2 * (e[2] + m + j)
                            mm = mod_turn(G[0][:, o:o + 2], mrow[:, j * P:(j + 1) * P])
                    mm.then_inc(full["mturn"], 1)
                elif kind == "mod":
                    unit_free(e)
                    lo_wait(pe, n0)
                    mod_matmul(N[0:MC, 256:256 + P], n0)
                elif kind == "mturn":
                    mrows[0] += 1
                    pe.wait_ge(mrow_ready, mrows[0])
                    mm = mod_turn(N[:, 2 * e[2]:2 * e[2] + 2], mrow[:, 0:P])
                    if e[2] == 47:
                        mm.then_inc(full["mturn"], 1)
                elif kind == "proj":
                    name, j, _ = W_IN[e[2]]
                    unit_free(e)
                    lo_wait(pe, n0)
                    ready = (lambda k: h_wait(pe, pre_no(L, 0), k)) if e[2] == 0 else None
                    project(A[PLAN.acc[e]], n0, tokens(L, name), H, ready=ready)
                elif kind == "z":
                    tt = e[2]
                    unit_free(e)
                    read_out(pe, proj(L, "lr", 0))
                    pe.wait_ge(lr_ones, L + 1)
                    pe.wait_ge(wd_in, 16 * (L + 1))
                    pe.matmul(unit_of(e), lrT[0:33, tt * P:(tt + 1) * P], wd[:, :],
                              start=True, stop=True).then_inc(full["z"], 1)
                elif kind == "turn":
                    unit_free(e)
                    j = e[2]
                    src = kT[:, j, :] if j < 2 else vst[:, j % 2, :]
                    read_out(pe, proj(L, *(("k", j) if j < 2 else ("v", j - 2))))
                    for tt in range(TT_ALL):
                        m = pe.transpose(G[tt // 4][:, (tt % 4) * P:(tt % 4 + 1) * P], src[:, tt * P:(tt + 1) * P], ident[:, :])
                    m.then_inc(full["turn"], 1)
                elif kind == "suffix":
                    g, tt = STEPS[e[2]]
                    unit_free(e)
                    read_out(pe, ("z", L, tt))
                    pe.matmul(N[:, 512:512 + KW], mat[:, 512 + g * P:512 + (g + 1) * P], ls[:, tt, g * KW:(g + 1) * KW],
                              start=True, stop=True)
                    for pr in range(2):
                        m = pe.matmul(N[:, 768 + 2 * pr:770 + 2 * pr], ls[:, tt, g * KW + pr * P:g * KW + (pr + 1) * P],
                                      mat[:, 768:770], start=True, stop=True)
                    m.then_inc(full["suffix"], 1)
                elif kind == "dstate":
                    g, tt = STEPS[e[2]]
                    unit_free(e)
                    pe.wait_ge(ku_ready, 12 * L + e[2] + 1)
                    if e[2] == 0:
                        read_out(pe, ("turn", L, 5))
                    for c in range(2):
                        for pr in range(2):
                            for hp in range(2):
                                h, row = 2 * pr + hp, slice(c * 64, c * 64 + 64)
                                m = pe.matmul(G[c][hp * 64:hp * 64 + 64, pr * DV:(pr + 1) * DV],
                                              eu[row, g, h * DK:(h + 1) * DK], vtok[row, tt, h * DV:(h + 1) * DV],
                                              start=True, stop=True)
                    m.then_inc(full["dstate"], 1)
                elif kind == "four":
                    tt = e[2]
                    unit_free(e)
                    read_out(pe, proj(L, "f", 0))
                    read_out(pe, proj(L, "f", 1))
                    for ch in range(2):
                        m = pe.matmul(unit_of(e)[:, ch * 256:(ch + 1) * 256], uF[:, ch, tt * P:(tt + 1) * P], chan[:, :],
                                      start=True, stop=True)
                    m.then_inc(full["four"], 1)
                elif kind == "dft":
                    unit_free(e)
                    lo_wait(pe, n0)
                    if e[2] == 0:
                        for tt in tiles_of(L)[-2:]:
                            read_out(pe, ("four", L, tt))
                    s = n0 % RING
                    ab = [t[:, 0:4, :].rearrange("p a b -> p (a b)") for t in H]
                    ctx_part = e[2] == 4
                    tts = (4, 5) if ctx_part else (e[2],)
                    w = CTX if ctx_part else SEQ
                    for ch in range(2):
                        dst = A[ch][:, SEQ:TOK] if ctx_part else A[ch][:, 0:SEQ]
                        for a, tt in enumerate(tts):
                            for part in range(2):
                                lhs = [t[:, tt * 512 + ch * 256 + part * P:tt * 512 + ch * 256 + (part + 1) * P] for t in ab]
                                o = (2 * a + part) * w
                                first = part == 0 and (a == 0 if ctx_part else e[2] == 0)
                                last = part == 1 and (a == 1 if ctx_part else e[2] == 3)
                                for p, (l, r) in enumerate(((lhs[0], w_hi), (lhs[0], w_lo), (lhs[1], w_hi))):
                                    m = pe.matmul(dst, l, r[:, s, o:o + w], start=(first and p == 0), stop=(last and p == 2))
                    m.then_inc(chunk_used, 1)
                elif kind == "gate":
                    tt, g = e[2], e[3]
                    unit_free(e)
                    read_out(pe, ("z", L, tt))
                    for pr in range(2):
                        m = pe.matmul(G[g][:, pr * 256:(pr + 1) * 256], ls[:, tt, g * KW + pr * P:g * KW + (pr + 1) * P],
                                      mat[:, g * 256:(g + 1) * 256], start=True, stop=True)
                    m.then_inc(full["gate"], 1)
                elif kind == "score":
                    tt = e[2]
                    b = turn(L, tt)
                    unit_free(e)
                    pe.wait_ge(qk_ready, 2 * (nth(L, tt) + 1))
                    for g in range(2):
                        for pr in range(2):
                            for hp in range(2):
                                row = slice(hp * 64, hp * 64 + 64)
                                o = hp * 512 + (g * 2 + pr) * P
                                m = pe.matmul(N[:, o:o + P], E[row, b, g, 1, pr, :], E[row, b, g, 0, pr, :], start=True, stop=True)
                    m.then_inc(full["score"], 1)
                elif kind == "o":
                    tt = e[2]
                    b = turn(L, tt)
                    unit_free(e)
                    read_out(pe, ("score", L, tt))
                    read_out(pe, ("dstate", L, 11))
                    for h in range(HEADS):
                        pr, hp = divmod(h, 2)
                        row = slice(hp * 64, hp * 64 + 64)
                        for g in range(2):
                            pe.matmul(o_at(b, h), vtok[:, tt, h * DV:(h + 1) * DV], Pm[:, b, hp, g, pr, :],
                                      start=(g == 0), stop=False)
                        for g in range(2):
                            for c in range(2):
                                m = pe.matmul(o_at(b, h)[:, c * 64:c * 64 + 64], S[row, g, 2 * tt + c, pr, :],
                                              E[row, b, g, 2, pr, c * 64:c * 64 + 64], start=False, stop=(g == 1 and c == 1))
                    m.then_inc(full["o"], 1)
                elif kind == "msq":
                    b = turn(L, e[2])
                    pe.wait_ge(osq_ready, nth(L, e[2]) + 1)
                    for hp in range(2):
                        m = pe.matmul(A[b][:, hp * 512 + 256:hp * 512 + 512], one_v[:, :], osq[:, hp * 256:(hp + 1) * 256],
                                      start=True, stop=True)
                    m.then_inc(full["msq"], 1)
                elif kind == "wout":
                    T = tokens(L)
                    pe.wait_ge(ylo_ready, 6 * L + len(tiles_of(L)))
                    read_out(pe, ("dft", L, 0))
                    pe.wait_ge(conv_ready, 2 * (L + 1))
                    with pe.Fori(0, KT // 4, 1) as i:
                        for j in range(4):
                            pe.wait_ge(lo_done, 4 * i + (n0 + j - N_MOD0 + 1))
                            pe.wait_ge(free[f"A{j % 2}"], 2 * i + (PLAN.acc[e][j % 2] + j // 2))
                            project(A[j % 2], n0 + j, T, H)
                elif kind == "ffn_in":
                    T, per = tokens(L), 4 if L == 0 else 2
                    nb = BLOCKS[e[2]]
                    unit_free(e)
                    tile = (lambda k: h_wait(pe, pre_no(L, 1), k)) if e[2] == 0 else None
                    pairs, at = 4 // per, per - 2
                    rows = mrows[0]
                    with pe.Fori(0, nb // pairs, 1) as i:
                        if L == 0:
                            for j in range(2):
                                pe.wait_ge(lo_done, 4 * i + (n0 + j - N_MOD0 + 1))
                                mod_matmul(G[0][0:MC, 256 + j * P:256 + (j + 1) * P], n0 + j)
                        for q in range(pairs):
                            for j in range(2):
                                c = q * per + at + j
                                pe.wait_ge(lo_done, 4 * i + (n0 + c - N_MOD0 + 1))
                                pe.wait_ge(free[f"A{j}"], pairs * i + (PLAN.acc[e][j] + q))
                                project(A[j], n0 + c, T, H, ready=tile if c == at else None)
                                if L == 0 and j == 0:
                                    pe.wait_ge(mrow_ready, i + (rows + 1))
                                    for r in range(2):
                                        o = 4 * i + (4 * e[3] + 2 * r)
                                        mod_turn(G[0][:, bass.ds(o, 2)], mrow[:, r * P:(r + 1) * P])
                    mrows[0] += nb if L == 0 else 0
                elif kind == "ffn_out":
                    T = tokens(L)
                    last = 1 + HID * L + sum(BLOCKS[:e[2] + 1])
                    pe.wait_ge(g_ready, last - 1)

                    def ready(k):
                        if k == BLOCKS[e[2]] - 1:
                            pe.wait_ge(g_ready, last)

                    with pe.Fori(0, KT // 4, 1) as i:
                        for j in range(4):
                            pe.wait_ge(lo_done, 4 * i + (n0 + j - N_MOD0 + 1))
                            pe.wait_ge(free[f"A{j % 2}"], 2 * i + (PLAN.acc[e][j % 2] + j // 2))
                            project(A[j % 2], n0 + j, T, (g_hi, g_lo), K=BLOCKS[e[2]], ready=ready)
                elif kind == "postnorm":
                    unit_free(e)
                    pe.wait_ge(ssq_ready, KT * (2 * L + e[2] + 1))
                    for t0, t1, _ in segments(norm_tokens(e)):
                        m = pe.matmul(N[:, t0:t1], one_d[:, :], ssq[:, t0:t1], start=True, stop=True)
                    m.then_inc(full["postnorm"], 1)
                elif kind == "prenorm":
                    unit_free(e)
                    base = KT * pre_no(L, e[2])
                    pe.wait_ge(consts_in, 16 * 6)
                    for k in range(KT):
                        pe.wait_ge(sq_ready, base + k + 1)
                        for t0, t1, _ in segments(norm_tokens(e)):
                            m = pe.matmul(N[:, t0:t1], one_d[:, :], sqb[:, k % 2, t0:t1], start=(k == 0), stop=(k == KT - 1))
                        m.then_inc(sq_used, 1)

        @block.scalar
        def _(act):
            steps = [0]

            def link(ins):
                steps[0] += 1
                ins.then_inc(act_step, 1)
                act.wait_ge(act_step, steps[0])

            def high(n, i=None, per=4):
                if n >= N_CHUNKS:
                    return
                if n < N_MOD0:
                    act.wait_ge(first_in[n], 16)
                    src = raw0[:, n, :]
                else:
                    r = 16 * ((n - N_MOD0) // RAW + 1)
                    act.wait_ge(raw_in[n % RAW], r if i is None else (16 * per // RAW) * i + r)
                    src = raw[:, n % RAW, :]
                if n >= RING:
                    act.wait_ge(chunk_used, n - RING + 1 if i is None else per * i + (n - RING + 1))
                act.activation(w_hi[:, n % RING, :], src, ACT.Copy).then_inc(hi_done, 1)

            def normalise(e, T, dst, parts, eps_col):
                for (a, b, u) in parts:
                    act.activation(dst[:, a:b], N[:, a:b], ACT.Ln, bias=eps_col).then_inc(free[u], 1)
                read_out(act, e)
                return act.activation(dst[:, 0:T], dst[:, 0:T], ACT.Exp, scale=-0.5)

            act.dma_start(par[:, :], cols).then_inc(par_in, 16)
            for k in range(0, KT, 4):
                act.dma_start(x[:, k:k + 4, :], xT[:, k:k + 4, :]).then_inc(x_in, 16)
            act.dma_start(posr[:, :, :], pos_row).then_inc(x_in, 16)
            act.dma_start(posc[:, :, :], pos_col).then_inc(x_in, 16)
            for dst, src in ((mask, masks), (mat, mats), (chan, wide[:, 0:256]), (one_d, wide[:, 256:384]),
                             (one_v, wide[:, 384:512]), (ident, wide[:, 512:640])):
                act.dma_start(dst[:], src).then_inc(consts_in, 16)
            act.dma_start(wd[:, :], wdec[:, 0, :]).then_inc(wd_in, 16)
            act.dma_start(sel[:, :], wide[0:4, 640:642]).then_inc(sel_in, 16)
            act.wait_ge(par_in, 16)
            act.activation(csil[:, :, :].rearrange("p v k -> p (v k)"), par[:, DEPTH * PCOLS:DEPTH * PCOLS + 16],
                           ACT.Silu).then_inc(csil_ready, 1)
            act.wait_ge(csil_ready, 1)
            act.wait_ge(consts_set, 1)
            act.activation(c4[:, :, 0:2], csil[:, :, :].rearrange("p v k -> p k v"), ACT.Copy).then_inc(c4hi_ready, 1)
            act.preload_act_table_set(LN_SET)
            for n in range(RING):
                high(n)

            for e in ORDER:
                kind, L = e[0], e[1]
                n0, nc_ = PLAN.n0[e], len(chunks_of(e))
                if kind == "mods" and L == 0:
                    for m in range(nc_):
                        high(n0 + m + RING)
                        if m % 8 == 7:
                            act.wait_ge(chunk_used, n0 + m + 1)
                            act.activation(mrow0[:, (m - 7) * P:(m + 1) * P], A[m // 8][0:4, :],
                                           ACT.Copy).then_inc(free[f"A{m // 8}"], 1)
                elif kind == "mods":
                    for m in range(nc_):
                        high(n0 + m + RING)
                        if m % 2:
                            act.wait_ge(chunk_used, n0 + m + 1)
                            act.activation(mrow[:, :], G[0][0:4, 256:512], ACT.Copy).then_inc(mrow_ready, 1)
                elif kind == "mod":
                    act.wait_ge(chunk_used, n0 + 1)
                    act.activation(mrow[:, 0:P], N[0:4, 256:256 + P], ACT.Copy).then_inc(mrow_ready, 1)
                    high(n0 + RING)
                elif kind == "proj":
                    name, j, _ = W_IN[e[2]]
                    T = tokens(L, name)
                    high(n0 + RING)
                    if e[2] == 0:
                        if L:
                            act.dma_start(wd[:, :], wdec[:, L, :]).then_inc(wd_in, 16)
                        act.wait_ge(x_kept, 32 * (L + 1))
                    if name == "u":
                        continue
                    src = A[PLAN.acc[e]]
                    act.wait_ge(chunk_used, n0 + 1)
                    if name == "v" and j >= 2:
                        act.wait_ge(full["turn"], 6 * L + j + 1)
                    dst = {"lr": lrT[0:32, 0:T], "k": kT[:, j % 2, 0:T], "v": vst[:, j % 2, 0:T], "q": qT[:, j % 2, 0:T],
                           "f": uF[:, j % 2, 0:T], "c": cgz[:, j % 2, 0:T], "b": bg[:, j % 2, 0:T], "r": r_s[:, j, 0:T]}[name]
                    rows = 32 if name == "lr" else P
                    if name == "r":
                        m = act.activation(dst, src[0:rows, 0:T], ACT.Silu)
                    else:
                        m = act.activation(dst, src[0:rows, 0:T], ACT.Copy, scale=DK ** -0.5 if name == "q" else 1.0)
                    m.then_inc(free[f"A{PLAN.acc[e]}"], 1)
                    if name == "lr" or (name, j) == ("r", 3):
                        act.preload_act_table_set(LN_SET)
                elif kind == "z":
                    q = TT_ALL * L + e[2]
                    b = e[2] % 2
                    act.wait_ge(zneg_ready, q + 1)
                    link(act.activation(zs[:, b, :], zs[:, b, :], ACT.Exp))
                    act.activation(zs[:, b, :], zs[:, b, :], ACT.Ln, bias=1.0).then_inc(zln_ready, 1)
                elif kind == "turn":
                    j = e[2]
                    act.wait_ge(full["turn"], PLAN.full[e])
                    dst = ktok[:, :, j * P:(j + 1) * P] if j < 2 else vtok[:, :, (j - 2) * P:(j - 1) * P]
                    for half, (a, b) in enumerate(((0, 4), (4, 6))):
                        m = act.activation(dst[:, a:b, :], G[half][:, 0:(b - a) * P].rearrange("p (a b) -> p a b", b=P), ACT.Copy)
                        m.then_inc(free[f"G{half}"], 1)
                elif kind == "suffix":
                    g, tt = STEPS[e[2]]
                    act.wait_ge(full["suffix"], PLAN.full[e])
                    act.activation(eu[:, g, :], N[:, 512:512 + KW], ACT.Exp)
                    m = act.activation(dec[:, e[2], :], N[:, 768:772], ACT.Exp)
                    m.then_inc(free["N1"], 1)
                elif kind == "four":
                    tt = e[2]
                    act.wait_ge(full["four"], PLAN.full[e])
                    ab = h_hi[:, 0:4, :].rearrange("p a b -> p (a b)")
                    act.activation(ab[:, tt * 512:(tt + 1) * 512], unit_of(e), ACT.Copy).then_inc(ab_hi, 1)
                elif kind == "dft":
                    high(n0 + RING)
                    if e[2] == 0:
                        for j in range(2):
                            act.wait_ge(conv_f, 2 * L + j + 1)
                            act.activation(h_hi[:, 6 + j, 0:tokens(L)], bg[:, j, 0:tokens(L)], ACT.Copy).then_inc(conv_hi, 1)
                    if e[2] == (3 if L else 4):
                        act.wait_ge(chunk_used, n0 + 1)
                        for ch in range(2):
                            act.activation(h_hi[:, 4 + ch, 0:tokens(L)], A[ch][:, 0:tokens(L)], ACT.Copy).then_inc(four_hi, 1)
                elif kind == "gate":
                    tt, g = e[2], e[3]
                    b = turn(L, tt)
                    act.wait_ge(full["gate"], PLAN.full[e])
                    src = G[g][:, :].rearrange("p (r w t) -> p r w t", r=2, w=2)
                    if nth(L, tt) - 6 * L >= 2:
                        act.wait_ge(full["o"], 6 * L + tiles_of(L).index(tt) - 1)
                    elif tiles_of(L).index(tt) == 0:
                        read_out(act, ("dstate", L, 11))
                        act.wait_ge(conv_f, 2 * (L + 1))
                    act.activation(E[:, b, g, 0, :, :], src[:, :, 1, :], ACT.Exp)
                    act.activation(E[:, b, g, 1, :, :], src[:, :, 1, :], ACT.Exp, scale=-1.0)
                    m = act.activation(E[:, b, g, 2, :, :], src[:, :, 0, :], ACT.Exp)
                    m.then_inc(free[f"G{g}"], 1)
                elif kind == "o":
                    b = turn(L, e[2])
                    act.wait_ge(full["o"], PLAN.full[e])
                    if tiles_of(L).index(e[2]) >= 1:
                        act.wait_ge(full["msq"], nth(L, e[2]))
                    act.activation(osq[:, :].rearrange("p (q r) -> p q r", q=2), o_all(b, 0), ACT.Square).then_inc(osq_ready, 1)
                elif kind == "msq":
                    b = turn(L, e[2])
                    q = nth(L, e[2])
                    act.wait_ge(full["msq"], PLAN.full[e])
                    if tiles_of(L).index(e[2]) >= 2:
                        act.wait_ge(ylo_ready, q - 1)
                    flat = rb[:, b, :, :].rearrange("p (q r) t -> p q (r t)", q=2)
                    link(act.activation(flat, o_all(b, 1), ACT.Ln, bias=eps[:, 0:1]))
                    act.activation(flat, flat, ACT.Exp, scale=-0.5).then_inc(orstd_ready, 1)
                    act.wait_ge(yg_ready, q + 1)
                    act.activation(y_all(h_hi, e[2]), rb[:, b, :, :].rearrange("p (q r) t -> p q r t", q=2), ACT.Copy).then_inc(yhi_ready, 1)
                elif kind == "wout":
                    act.wait_ge(ylo_ready, 6 * L + len(tiles_of(L)))
                    for k in range(0, KT, 4):
                        act.dma_start(x[:, k:k + 4, :], x_keep[:, k:k + 4, :]).then_inc(x_back, 16)
                    with act.Fori(0, KT // 4, 1) as i:
                        for j in range(4):
                            high(n0 + j + RING, i)
                elif kind == "ffn_in":
                    T, per = tokens(L), 4 if L == 0 else 2
                    nb, pairs = BLOCKS[e[2]], 2 if L else 1
                    p0 = HID * L + e[3]
                    if e[2] == 0:
                        act.preload_act_table_set("silu_and_others")
                    pairs, at = 4 // per, per - 2
                    with act.Fori(0, nb // pairs, 1) as i:
                        for q in range(pairs):
                            if L == 0:
                                high(n0 + RING, i)
                                high(n0 + 1 + RING, i)
                                act.wait_ge(chunk_used, 4 * i + (n0 + 2))
                                act.activation(mrow[:, :], G[0][0:4, 256:512], ACT.Copy).then_inc(mrow_ready, 1)
                            c = n0 + q * per + at
                            high(c + RING, i)
                            act.wait_ge(chunk_used, 4 * i + (c + 1))
                            act.wait_ge(g_ready, pairs * i + (p0 + q + 1))
                            act.activation(sil[:, 0:T], A[0][:, 0:T], ACT.Silu).then_inc(free["A0"], 1)
                            high(c + 1 + RING, i)
                            act.wait_ge(free["A1"], pairs * i + (PLAN.acc[e][1] + q + 1))
                            act.activation(g_hi[:, bass.ds(pairs * i + q, 1), 0:T], sqb[:, 0:1, 0:T], ACT.Copy).then_inc(ghi_ready, 1)
                elif kind == "ffn_out":
                    if n0 + KT + RING > N_CHUNKS:
                        for j in range(KT):
                            high(n0 + j + RING)
                    else:
                        with act.Fori(0, KT // 4, 1) as i:
                            for j in range(4):
                                high(n0 + j + RING, i)
                elif kind == "postnorm":
                    T = norm_tokens(e)
                    act.preload_act_table_set(LN_SET)
                    act.wait_ge(full["postnorm"], PLAN.full[e])
                    parts = [(t0, t1, f"N{v}") for t0, t1, v in segments(T)]
                    normalise(e, T, rstd, parts, eps[:, 0:1]).then_inc(rstd_ready, 1)
                    if L == 1 and e[2] == 1:
                        for k in range(KT):
                            act.wait_ge(xnew_ready, KT * (pre_no(L, 1) + 1) + k + 1)
                            act.dma_start(out[:, k, :], x[:, k, 0:SEQ]).then_inc(out_sent, 16)
                        act.wait_ge(out_sent, 16 * KT)
                elif kind == "prenorm":
                    T = norm_tokens(e)
                    q = pre_no(L, e[2])
                    for k in range(KT):
                        act.wait_ge(xnew_ready, KT * q + k + 1)
                        if KT * q + k >= 2:
                            act.wait_ge(sq_used, KT * q + k - 1)
                        act.activation(sqb[:, k % 2, 0:T], x[:, k, 0:T], ACT.Square).then_inc(sq_ready, 1)
                    if e[2] == 0:
                        for k in range(0, KT, 4):
                            act.dma_start(x_keep[:, k:k + 4, :], x[:, k:k + 4, :]).then_inc(x_kept, 16)
                    act.wait_ge(sq_used, KT * (q + 1))
                    parts = [(t0, t1, f"N{v}") for t0, t1, v in segments(T)]
                    normalise(e, T, rstd, parts, eps[:, 0:1]).then_inc(rstd_ready, 1)
                    for k in range(KT):
                        act.wait_ge(haff_ready, KT * q + k + 1)
                        act.activation(h_hi[:, k, 0:T], y[:, k, 0:T], ACT.Copy).then_inc(hhi_ready, 1)

        @block.vector
        def _(dve):
            steps = [0]

            def link(ins):
                steps[0] += 1
                ins.then_inc(dve_step, 1)
                dve.wait_ge(dve_step, steps[0])

            dve.memset(eps[:, :], EPS)
            dve.memset(c4[:, :, :].bitcast(F32), 0.0).then_inc(consts_set, 1)
            dve.memset(coef[:, 0, 0, 0, :], 0.0).then_inc(g_ready, 1)
            dve.wait_ge(c4hi_ready, 1)
            dve.tensor_tensor(c4[:, :, 2:4], csil[:, :, :].rearrange("p v k -> p k v"), c4[:, :, 0:2].bitcast(F32),
                              ALU.subtract).then_inc(c_ready, 1)
            for n in range(N_MOD0):
                dve.wait_ge(hi_done, n + 1)
                dve.tensor_tensor(w_lo[:, n % RING, :], raw0[:, n, :], w_hi[:, n % RING, :].bitcast(F32),
                                  ALU.subtract).then_inc(lo_first, 1)

            def modulation(L, a, b, unit, before):
                src = (N if unit == "N0" else G[0])[:, 0:96].rearrange("p (m v) -> p m v", v=2)
                for v in range(2):
                    m = dve.tensor_tensor(modT[:, a:b, v], src[:, a:b, v], col(L, PB + a, b - a), ALU.add)
                m.then_inc(free[unit], 1)
                dve.wait_ge(free[unit], before + 1)
                for w in range(a // KT, b // KT):
                    src = modT[:, w * KT:(w + 1) * KT, :]
                    for v in range(2):
                        if w % 3 == 0:
                            m = dve.tensor_copy(coef[:, L, w, :, v], src[:, :, v])
                        else:
                            gain = col(L, PG + KT * {1: 0, 2: 1, 4: 2, 5: 3}[w], KT)
                            m = dve.scalar_tensor_tensor(coef[:, L, w, :, v], src[:, :, v], 1.0 if w % 3 == 1 else 0.0,
                                                         gain, ALU.add, ALU.mult)
                link(m)

            for e in ORDER:
                kind, L = e[0], e[1]
                n0 = PLAN.n0[e]
                if kind == "mods":
                    if L == 0:
                        dve.wait_ge(x_in, 64)
                        for k in range(KT):
                            p = posr[:, k, :].rearrange("p (r c) -> p r c", c=1).to_broadcast([P, 8, 64]) if k < 4 else \
                                posc[:, k - 4:k - 3, :].to_broadcast([P, 8, 64])
                            xk = x[:, k, 0:SEQ].rearrange("p (r c) -> p r c", r=8)
                            dve.tensor_tensor(xk, xk, p, ALU.add).then_inc(xnew_ready, 1)
                    dve.wait_ge(full["mturn"], 2 * L + 1)
                    entry = ("ffn_in", 0, 0, 0) if L else e
                    modulation(L, 0, 48 if L else 16, *PLAN.before[entry][0])
                elif kind == "modend":
                    dve.wait_ge(full["mturn"], 2)
                    modulation(0, 16, 48, *PLAN.before[("mod", 0, 16)][0])
                elif kind == "proj":
                    name, j, _ = W_IN[e[2]]
                    T = tokens(L, name)
                    if e[2] == 0:
                        dve.wait_ge(x_kept, 32 * (L + 1))
                        dve.memset(lrT[32:33, :], 1.0).then_inc(lr_ones, 1)
                        dve.memset(S[:, 0, 8, :, :], 0.0)
                        link(dve.memset(S[:, 1, 11, :, :], 0.0))
                    if name == "u":
                        read_out(dve, proj(L, "c", j))
                        dve.wait_ge(chunk_used, n0 + 1)
                        m = dve.tensor_tensor(cgz[:, j, 0:T], cgz[:, j, 0:T], A[PLAN.acc[e]][:, 0:T], ALU.mult)
                        m.then_inc(free[f"A{PLAN.acc[e]}"], 1)
                    if name == "b":
                        read_out(dve, proj(L, "u", j))
                        for t0, t1, _ in segments(T):
                            tap = [col(L, PCW + 2 * w + j) for w in range(3)]
                            link(dve.tensor_scalar(cv[:, t0:t1], cgz[:, j, t0:t1], tap[1], col(L, PCB + j), ALU.mult, ALU.add))
                            link(dve.scalar_tensor_tensor(cv[:, t0 + 1:t1], cgz[:, j, t0:t1 - 1], tap[0], cv[:, t0 + 1:t1],
                                                          ALU.mult, ALU.add))
                            link(dve.scalar_tensor_tensor(cv[:, t0:t1 - 1], cgz[:, j, t0 + 1:t1], tap[2], cv[:, t0:t1 - 1],
                                                          ALU.mult, ALU.add))
                        read_out(dve, proj(L, "b", j))
                        dve.tensor_tensor(bg[:, j, 0:T], bg[:, j, 0:T], cv[:, 0:T], ALU.mult).then_inc(conv_f, 1)
                elif kind == "z":
                    tt = e[2]
                    b, q = tt % 2, TT_ALL * L + tt
                    dve.wait_ge(full["z"], PLAN.full[e])
                    link(dve.tensor_scalar(zs[:, b, :], unit_of(e), -1.0, None, ALU.mult))
                    dve.tensor_tensor(zs[:, b, :], zs[:, b, :], unit_of(e), ALU.min).then_inc(zneg_ready, 1)
                    dve.wait_ge(zln_ready, q + 1)
                    m = dve.scalar_tensor_tensor(ls[:, tt, :], unit_of(e), 0.0, zs[:, b, :], ALU.min, ALU.subtract)
                    m.then_inc(free[PLAN.before[e][0][0]], 1)
                elif kind == "suffix":
                    g, tt = STEPS[e[2]]
                    if e[2] == 0:
                        read_out(dve, ("turn", L, 1))
                    read_out(dve, e)
                    dve.tensor_tensor(eu[:, g, :], eu[:, g, :], ktok[:, tt, :], ALU.mult).then_inc(ku_ready, 1)
                elif kind == "dstate":
                    g, tt = STEPS[e[2]]
                    dve.wait_ge(full["dstate"], PLAN.full[e])
                    order = (0, 1) if g == 0 else (1, 0)
                    for c in order:
                        at = 2 * tt + c
                        after = {11: 0, 7: None}.get(at, at + 1) if g == 0 else {8: 7, 0: None}.get(at, at - 1)
                        if after is None:
                            continue
                        final = (g, at) in ((0, 6), (1, 1))
                        for pr in range(2):
                            m = dve.scalar_tensor_tensor(S[:, g, after, pr, :], S[:, g, at, pr, :],
                                                         dec[:, e[2], 2 * pr + c:2 * pr + c + 1],
                                                         G[c][:, pr * DV:(pr + 1) * DV], ALU.mult, ALU.add)
                            if pr == 1:
                                m.then_inc(free[f"G{c}"], 1)
                            elif final:
                                m.then_inc(free[f"G{1 - c}"], 1)
                        dve.wait_ge(free[f"G{c}"], PLAN.before[e][c][1] + 1)
                elif kind == "four":
                    tt = e[2]
                    q = 6 * L + tiles_of(L).index(tt)
                    ab = [t[:, 0:4, :].rearrange("p a b -> p (a b)")[:, tt * 512:(tt + 1) * 512] for t in (h_hi, h_lo)]
                    dve.wait_ge(ab_hi, q + 1)
                    m = dve.tensor_tensor(ab[1], unit_of(e), ab[0].bitcast(F32), ALU.subtract)
                    m.then_inc(free[PLAN.before[e][0][0]], 1)
                elif kind == "dft":
                    T = tokens(L)
                    if e[2] == 0:
                        for j in range(2):
                            dve.wait_ge(conv_hi, 2 * L + j + 1)
                            dve.tensor_tensor(h_lo[:, 6 + j, 0:T], bg[:, j, 0:T], h_hi[:, 6 + j, 0:T].bitcast(F32),
                                              ALU.subtract).then_inc(conv_ready, 1)
                    if e[2] == (3 if L else 4):
                        for ch in range(2):
                            dve.wait_ge(four_hi, 2 * L + ch + 1)
                            m = dve.tensor_tensor(h_lo[:, 4 + ch, 0:T], A[ch][:, 0:T], h_hi[:, 4 + ch, 0:T].bitcast(F32),
                                                  ALU.subtract)
                            m.then_inc(free[f"A{ch}"], 1)
                elif kind == "gate":
                    tt, g = e[2], e[3]
                    b = turn(L, tt)
                    if tiles_of(L).index(tt) == 0 and g == 0:
                        link(dve.memset(Pm[:, :, :, :, :, :], 0.0))
                    read_out(dve, e)
                    q_, k_ = qT[:, :, tt * P:(tt + 1) * P], kT[:, :, tt * P:(tt + 1) * P]
                    dve.tensor_tensor(E[:, b, g, 0, :, :], E[:, b, g, 0, :, :], q_, ALU.mult)
                    dve.tensor_tensor(E[:, b, g, 1, :, :], E[:, b, g, 1, :, :], k_, ALU.mult)
                    dve.tensor_tensor(E[:, b, g, 2, :, :], E[:, b, g, 2, :, :], q_, ALU.mult).then_inc(qk_ready, 1)
                elif kind == "score":
                    b = turn(L, e[2])
                    dve.wait_ge(full["score"], PLAN.full[e])
                    if tiles_of(L).index(e[2]) >= 2:
                        dve.wait_ge(full["o"], nth(L, e[2]) - 1)
                    for hp in range(2):
                        for g in range(2):
                            m = dve.copy_predicated(Pm[:, b, hp, g, :, :],
                                                    mask[:, g:g + 1, :].to_broadcast([P, 2, P]),
                                                    N[:, hp * 512 + g * 256:hp * 512 + (g + 1) * 256].rearrange("p (r t) -> p r t", r=2))
                        m.then_inc(free[f"N{hp}"], 1)
                elif kind == "msq":
                    tt = e[2]
                    b, q = turn(L, tt), nth(L, tt)
                    dve.wait_ge(orstd_ready, q + 1)
                    flat = rb[:, b, :, :].rearrange("p (q r) t -> p q (r t)", q=2)
                    m = dve.tensor_tensor(flat, o_all(b, 0), flat, ALU.mult)
                    m.then_inc(free[f"A{b}"], 1)
                    read_out(dve, ("o", L, tt))
                    for h in range(HEADS):
                        at = (h % 2) * 2 + h // 2
                        m = dve.scalar_tensor_tensor(rb[:, b, at, :], rb[:, b, at, :], col(L, PGN + h),
                                                     r_s[:, h, tt * P:(tt + 1) * P], ALU.mult, ALU.mult)
                    m.then_inc(yg_ready, 1)
                    dve.wait_ge(yhi_ready, q + 1)
                    dve.tensor_tensor(y_all(h_lo, tt), rb[:, b, :, :].rearrange("p (q r) t -> p q r t", q=2),
                                      y_all(h_hi, tt).bitcast(F32), ALU.subtract).then_inc(ylo_ready, 1)
                elif kind in ("wout", "ffn_out"):
                    T = tokens(L)
                    last = kind == "wout" or e[2] == 2
                    add = kind == "ffn_out" and e[2] > 0
                    if last:
                        link(dve.memset(ssq[:, 0:T], 0.0))
                    for j in range(2):
                        dve.wait_ge(free[f"A{j}"], PLAN.acc[e][j])
                    base = steps[0]
                    sums = KT * (2 * L + (kind == "ffn_out"))
                    with dve.Fori(0, KT // 4, 1) as i:
                        for j in range(4):
                            ym = y[:, bass.ds(4 * i + j, 1), 0:T]
                            src = A[j % 2][:, 0:T].rearrange("p (a t) -> p a t", a=1)
                            dve.wait_ge(chunk_used, 4 * i + (n0 + j + 1))
                            m = dve.tensor_tensor(ym, src, ym, ALU.add) if add else dve.tensor_copy(ym, src)
                            m.then_inc(free[f"A{j % 2}"], 1)
                            if last:
                                dve.wait_ge(free[f"A{j % 2}"], 2 * i + (PLAN.acc[e][j % 2] + j // 2 + 1))
                                s3 = sqb[:, 0:1, 0:T]
                                dve.tensor_tensor(s3, ym, ym, ALU.mult).then_inc(dve_step, 1)
                                dve.wait_ge(dve_step, 4 * i + (base + j + 1))
                                q3 = sqb[:, 1:2, 0:T]
                                dve.tensor_tensor(q3, q3, s3, ALU.add).then_inc(ssq_ready, 1)
                                dve.wait_ge(ssq_ready, 4 * i + (sums + j + 1))
                    steps[0] += KT if last else 0
                elif kind == "ffn_in":
                    T, per = tokens(L), 4 if L == 0 else 2
                    nb = BLOCKS[e[2]]
                    p0 = HID * L + e[3]
                    pairs, at = 4 // per, per - 2
                    with dve.Fori(0, nb // pairs, 1) as i:
                        for q in range(pairs):
                            dve.wait_ge(free["A0"], pairs * i + (PLAN.acc[e][0] + q + 1))
                            dve.wait_ge(chunk_used, 4 * i + (n0 + q * per + at + 2))
                            dve.tensor_tensor(sil[:, 0:T], sil[:, 0:T], A[1][:, 0:T], ALU.mult).then_inc(free["A1"], 1)
                            dve.wait_ge(ghi_ready, pairs * i + (p0 + q + 1))
                            gp = bass.ds(pairs * i + q, 1)
                            dve.tensor_tensor(g_lo[:, gp, 0:T], sqb[:, 0:1, 0:T], g_hi[:, gp, 0:T].bitcast(F32),
                                              ALU.subtract).then_inc(g_ready, 1)
                elif kind == "postnorm":
                    T = norm_tokens(e)
                    no = 2 * L + e[2]
                    if e[2] == 0:
                        dve.wait_ge(x_back, 32 * (L + 1))
                    dve.wait_ge(rstd_ready, 1 + 2 * no + 1)
                    for k in range(KT):
                        if k % 2:
                            dve.wait_ge(yn_ready, 4 * no + k // 2 + 1)
                        else:
                            link(dve.tensor_tensor(y[:, k, 0:T], y[:, k, 0:T], rstd[:, 0:T], ALU.mult))
                        for t0, t1, v in segments(T):
                            m = dve.scalar_tensor_tensor(x[:, k, t0:t1], y[:, k, t0:t1], coef[:, L, 3 * e[2] + 2, k, v:v + 1],
                                                         x[:, k, t0:t1], ALU.mult, ALU.add)
                        m.then_inc(xnew_ready, 1)
                elif kind == "prenorm":
                    T = norm_tokens(e)
                    q = pre_no(L, e[2])
                    dve.wait_ge(rstd_ready, 2 * q + 1)

                    def low(k):
                        dve.wait_ge(hhi_ready, KT * q + k + 1)
                        dve.tensor_tensor(h_lo[:, k, 0:T], y[:, k, 0:T], h_hi[:, k, 0:T].bitcast(F32),
                                          ALU.subtract).then_inc(hlo_ready_v, 1)

                    for k in range(KT):
                        link(dve.tensor_tensor(y[:, k, 0:T], x[:, k, 0:T], rstd[:, 0:T], ALU.mult))
                        for t0, t1, v in segments(T):
                            c = [coef[:, L, 3 * e[2] + w, k, v:v + 1] for w in range(2)]
                            m = dve.tensor_scalar(y[:, k, t0:t1], y[:, k, t0:t1], c[1], c[0], ALU.mult, ALU.add)
                        m.then_inc(haff_ready, 1)
                        if k == 4:
                            low(3)
                    low(7)


def stream_layout(a):
    out = np.zeros((N_CHUNKS, P, 1024), np.float32)
    ang = lambda n: 2 * np.pi * (np.outer(np.arange(n), np.arange(n)) % n) / n
    dft = {}
    for n in (SEQ, CTX):
        s = 1.0 / np.sqrt(n * 64.0)
        dft[n] = (np.cos(ang(n)) * s, -np.sin(ang(n)) * s)

    def tile(w, k0, K, m):
        return w[k0 * P:(k0 + K) * P, m:m + P].reshape(K, P, -1).transpose(1, 0, 2)

    for e in ORDER:
        for i, c in enumerate(chunks_of(e)):
            dst = out[PLAN.n0[e] + i]
            if c[0] == "dft":
                if c[1] < 4:
                    dst[:, 0:512], dst[:, 512:] = (t[c[1] * P:(c[1] + 1) * P] for t in dft[SEQ])
                else:
                    for s in range(2):
                        for q in range(2):
                            dst[:, (2 * s + q) * CTX:(2 * s + q + 1) * CTX] = dft[CTX][q][s * P:(s + 1) * P]
                continue
            name = {"mod": "w_mod", "in": "w_in", "out": "w_out", "fin": "w_ffn_in", "fout": "w_ffn_out"}[c[0]]
            w = a[name][c[1]]
            k0, K = (c[3], c[4]) if c[0] == "fout" else (0, KT)
            m = c[2] if c[0] == "in" else c[2] * P
            dst[:, 0:K * P] = tile(w, k0, K, m).reshape(P, K * P)
    return out


def constants():
    t = np.arange(P)
    same = (t[:, None] // CHUNK) == (t[None, :] // CHUNK)
    s_, t_ = t[:, None] % CHUNK, t[None, :] % CHUNK
    half = CHUNK // 2
    before, after = same & (s_ <= t_), same & (s_ >= t_)
    mats = [before, before * 1.0 - (same & (s_ < half)), after, after * 1.0 - (same & (s_ >= half)),
            same & (s_ > t_), same & (s_ < t_), np.stack([t < CHUNK, t >= CHUNK], 1)]
    mats = np.concatenate([m.astype(np.float32) for m in mats], 1) / 16.0
    masks = np.stack([before, after], 1).astype(np.int32)
    a = 2 * np.pi * (np.outer(np.arange(64), np.arange(64)) % 64) / 64
    chan = np.zeros((P, 2 * P))
    for g in range(2):
        r = slice(g * 64, g * 64 + 64)
        chan[r, g * 64:g * 64 + 64] = np.cos(a)
        chan[r, P + g * 64:P + g * 64 + 64] = np.sin(a)
    wide = np.concatenate([chan, np.full((P, P), 1.0 / D), np.full((P, P), 1.0 / DV), np.eye(P),
                           np.tile(np.eye(2), (64, 1))], 1)
    rows = SEQ // 64
    row, c = np.repeat(np.arange(rows, dtype=np.float32), 64), np.tile(np.arange(64, dtype=np.float32), rows)
    quarter = D // 4
    f = (1.0 / (np.float32(10000.0) ** (np.arange(quarter, dtype=np.float32) / np.float32(quarter)))).astype(np.float32)
    enc = lambda p: np.concatenate([np.sin(p[:, None] * f[None]), np.cos(p[:, None] * f[None])], -1)
    pos = np.concatenate([enc(row), enc(c)], -1).astype(np.float32)
    return masks, mats.astype(np.float32), wide.astype(np.float32), pos


def feature_major(a):
    return np.ascontiguousarray(a.T.reshape(-1, P, a.shape[0]).transpose(1, 0, 2))


def kernel(**inputs):
    import numpy as _np
    import concourse.bacc as _bacc
    from concourse import mybir as _mybir
    from concourse.bass_utils import run_bass_kernel_spmd as _run

    a = {k: _np.asarray(v) for k, v in inputs.items()}
    masks, mats, wide, pos = constants()
    column = lambda v: v.reshape(-1, P).T
    cols = []
    for L in range(DEPTH):
        cols += [column(a[k][L]) for k in ("b_mod", "g_mix_pre", "g_mix_post", "g_ffn_pre", "g_ffn_post", "conv_w",
                                           "conv_b", "gla_norm_w")]
    cols += [column(a["c"][0]), column(a["c_ctx"])]
    wdec = _np.zeros((33, DEPTH, 512), _np.float32)
    for L in range(DEPTH):
        wdec[0:16, L, 0:256], wdec[32, L, 0:256] = a["w_dec_f"][L], a["b_dec_f"][L]
        wdec[16:32, L, 256:512], wdec[32, L, 256:512] = a["w_dec_b"][L], a["b_dec_b"][L]
    arrays = {
        "stream": stream_layout(a),
        "xT": _np.concatenate([feature_major(a["x"][0]), feature_major(a["ctx"][0])], 2),
        "pos_row": feature_major(pos[::64, 0:D // 2]),
        "pos_col": feature_major(pos[0:64, D // 2:]),
        "cols": _np.concatenate(cols, 1),
        "wdec": wdec,
        "masks": masks,
        "mats": mats,
        "wide": wide,
    }
    arrays = {k: _np.ascontiguousarray(v) for k, v in arrays.items()}
    nc = _bacc.Bacc("TRN2", target_bir_lowering=False, num_devices=1)
    args = [nc.dram_tensor(k, v.shape, _mybir.dt.from_np(v.dtype), kind="ExternalInput").ap() for k, v in arrays.items()]
    args.append(nc.dram_tensor("x_keep", (P, KT, TOK), F32, kind="Internal").ap())
    args.append(nc.dram_tensor("out_0_dram", (P, KT, SEQ), F32, kind="ExternalOutput").ap())
    bass_hybrid_block(nc, *args)
    r = _run(nc, [arrays], core_ids=[0])
    got = r.results[0]["out_0_dram"]
    return _np.ascontiguousarray(got.transpose(1, 0, 2).reshape(D, SEQ).T)[None]
```

```python
from contextlib import ExitStack

import numpy as np

import concourse.bass as bass
from concourse import mybir
from concourse.alu_op_type import AluOpType as ALU

F32 = mybir.dt.float32
F32R = mybir.dt.float32r
I32 = mybir.dt.int32
ACT = mybir.ActivationFunctionType

P = 128
DEPTH, D, SEQ, CTX = 2, 1024, 512, 256
TOK = SEQ + CTX
KT = D // P
TT_ALL, TT_LAT = TOK // P, SEQ // P
HEADS, DK, DV, RANK, CHUNK = 4, 64, 128, 16, 64
HID = 2816 // P
BLOCKS = (8, 8, 6)
EPS = 1e-6
LN_SET = "natural_log_exp_and_others"

KW, VW, FW = HEADS * DK, HEADS * DV, 256
C_LR = KW + VW
C_Q = C_LR + 2 * RANK
C_R = C_Q + KW
C_F = C_R + VW
C_B, C_C, C_U = C_F + FW, C_F + 2 * FW, C_F + 3 * FW
W_IN = ([("lr", 0, C_LR)] + [("k", j, j * P) for j in range(2)] + [("v", j, KW + j * P) for j in range(4)]
        + [("r", j, C_R + j * P) for j in range(4)] + [("q", j, C_Q + j * P) for j in range(2)]
        + [("f", j, C_F + j * P) for j in range(2)] + [("c", j, C_C + j * P) for j in range(2)]
        + [("u", j, C_U + j * P) for j in range(2)] + [("b", j, C_B + j * P) for j in range(2)])
STATE_NAMES = ("lr", "k", "v")
STEPS = [(0, 4), (1, 5), (0, 5), (1, 4), (0, 0), (1, 3), (0, 1), (1, 2), (0, 2), (1, 1), (0, 3), (1, 0)]
MC = 66
FILLS = ((3, 3, 3, 3, 3, 3), (3, 3, 3, 3))
MOD_BETWEEN = ((16, 48), (18, 36))
COEFS = ((0, 16), (32, 48))
PB, PG, PCW, PCB, PGN, PCOLS = 0, 48, 80, 86, 88, 92
N_MOD0 = 16
BEFORE_X = 4


def tiles_of(L):
    return (4, 5, 0, 1, 2, 3) if L == 0 else (0, 1, 2, 3)


def fill_of(L, tt):
    sizes = FILLS[0] + FILLS[1]
    at = len(FILLS[0]) * L + tiles_of(L).index(tt)
    return sum(sizes[:at]) + (MOD_BETWEEN[1][1] - MOD_BETWEEN[1][0] if L else 0), sizes[at]


def before_fill(L, tt):
    return (FILLS[0] + FILLS[1])[len(FILLS[0]) * L + tiles_of(L).index(tt) - 1]


def build_order():
    order = [("start", 0, 0, BEFORE_X)]
    order += [("sq", 0, 0, s, k) for s in range(2) for k in range(KT)]
    order += [("start", 0, BEFORE_X, N_MOD0 - BEFORE_X), ("keep", 0, 0), ("keep", 0, 1), ("rstd", 0, 0, 0), ("rstd", 0, 0, 1)]
    order += [("nrm", 0, 0, s, k) for s in range(2) for k in range(KT)]
    order += [("head", -1, 1, j, s) for s in range(2) for j in range(2)]
    mod, before = [0], [None]

    def mods(L, n):
        first, end = MOD_BETWEEN[L]
        if before[0]:
            order.append(("mturn", L) + before[0])
            before[0] = None
        if mod[0] < end:
            before[0] = (mod[0], n)
            order.append(("mod", L, mod[0], n))
            mod[0] += n

    def tail(L, w):
        nxt = (L, 1) if w == 0 else (L + 1, 0)
        more = nxt[0] < DEPTH
        late = lambda m: order.append(("late", L, w, m))

        def steps(kind, s, ks):
            if kind == "res":
                order.extend(("res", L, w, s, k) for k in ks)
            elif more:
                order.extend((kind,) + nxt + (s, k) for k in ks)

        def take(m):
            order.append(("take", L, w, m))

        def ahead(m):
            order.append(("ahead", L, w, m))

        if L == 0:
            late(0)
            order.append(("mean", L, w, 0))
            late(1)
            ahead(0)
            take(0)
            steps("res", 0, (0, 1))
            take(1)
            for i in range(4):
                late(2 + i)
                ahead(1 + i)
                steps("sq", 0, ((0,), (1, 2), (3, 4), (5, 6, 7))[i])
                if i < 3:
                    steps("res", 0, (2 * i + 2, 2 * i + 3))
                take(2 + i)
            order.append(("rstd",) + nxt + (0,))
            if w:
                order.append(("keep", 1, 0))
            late(6)
            ahead(5)
            steps("nrm", 0, range(3))
            late(7)
            ahead(6)
            take(6)
            steps("nrm", 0, range(3, KT))
            ahead(7)
            take(7)
            order.append(("head", L, w, 0, 0))
            order.append(("mean", L, w, 1))
            steps("res", 1, range(KT))
            order.append(("head", L, w, 1, 0))
            steps("sq", 1, range(KT))
            if w:
                order.append(("keep", 1, 1))
            order.append(("rstd",) + nxt + (1,))
            steps("nrm", 1, range(KT))
            order.extend((("head", L, w, 0, 1), ("head", L, w, 1, 1)))
        else:
            order.append(("mean", L, w, 0))
            steps("res", 0, range(KT))
            if more:
                steps("sq", 0, range(KT))
                order.append(("rstd",) + nxt + (0,))
                steps("nrm", 0, range(KT))
                order.extend((("head", L, w, 0, 0), ("head", L, w, 1, 0)))
            else:
                order.append(("send", 0))

    for L in range(DEPTH):
        z, t, s, d = list(range(TT_ALL)), list(range(6)), list(range(12)), list(range(12))
        mod[0] = MOD_BETWEEN[L][0]
        for x, (name, j, _) in enumerate(W_IN):
            order.append(("proj", L, x))
            if 1 <= x <= 3:
                order.append(("z", L, z.pop(0)))
                order.append(("z", L, z.pop(0)))
            if 4 <= x <= 8:
                order.append(("turn", L, t.pop(0)))
            if x >= (3 if L else 1):
                mods(L, 2 if L == 0 and 5 <= x < 17 else 1)
            if x == 4:
                order.append(("turn", L, t.pop(0)))
            if x >= 8:
                if s:
                    order.append(("suffix", L, s.pop(0)))
                if x >= 9 and d:
                    order.append(("dstate", L, d.pop(0)))
        mods(L, 0)
        order.append(("modend", L))
        while d:
            if s:
                order.append(("suffix", L, s.pop(0)))
            order.append(("dstate", L, d.pop(0)))
        tiles = tiles_of(L)
        for tt in tiles:
            order.append(("four", L, tt))
        for g in (0, 1):
            order.append(("gate", L, tiles[0], g))
        for s4 in range(5 if L == 0 else 4):
            order.append(("dft", L, s4))
        for a, tt in enumerate(tiles):
            order.append(("score", L, tt))
            order.append(("fill", L, tt))
            if a + 1 < len(tiles):
                for g in (0, 1):
                    order.append(("gate", L, tiles[a + 1], g))
            if a:
                order.append(("msq", L, tiles[a - 1]))
            order.append(("o", L, tt))
        order.append(("msq", L, tiles[-1]))
        order.append(("coef", L))
        order.append(("wout", L))
        tail(L, 0)
        first = 0
        for b, nb in enumerate(BLOCKS):
            order.append(("ffn_in", L, b, first))
            order.append(("ffn_out", L, b))
            first += nb
        tail(L, 1)
    return order


ORDER = build_order()


def chunks_of(e):
    kind, L = e[0], e[1]
    if kind == "start":
        return [("mod", L, m) for m in range(e[2], e[2] + e[3])]
    if kind == "fill":
        m, n = fill_of(L, e[2])
        return [("mod", 1, i) for i in range(m, m + n)]
    if kind == "mod":
        return [("mod", L, e[2] + j) for j in range(e[3])]
    if kind == "proj":
        return [("in", L, W_IN[e[2]][2])]
    if kind == "dft":
        return [("dft", e[2])]
    if kind == "late":
        return [("out", L, e[3]) if e[2] == 0 else ("fout", L, e[3], sum(BLOCKS[:2]), BLOCKS[2])]
    if kind == "wout":
        return [("out", L, m) for m in range(KT)]
    if kind == "ffn_in":
        out = []
        for p in range(e[3], e[3] + BLOCKS[e[2]]):
            out += [("fin", L, p), ("fin", L, HID + p)]
        return out
    if kind == "ffn_out":
        first = sum(BLOCKS[:e[2]])
        return [("fout", L, m, first, BLOCKS[e[2]]) for m in range(KT)]
    return []


def tokens(L, name=None):
    return TOK if L == 0 or name in STATE_NAMES else SEQ


def segments(T):
    return [(0, SEQ, 0)] + ([(SEQ, TOK, 1)] if T > SEQ else [])


def parts(e):
    both = e[1] == 0 or (e[0] in ("sq", "rstd", "nrm") and e[2] == 0)
    return [(0, SEQ, 0), (SEQ, TOK, 1)] if both else [(0, SEQ, 0)]


def sums_before(L, w):
    return KT * (2 * w if L == 0 else 4 + w)


def span(e):
    return parts(e)[e[3]]


FULL = ("z", "turn", "suffix", "dstate", "four", "gate", "score", "o", "msq", "mean")


class Plan:

    def __init__(self):
        self.n0, self.full, self.before, self.acc = {}, {}, {}, {}
        n, used, kinds, copies, acc = 0, dict.fromkeys(("A0", "A1", "N0", "N1", "G0", "G1"), 0), {}, {}, 0
        g = 0
        for e in ORDER:
            kind, L = e[0], e[1]
            self.n0[e] = n
            n += len(chunks_of(e))
            units = []
            if kind == "start" and e[2] == 0:
                units = ["G0", "A0", "A1"]
            elif kind == "proj":
                if e[2] == 0:
                    acc = 0
                units = [f"A{acc % 2}"]
                self.acc[e] = acc % 2
                acc += 1
            elif kind in ("z", "turn", "four"):
                if kind == "turn":
                    units = ["G0", "G1"]
                else:
                    units = [f"G{g % 2}"]
                    g += 1
            elif kind == "mod" and e[2] == MOD_BETWEEN[L][0]:
                units = ["N0"]
            elif kind == "suffix":
                units = ["N1"]
            elif kind == "dstate":
                units = ["G0", "G1"]
            elif kind == "gate":
                units = [f"G{e[3]}"]
            elif kind == "dft" and e[2] == 0:
                units = ["A0", "A1"]
            elif kind == "score":
                units = ["N0", "N1"]
            elif kind == "o":
                units = [f"A{self.tile_turn(L, e[2])}"]
            elif kind == "wout":
                units = []
                self.acc[e] = (used["A0"], used["A1"])
                used["A0"] += KT // 2
                used["A1"] += KT // 2
            elif kind == "ffn_in":
                self.acc[e] = (used["A0"], used["A1"])
                used["A0"] += BLOCKS[e[2]]
                used["A1"] += BLOCKS[e[2]]
            elif kind == "ffn_out":
                self.acc[e] = (used["A0"], used["A1"])
                used["A0"] += KT // 2
                used["A1"] += KT // 2
            elif kind == "late":
                units = [f"A{e[3] % 2}"]
            elif kind == "mean" or kind == "sq" and e[4] == 0:
                units = [f"N{e[3]}"]
            self.before[e] = [(u, used[u]) for u in units]
            for u in units:
                used[u] += 1
            fk = kind
            if kind not in FULL:
                fk = None
            if fk:
                kinds[fk] = kinds.get(fk, 0) + 1
                self.full[e] = kinds[fk]
        self.total = n

    @staticmethod
    def tile_turn(L, tt):
        return tiles_of(L).index(tt) % 2


PLAN = Plan()
ROWS = {e: i + 1 for i, e in enumerate(x for x in ORDER if x[0] in ("mod", "fill"))}
LOW_V = (0, 3, 5, 7)
SQ, NRM, RES = ({e: i + 1 for i, e in enumerate(x for x in ORDER if x[0] == kind)} for kind in ("sq", "nrm", "res"))
YN = {e: i + 1 for i, e in enumerate(x for x in ORDER if x[0] == "res" and x[1] == 1 and x[4] % 2)}
RSTD = {e: i + 1 for i, e in enumerate(x for x in ORDER if x[0] in ("mean", "rstd"))}
LOWS = {e: i + 1 for own in (True, False)
        for i, e in enumerate(x for x in ORDER if x[0] == "nrm" and (x[4] in LOW_V) == own)}


def before_pre(e):
    return ("res",) + ((e[1], 0) if e[2] else (e[1] - 1, 1)) + e[3:]


WIDTH = [c[4] * P if c[0] == "fout" else 1024 for e in ORDER for c in chunks_of(e)]
RAW, RING = 2, 4
N_CHUNKS = PLAN.total


def bass_hybrid_block(nc: bass.Bass, stream, xT, pos_row, pos_col, cols, wdec, masks, mats, wide, x_keep, out):
    with ExitStack() as ctx:
        def sb(name, shape, dt=F32, stack=None):
            return (stack or ctx).enter_context(nc.sbuf_tensor(name, shape, dt))

        def sem(name):
            return ctx.enter_context(nc.semaphore(name))

        h_hi = sb("h_hi", [P, KT, TOK], F32R)
        h_lo = sb("h_lo", [P, KT, TOK], F32R)
        raw = sb("raw", [P, RAW, 1024])
        w_hi = sb("w_hi", [P, RING, 1024], F32R)
        w_lo = sb("w_lo", [P, RING, 1024], F32R)
        par = sb("par", [P, DEPTH * PCOLS + 16])
        wd = sb("wd", [33, 512])
        mask = sb("mask", [P, 2, P], I32)
        mat = sb("mat", [P, 4 * P + 2 * P + 2])
        chan = sb("chan", [P, 2 * P])
        one_d = sb("one_d", [P, P])
        one_v = sb("one_v", [P, P])
        ident = sb("ident", [P, P])
        eps = sb("eps", [P, 1])
        csil = sb("csil", [P, KT, 2])
        c4 = sb("c4", [P, KT, MC], F32R)
        sel = sb("sel", [4, 2])
        modT = sb("modT", [P, 48, 2])
        coef = sb("coef", [P, DEPTH, 6, KT, 2])
        dec = sb("dec", [P, 12, 4])

        start, mix, ffn = ExitStack(), ExitStack(), ExitStack()
        with start:
            raw0 = sb("raw0", [P, N_MOD0, 1024], stack=start)
            mrow0 = sb("mrow0", [2, N_MOD0 * P], stack=start)
        with ffn:
            y = sb("y", [P, KT, TOK], stack=ffn)
            hidden, norm = ExitStack(), ExitStack()
            with hidden:
                g_hi = sb("g_hi", [P, 8, TOK], F32R, stack=hidden)
                g_lo = sb("g_lo", [P, 8, TOK], F32R, stack=hidden)
            with norm:
                sb("before_rstd", [P, 7, TOK], stack=norm)
                rstd = sb("rstd", [P, TOK], stack=norm)
                sb("before_sqs", [P, 6, TOK], stack=norm)
                sqs = [sb(f"sqs{j}", [P, TOK], stack=norm) for j in range(2)]
            sb("hidden_place", [P, 16, TOK], stack=ffn)
            sqb = sb("sqb", [P, 2, TOK], stack=ffn)
            x = sb("x", [P, KT, TOK], stack=ffn)
            posr = sb("posr", [P, 4, 8], stack=ffn)
            posc = sb("posc", [P, 4, 64], stack=ffn)
        ssq, sil = sqb[:, 1, :], sqb[:, 0, :]
        with mix:
            kT = sb("kT", [P, 2, TOK], stack=mix)
            qT = sb("qT", [P, 2, TOK], stack=mix)
            ktok = sb("ktok", [P, TT_ALL, KW], stack=mix)
            vtok = sb("vtok", [P, TT_ALL, VW], stack=mix)
            ls = sb("ls", [P, TT_ALL, 2 * KW], stack=mix)
            S = sb("S", [P, 2, 12, 2, DV], stack=mix)
            r_s = sb("r_s", [P, 4, TOK], stack=mix)
            early, late = ExitStack(), ExitStack()
            with early:
                lrT = sb("lrT", [33, TOK], stack=early)
                mrow = sb("mrow", [4, 2 * P], stack=early)
                eu = sb("eu", [P, 2, KW], stack=early)
                vst = sb("vst", [P, 2, TOK], stack=early)
                zs = sb("zs", [P, 2, 2 * KW], stack=early)
                cgz = sb("cgz", [P, 2, TOK], stack=early)
                bg = sb("bg", [P, 2, TOK], stack=early)
            uF = vst
            cv = zs[:, :, :].rearrange("p a b -> p (a b)")[:, 0:TOK]
            with late:
                E = sb("E", [P, 2, 2, 3, 2, P], stack=late)
                Pm = sb("Pm", [P, 2, 2, 2, 2, P], stack=late)
                osq = sb("osq", [P, 4 * P], stack=late)
                frow = sb("frow", [4, 3 * P], stack=late)
                rb = sb("rb", [P, 2, 4, P], stack=late)

        def ps(name, n):
            return ctx.enter_context(nc.psum_tensor(name, [P, n], F32))

        A = [ps("A0", 1024), ps("A1", 1024)]
        N = ps("N", 1024)
        G = [ps("G0", 512), ps("G1", 512)]

        first_in = [sem(f"first_in{j}") for j in range(N_MOD0)]
        raw_in = [sem(f"raw_in{j}") for j in range(RAW)]
        hi_done, lo_done, chunk_used = sem("hi_done"), sem("lo_done"), sem("chunk_used")
        free = {u: sem(f"free_{u}") for u in ("A0", "A1", "N0", "N1", "G0", "G1")}
        full = {k: sem(f"full_{k}") for k in FULL}
        one_in = sem("one_in")
        par_in, consts_in, x_in, ctx_in, wd_in = (
            sem("par_in"), sem("consts_in"), sem("x_in"), sem("ctx_in"), sem("wd_in"))
        x_kept, x_back, out_sent = sem("x_kept"), sem("x_back"), sem("out_sent")
        eps_set = sem("eps_set")
        c_ready, csil_ready, c4hi_ready = sem("c_ready"), sem("csil_ready"), sem("c4hi_ready")
        lr_ones = sem("lr_ones")
        zneg_ready, zln_ready, ku_ready = sem("zneg_ready"), sem("zln_ready"), sem("ku_ready")
        ab_hi, four_hi = sem("ab_hi"), sem("four_hi")
        conv_f, conv_hi, conv_ready = sem("conv_f"), sem("conv_hi"), sem("conv_ready")
        qk_ready = sem("qk_ready")
        osq_ready, orstd_ready, yg_ready, yhi_ready, ylo_ready = (
            sem("osq_ready"), sem("orstd_ready"), sem("yg_ready"), sem("yhi_ready"), sem("ylo_ready"))
        ssq_ready, rstd_ready, xnew_ready, sq_ready, sq_used = (
            sem("ssq_ready"), sem("rstd_ready"), sem("xnew_ready"), sem("sq_ready"), sem("sq_used"))
        haff_ready, hhi_ready = sem("haff_ready"), sem("hhi_ready")
        yn_ready = sem("yn_ready")
        hlo_ready_p, hlo_ready_v = sem("hlo_ready_p"), sem("hlo_ready_v")
        mod_read, coef_step, mrow_ready, mod_turned = sem("mod_read"), sem("coef_step"), sem("mrow_ready"), sem("mod_turned")
        sel_in, c4_zero = sem("sel_in"), sem("c4_zero")
        ghi_ready, g_ready = sem("ghi_ready"), sem("g_ready")
        dve_step, act_step = sem("dve_step"), sem("act_step")

        def col(L, at, n=1):
            return par[:, L * PCOLS + at:L * PCOLS + at + n]

        def turn(L, tt):
            return tiles_of(L).index(tt) % 2

        def nth(L, tt):
            return 6 * L + tiles_of(L).index(tt)

        def lo_wait(eng, n):
            eng.wait_ge(lo_done, n - N_MOD0 + 1)

        def read_out(eng, e):
            for u, before in PLAN.before[e]:
                eng.wait_ge(free[u], before + 1)

        def proj(L, name, j):
            return ("proj", L, [w[:2] for w in W_IN].index((name, j)))

        def h_wait(eng, L, w, s, k):
            e = ("nrm", L, w, s, k)
            eng.wait_ge(hlo_ready_v if k in LOW_V else hlo_ready_p, LOWS[e])

        def unit_of(e):
            u = PLAN.before[e][0][0]
            return G[int(u[1])][:, :]

        def o_at(b, h):
            pr, hp = divmod(h, 2)
            return A[b][:, hp * 512 + pr * P:hp * 512 + (pr + 1) * P]

        def o_all(b, mean):
            return A[b][:, :].rearrange("p (q m r) -> p q m r", q=2, m=2)[:, :, mean, :]

        def y_all(h, tt):
            return h[:, 0:4, tt * P:(tt + 1) * P].rearrange("p (r q) t -> p q r t", q=2)

        block = ctx.enter_context(nc.Block())

        @block.sync
        def _(sp):
            sp.dma_start(par[:, :], cols).then_inc(par_in, 16)
            sp.dma_start(one_d[:, :], wide[:, 256:384]).then_inc(one_in, 16)
            for n in range(N_MOD0 + RAW):
                if n == BEFORE_X:
                    sp.dma_start(x[:, :, 0:SEQ], xT[:, :, 0:SEQ]).then_inc(x_in, 16)
                    sp.dma_start(x[:, :, SEQ:TOK], xT[:, :, SEQ:TOK]).then_inc(ctx_in, 16)
                if n < N_MOD0:
                    sp.dma_start(raw0[:, n, :], stream[n]).then_inc(first_in[n], 16)
                else:
                    sp.dma_start(raw[:, n % RAW, :], stream[n]).then_inc(raw_in[n % RAW], 16)
            first = N_MOD0 + RAW
            with sp.Fori(0, (N_CHUNKS - first) // RAW, 1) as i:
                for j in range(RAW):
                    sp.wait_ge(lo_done, RAW * i + (j + 1))
                    sp.dma_start(raw[:, j, :], stream[RAW * i + (first + j)]).then_inc(raw_in[j], 16)
            for n in range(N_CHUNKS - (N_CHUNKS - first) % RAW, N_CHUNKS):
                lo_wait(sp, n - RAW)
                sp.dma_start(raw[:, n % RAW, :], stream[n]).then_inc(raw_in[n % RAW], 16)

        @block.gpsimd
        def _(pool):
            done = [N_MOD0]

            def low(n, i=None):
                at = n - N_MOD0 + 1
                pool.wait_ge(hi_done, at if i is None else 4 * i + at)
                pool.tensor_tensor(w_lo[:, n % RING, 0:WIDTH[n]], raw[:, n % RAW, 0:WIDTH[n]],
                                   w_hi[:, n % RING, 0:WIDTH[n]].bitcast(F32), ALU.subtract).then_inc(lo_done, 1)

            def low_until(end):
                while done[0] < end:
                    n = done[0]
                    same = next((m for m in range(n, end) if WIDTH[m] != WIDTH[n]), end)
                    rounds = (same - n) // 4
                    if rounds > 1:
                        with pool.Fori(0, rounds, 1) as i:
                            for j in range(4):
                                low(n + j, i)
                        n += 4 * rounds
                    for m in range(n, same):
                        low(m)
                    done[0] = same

            for e in ORDER:
                if e[0] == "res" and e in YN:
                    low_until(min(N_CHUNKS, PLAN.n0[e] + RING - 1))
                    k, (t0, t1, _) = e[4], span(e)
                    pool.wait_ge(rstd_ready, RSTD[("mean",) + e[1:4]])
                    pool.tensor_tensor(y[:, k, t0:t1], y[:, k, t0:t1], rstd[:, t0:t1], ALU.mult).then_inc(yn_ready, 1)
                if e[0] == "nrm" and e[4] not in LOW_V:
                    low_until(PLAN.n0[e] + (RAW if PLAN.n0[e] == N_MOD0 else RING - 1))
                    k, (t0, t1, _) = e[4], span(e)
                    pool.wait_ge(hhi_ready, NRM[e])
                    pool.tensor_tensor(h_lo[:, k, t0:t1], y[:, k, t0:t1], h_hi[:, k, t0:t1].bitcast(F32),
                                       ALU.subtract).then_inc(hlo_ready_p, 1)
            low_until(N_CHUNKS)

        @block.tensor
        def _(pe):
            def unit_free(e):
                for u, before in PLAN.before[e]:
                    if before:
                        pe.wait_ge(free[u], before)

            def split_matmul(dst, n, ranges, k, src, first, last):
                s, (hi, lo) = n % RING, src
                wh, wl = w_hi[:, s, k * P:(k + 1) * P], w_lo[:, s, k * P:(k + 1) * P]
                for a, b, p in ((wh, hi, 0), (wh, lo, 1), (wl, hi, 2)):
                    for t0, t1, _ in ranges:
                        m = pe.matmul(dst[:, t0:t1], a, b[:, k, t0:t1], start=(first and p == 0), stop=(last and p == 2))
                return m

            def project(dst, n, ranges, src, K=KT, ready=None, first=0):
                for i in range(K):
                    k = (first + i) % K
                    if ready:
                        ready(k)
                    m = split_matmul(dst, n, ranges, k, src, i == 0, i == K - 1)
                return m

            def mod_matmul(dst, n):
                for k in range(KT):
                    for w in (w_hi, w_lo):
                        m = pe.matmul(dst, c4[:, k, :], w[:, n % RING, k * P:(k + 1) * P],
                                      start=(k == 0 and w is w_hi), stop=(k == KT - 1 and w is w_lo))
                m.then_inc(chunk_used, 1)

            def mod_turn(dst, rows, sums):
                for j in range(rows.shape[1] // P):
                    m = pe.matmul(dst[:, 2 * j:2 * j + 2], rows[:, j * P:(j + 1) * P], sums, start=True, stop=True)
                return m

            mrows = [0]

            def mod_turn_next(dst, src, n):
                mrows[0] += 1
                pe.wait_ge(mrow_ready, mrows[0])
                return mod_turn(dst, src[:, 0:n * P], sel[:, :])

            H = (h_hi, h_lo)
            for e in ORDER:
                kind, L = e[0], e[1]
                n0 = PLAN.n0[e]
                if kind == "start":
                    pe.wait_ge(csil_ready, 1)
                    for m in range(e[2], e[2] + e[3]):
                        pe.wait_ge(first_in[m], 16)
                        for k in range(KT):
                            mm = pe.matmul(A[m // 8][0:2, (m % 8) * P:(m % 8 + 1) * P], csil[:, k, :],
                                           raw0[:, m, k * P:(k + 1) * P], start=(k == 0), stop=(k == KT - 1))
                        mm.then_inc(chunk_used, 1)
                    if e[2]:
                        pe.wait_ge(sel_in, 16)
                        pe.wait_ge(consts_in, 16 * 5)
                        for h in range(2):
                            pe.wait_ge(free[f"A{h}"], 1)
                            mm = mod_turn(G[0][:, 16 * h:16 * h + 16], mrow0[:, h * 1024:(h + 1) * 1024], sel[0:2, :])
                        mm.then_inc(mod_turned, 1)
                elif kind == "mod":
                    pe.wait_ge(c_ready, 1)
                    unit_free(e)
                    for j in range(e[3]):
                        lo_wait(pe, n0 + j)
                        mod_matmul(N[0:MC, 256 + j * P:256 + (j + 1) * P], n0 + j)
                elif kind == "mturn":
                    mm = mod_turn_next(N[:, 2 * e[2]:2 * (e[2] + e[3])], mrow, e[3])
                    if e[2] + e[3] == MOD_BETWEEN[L][1]:
                        mm.then_inc(mod_turned, 1)
                elif kind == "fill":
                    b = turn(L, e[2])
                    unit_free(("o", L, e[2]))
                    m, n = fill_of(L, e[2])
                    if e[2] != tiles_of(L)[0]:
                        mod_turn_next(A[b][:, 896:896 + 2 * before_fill(L, e[2])], frow, before_fill(L, e[2]))
                    for j in range(n):
                        lo_wait(pe, n0 + j)
                        mod_matmul(A[b][0:MC, j * P:(j + 1) * P], n0 + j)
                elif kind == "coef":
                    pe.wait_ge(free["N0"], PLAN.before[("score", L, tiles_of(L)[-1])][0][1] + 1)
                    mod_turn_next(N[:, 0:2 * FILLS[L][-1]], frow, FILLS[L][-1]).then_inc(mod_turned, 1)
                elif kind == "proj":
                    name, j, _ = W_IN[e[2]]
                    if e[2] < 2:
                        continue
                    unit_free(e)
                    lo_wait(pe, n0)
                    project(A[PLAN.acc[e]], n0, segments(tokens(L, name)), H).then_inc(chunk_used, 1)
                elif kind == "head":
                    w, j, s = e[2:]
                    to = ("ffn_in", L, 0, 0) if w == 0 else ("proj", L + 1, j)
                    n = PLAN.n0[to] + (j if w == 0 else 0)
                    pre = (L, 1) if w == 0 else (L + 1, 0)
                    dst = A[j if w == 0 else PLAN.acc[to]]
                    if s == 0:
                        if w == 0:
                            pe.wait_ge(free[f"A{j}"], PLAN.acc[to][j])
                        else:
                            unit_free(to)
                        lo_wait(pe, n)
                    m = project(dst, n, [parts(("nrm",) + pre)[s]], H, ready=lambda k: h_wait(pe, *pre, s, k))
                    if s == len(parts(("nrm",) + pre)) - 1:
                        m.then_inc(chunk_used, 1)
                elif kind == "late":
                    unit_free(e)
                    lo_wait(pe, n0)
                    src, K = (H, KT) if e[2] == 0 else ((g_hi, g_lo), BLOCKS[2])
                    project(A[e[3] % 2], n0, [parts(e)[1]], src, K=K).then_inc(chunk_used, 1)
                elif kind == "z":
                    tt = e[2]
                    unit_free(e)
                    read_out(pe, proj(L, "lr", 0))
                    pe.wait_ge(lr_ones, L + 1)
                    pe.wait_ge(wd_in, 16 * (L + 1))
                    pe.matmul(unit_of(e), lrT[0:33, tt * P:(tt + 1) * P], wd[:, :],
                              start=True, stop=True).then_inc(full["z"], 1)
                elif kind == "turn":
                    unit_free(e)
                    j = e[2]
                    src = kT[:, j, :] if j < 2 else vst[:, j % 2, :]
                    read_out(pe, proj(L, *(("k", j) if j < 2 else ("v", j - 2))))
                    for tt in range(TT_ALL):
                        m = pe.transpose(G[tt // 4][:, (tt % 4) * P:(tt % 4 + 1) * P], src[:, tt * P:(tt + 1) * P], ident[:, :])
                    m.then_inc(full["turn"], 1)
                elif kind == "suffix":
                    g, tt = STEPS[e[2]]
                    unit_free(e)
                    read_out(pe, ("z", L, tt))
                    pe.matmul(N[:, 512:512 + KW], mat[:, 512 + g * P:512 + (g + 1) * P], ls[:, tt, g * KW:(g + 1) * KW],
                              start=True, stop=True)
                    for pr in range(2):
                        m = pe.matmul(N[:, 768 + 2 * pr:770 + 2 * pr], ls[:, tt, g * KW + pr * P:g * KW + (pr + 1) * P],
                                      mat[:, 768:770], start=True, stop=True)
                    m.then_inc(full["suffix"], 1)
                elif kind == "dstate":
                    g, tt = STEPS[e[2]]
                    unit_free(e)
                    pe.wait_ge(ku_ready, 12 * L + e[2] + 1)
                    if e[2] == 0:
                        read_out(pe, ("turn", L, 5))
                    for c in range(2):
                        for pr in range(2):
                            for hp in range(2):
                                h, row = 2 * pr + hp, slice(c * 64, c * 64 + 64)
                                m = pe.matmul(G[c][hp * 64:hp * 64 + 64, pr * DV:(pr + 1) * DV],
                                              eu[row, g, h * DK:(h + 1) * DK], vtok[row, tt, h * DV:(h + 1) * DV],
                                              start=True, stop=True)
                    m.then_inc(full["dstate"], 1)
                elif kind == "four":
                    tt = e[2]
                    unit_free(e)
                    read_out(pe, proj(L, "f", 0))
                    read_out(pe, proj(L, "f", 1))
                    for ch in range(2):
                        m = pe.matmul(unit_of(e)[:, ch * 256:(ch + 1) * 256], uF[:, ch, tt * P:(tt + 1) * P], chan[:, :],
                                      start=True, stop=True)
                    m.then_inc(full["four"], 1)
                elif kind == "dft":
                    unit_free(e)
                    lo_wait(pe, n0)
                    if e[2] == 0:
                        for tt in tiles_of(L)[-2:]:
                            read_out(pe, ("four", L, tt))
                    s = n0 % RING
                    ab = [t[:, 0:4, :].rearrange("p a b -> p (a b)") for t in H]
                    ctx_part = e[2] == 4
                    tts = (4, 5) if ctx_part else (e[2],)
                    w = CTX if ctx_part else SEQ
                    for ch in range(2):
                        dst = A[ch][:, SEQ:TOK] if ctx_part else A[ch][:, 0:SEQ]
                        for a, tt in enumerate(tts):
                            for part in range(2):
                                lhs = [t[:, tt * 512 + ch * 256 + part * P:tt * 512 + ch * 256 + (part + 1) * P] for t in ab]
                                o = (2 * a + part) * w
                                first = part == 0 and (a == 0 if ctx_part else e[2] == 0)
                                last = part == 1 and (a == 1 if ctx_part else e[2] == 3)
                                for p, (l, r) in enumerate(((lhs[0], w_hi), (lhs[0], w_lo), (lhs[1], w_hi))):
                                    m = pe.matmul(dst, l, r[:, s, o:o + w], start=(first and p == 0), stop=(last and p == 2))
                    m.then_inc(chunk_used, 1)
                elif kind == "gate":
                    tt, g = e[2], e[3]
                    unit_free(e)
                    read_out(pe, ("z", L, tt))
                    for pr in range(2):
                        m = pe.matmul(G[g][:, pr * 256:(pr + 1) * 256], ls[:, tt, g * KW + pr * P:g * KW + (pr + 1) * P],
                                      mat[:, g * 256:(g + 1) * 256], start=True, stop=True)
                    m.then_inc(full["gate"], 1)
                elif kind == "score":
                    tt = e[2]
                    b = turn(L, tt)
                    unit_free(e)
                    pe.wait_ge(qk_ready, 2 * (nth(L, tt) + 1))
                    for g in range(2):
                        for pr in range(2):
                            for hp in range(2):
                                row = slice(hp * 64, hp * 64 + 64)
                                o = hp * 512 + (g * 2 + pr) * P
                                m = pe.matmul(N[:, o:o + P], E[row, b, g, 1, pr, :], E[row, b, g, 0, pr, :], start=True, stop=True)
                    m.then_inc(full["score"], 1)
                elif kind == "o":
                    tt = e[2]
                    b = turn(L, tt)
                    unit_free(e)
                    pe.wait_ge(mrow_ready, mrows[0] + 1)
                    if nth(L, tt):
                        pe.wait_ge(mod_read, nth(L, tt))
                    read_out(pe, ("score", L, tt))
                    read_out(pe, ("dstate", L, 11))
                    for h in range(HEADS):
                        pr, hp = divmod(h, 2)
                        row = slice(hp * 64, hp * 64 + 64)
                        for g in range(2):
                            pe.matmul(o_at(b, h), vtok[:, tt, h * DV:(h + 1) * DV], Pm[:, b, hp, g, pr, :],
                                      start=(g == 0), stop=False)
                        for g in range(2):
                            for c in range(2):
                                m = pe.matmul(o_at(b, h)[:, c * 64:c * 64 + 64], S[row, g, 2 * tt + c, pr, :],
                                              E[row, b, g, 2, pr, c * 64:c * 64 + 64], start=False, stop=(g == 1 and c == 1))
                    m.then_inc(full["o"], 1)
                elif kind == "msq":
                    b = turn(L, e[2])
                    pe.wait_ge(osq_ready, nth(L, e[2]) + 1)
                    for hp in range(2):
                        m = pe.matmul(A[b][:, hp * 512 + 256:hp * 512 + 512], one_v[:, :], osq[:, hp * 256:(hp + 1) * 256],
                                      start=True, stop=True)
                    m.then_inc(full["msq"], 1)
                elif kind == "wout":
                    read_out(pe, ("dft", L, 0))
                    pe.wait_ge(conv_ready, 2 * (L + 1))

                    def ready(k):
                        if k == 0:
                            pe.wait_ge(ylo_ready, 6 * L + len(tiles_of(L)))

                    with pe.Fori(0, KT // 4, 1) as i:
                        for j in range(4):
                            pe.wait_ge(lo_done, 4 * i + (n0 + j - N_MOD0 + 1))
                            pe.wait_ge(free[f"A{j % 2}"], 2 * i + (PLAN.acc[e][j % 2] + j // 2))
                            project(A[j % 2], n0 + j, [parts(e)[0]], H, ready=ready, first=4).then_inc(chunk_used, 1)
                elif kind == "ffn_in":
                    first = 4 if e[2] == 0 else 0

                    def ffn_chunk(j, i=None):
                        pe.wait_ge(lo_done, (0 if i is None else 4 * i) + (n0 + j - N_MOD0 + 1))
                        pe.wait_ge(free[f"A{j % 2}"], (0 if i is None else 2 * i) + (PLAN.acc[e][j % 2] + j // 2))
                        project(A[j % 2], n0 + j, segments(tokens(L)), H).then_inc(chunk_used, 1)

                    for j in range(2, first):
                        ffn_chunk(j)
                    with pe.Fori(0, (2 * BLOCKS[e[2]] - first) // 4, 1) as i:
                        for j in range(first, first + 4):
                            ffn_chunk(j, i)
                elif kind == "ffn_out":
                    last = 1 + HID * L + sum(BLOCKS[:e[2] + 1])
                    pe.wait_ge(g_ready, last - 1)
                    ranges = segments(tokens(L)) if e[2] < 2 else [parts(e)[0]]

                    def ready(k):
                        if k == BLOCKS[e[2]] - 1:
                            pe.wait_ge(g_ready, last)

                    with pe.Fori(0, KT // 4, 1) as i:
                        for j in range(4):
                            pe.wait_ge(lo_done, 4 * i + (n0 + j - N_MOD0 + 1))
                            pe.wait_ge(free[f"A{j % 2}"], 2 * i + (PLAN.acc[e][j % 2] + j // 2))
                            project(A[j % 2], n0 + j, ranges, (g_hi, g_lo), K=BLOCKS[e[2]],
                                    ready=ready).then_inc(chunk_used, 1)
                elif kind == "mean":
                    unit_free(e)
                    t0, t1, _ = span(e)
                    pe.wait_ge(ssq_ready, sums_before(L, e[2]) + KT * (e[3] + 1))
                    pe.matmul(N[:, 512 * e[3]:512 * e[3] + t1 - t0], one_d[:, :], ssq[:, t0:t1],
                              start=True, stop=True).then_inc(full["mean"], 1)
                elif kind == "sq":
                    s, k = e[3:]
                    t0, t1, _ = span(e)
                    unit_free(e)
                    if SQ[e] == 1:
                        pe.wait_ge(one_in, 16)
                    pe.wait_ge(sq_ready, SQ[e])
                    pe.matmul(N[:, 512 * s:512 * s + t1 - t0], one_d[:, :], sqs[k % 2][:, t0:t1],
                              start=(k == 0), stop=(k == KT - 1)).then_inc(sq_used, 1)

        @block.scalar
        def _(act):
            steps = [0]

            def link(ins):
                steps[0] += 1
                ins.then_inc(act_step, 1)
                act.wait_ge(act_step, steps[0])

            def high(n, i=None, per=4, width=None):
                if n >= N_CHUNKS:
                    return
                r = 16 * ((n - N_MOD0) // RAW + 1)
                act.wait_ge(raw_in[n % RAW], r if i is None else (16 * per // RAW) * i + r)
                width = width or (WIDTH[n] if i is None else 1024)
                src = raw[:, n % RAW, 0:width]
                if n >= N_MOD0 + RING:
                    act.wait_ge(chunk_used, n - RING + 1 if i is None else per * i + (n - RING + 1))
                act.activation(w_hi[:, n % RING, 0:width], src, ACT.Copy).then_inc(hi_done, 1)

            def normalise(e, used):
                t0, t1, _ = span(e)
                u, b = PLAN.before[used][0]
                act.activation(rstd[:, t0:t1], N[:, 512 * e[3]:512 * e[3] + t1 - t0], ACT.Ln,
                               bias=eps[:, 0:1]).then_inc(free[u], 1)
                act.wait_ge(free[u], b + 1)
                act.activation(rstd[:, t0:t1], rstd[:, t0:t1], ACT.Exp, scale=-0.5).then_inc(rstd_ready, 1)

            act.wait_ge(par_in, 16)
            act.activation(csil[:, :, :], par[:, DEPTH * PCOLS:DEPTH * PCOLS + 16].rearrange("p (v k) -> p k v", v=2),
                           ACT.Silu).then_inc(csil_ready, 1)
            act.wait_ge(csil_ready, 1)
            act.wait_ge(c4_zero, 1)
            act.activation(c4[:, :, 0:2], csil[:, :, :], ACT.Copy).then_inc(c4hi_ready, 1)
            act.dma_start(posr[:, :, :], pos_row).then_inc(x_in, 16)
            act.dma_start(posc[:, :, :], pos_col).then_inc(x_in, 16)
            for dst, src in ((mask, masks), (mat, mats), (chan, wide[:, 0:256]),
                             (one_v, wide[:, 384:512]), (ident, wide[:, 512:640])):
                act.dma_start(dst[:], src).then_inc(consts_in, 16)
            act.dma_start(wd[:, :], wdec[:, 0, :]).then_inc(wd_in, 16)
            act.dma_start(sel[:, :], wide[0:4, 640:642]).then_inc(sel_in, 16)
            act.preload_act_table_set(LN_SET)
            act.wait_ge(eps_set, 1)

            for e in ORDER:
                kind, L = e[0], e[1]
                n0, nc_ = PLAN.n0[e], len(chunks_of(e))
                if kind == "start" and e[2]:
                    for h in range(2):
                        act.wait_ge(chunk_used, 8 * (h + 1))
                        act.activation(mrow0[:, h * 1024:(h + 1) * 1024], A[h][0:2, :], ACT.Copy).then_inc(free[f"A{h}"], 1)
                    for j in range(RAW):
                        high(N_MOD0 + j)
                elif kind == "mod":
                    act.wait_ge(chunk_used, n0 + nc_)
                    act.activation(mrow[:, 0:nc_ * P], N[0:4, 256:256 + nc_ * P], ACT.Copy).then_inc(mrow_ready, 1)
                    for j in range(nc_):
                        high(n0 + j + RING)
                elif kind == "fill":
                    act.wait_ge(chunk_used, n0 + nc_)
                    act.activation(frow[:, 0:nc_ * P], A[turn(L, e[2])][0:4, 0:nc_ * P], ACT.Copy).then_inc(mrow_ready, 1)
                    high(n0 + RING)
                elif kind == "proj":
                    name, j, _ = W_IN[e[2]]
                    T = tokens(L, name)
                    if e[2] == 0:
                        if L:
                            act.dma_start(wd[:, :], wdec[:, L, :]).then_inc(wd_in, 16)
                        act.wait_ge(x_kept, 64 * (L + 1))
                    if name == "u":
                        high(n0 + RING)
                        continue
                    src = A[PLAN.acc[e]]
                    act.wait_ge(chunk_used, n0 + 1)
                    if name == "v" and j >= 2:
                        act.wait_ge(full["turn"], 6 * L + j + 1)
                    dst = {"lr": lrT[0:32, 0:T], "k": kT[:, j % 2, 0:T], "v": vst[:, j % 2, 0:T], "q": qT[:, j % 2, 0:T],
                           "f": uF[:, j % 2, 0:T], "c": cgz[:, j % 2, 0:T], "b": bg[:, j % 2, 0:T], "r": r_s[:, j, 0:T]}[name]
                    rows = 32 if name == "lr" else P
                    if name == "r":
                        m = act.activation(dst, src[0:rows, 0:T], ACT.Silu)
                    else:
                        m = act.activation(dst, src[0:rows, 0:T], ACT.Copy, scale=DK ** -0.5 if name == "q" else 1.0)
                    m.then_inc(free[f"A{PLAN.acc[e]}"], 1)
                    high(n0 + RING)
                    if name == "lr" or (name, j) == ("r", 3):
                        act.preload_act_table_set(LN_SET)
                elif kind == "z":
                    q = TT_ALL * L + e[2]
                    b = e[2] % 2
                    act.wait_ge(zneg_ready, q + 1)
                    link(act.activation(zs[:, b, :], zs[:, b, :], ACT.Exp))
                    act.activation(zs[:, b, :], zs[:, b, :], ACT.Ln, bias=1.0).then_inc(zln_ready, 1)
                elif kind == "turn":
                    j = e[2]
                    act.wait_ge(full["turn"], PLAN.full[e])
                    dst = ktok[:, :, j * P:(j + 1) * P] if j < 2 else vtok[:, :, (j - 2) * P:(j - 1) * P]
                    for half, (a, b) in enumerate(((0, 4), (4, 6))):
                        m = act.activation(dst[:, a:b, :], G[half][:, 0:(b - a) * P].rearrange("p (a b) -> p a b", b=P), ACT.Copy)
                        m.then_inc(free[f"G{half}"], 1)
                elif kind == "suffix":
                    g, tt = STEPS[e[2]]
                    act.wait_ge(full["suffix"], PLAN.full[e])
                    act.activation(eu[:, g, :], N[:, 512:512 + KW], ACT.Exp)
                    m = act.activation(dec[:, e[2], :], N[:, 768:772], ACT.Exp)
                    m.then_inc(free["N1"], 1)
                elif kind == "four":
                    tt = e[2]
                    act.wait_ge(full["four"], PLAN.full[e])
                    ab = h_hi[:, 0:4, :].rearrange("p a b -> p (a b)")
                    act.activation(ab[:, tt * 512:(tt + 1) * 512], unit_of(e), ACT.Copy).then_inc(ab_hi, 1)
                elif kind == "dft":
                    end = e[2] == (3 if L else 4)
                    if not end:
                        high(n0 + RING)
                    if e[2] == 0:
                        for j in range(2):
                            act.wait_ge(conv_f, 2 * L + j + 1)
                            act.activation(h_hi[:, 6 + j, 0:tokens(L)], bg[:, j, 0:tokens(L)], ACT.Copy).then_inc(conv_hi, 1)
                    if end:
                        act.wait_ge(chunk_used, n0 + 1)
                        for ch in range(2):
                            act.activation(h_hi[:, 4 + ch, 0:tokens(L)], A[ch][:, 0:tokens(L)], ACT.Copy).then_inc(four_hi, 1)
                        high(n0 + RING)
                elif kind == "gate":
                    tt, g = e[2], e[3]
                    b = turn(L, tt)
                    act.wait_ge(full["gate"], PLAN.full[e])
                    src = G[g][:, :].rearrange("p (r w t) -> p r w t", r=2, w=2)
                    if nth(L, tt) - 6 * L >= 2:
                        act.wait_ge(full["o"], 6 * L + tiles_of(L).index(tt) - 1)
                    elif tiles_of(L).index(tt) == 0:
                        read_out(act, ("dstate", L, 11))
                        act.wait_ge(conv_f, 2 * (L + 1))
                    act.activation(E[:, b, g, 0, :, :], src[:, :, 1, :], ACT.Exp)
                    act.activation(E[:, b, g, 1, :, :], src[:, :, 1, :], ACT.Exp, scale=-1.0)
                    m = act.activation(E[:, b, g, 2, :, :], src[:, :, 0, :], ACT.Exp)
                    m.then_inc(free[f"G{g}"], 1)
                elif kind == "o":
                    b = turn(L, e[2])
                    f = ("fill", L, e[2])
                    last_tile = e[2] == tiles_of(L)[-1]
                    if not last_tile:
                        for j in range(1, len(chunks_of(f))):
                            high(PLAN.n0[f] + j + RING)
                    act.wait_ge(full["o"], PLAN.full[e])
                    if tiles_of(L).index(e[2]) >= 1:
                        act.wait_ge(full["msq"], nth(L, e[2]))
                    act.activation(osq[:, :].rearrange("p (q r) -> p q r", q=2), o_all(b, 0), ACT.Square).then_inc(osq_ready, 1)
                    if last_tile:
                        for j in range(1, len(chunks_of(f))):
                            high(PLAN.n0[f] + j + RING)
                elif kind == "msq":
                    b = turn(L, e[2])
                    q = nth(L, e[2])
                    act.wait_ge(full["msq"], PLAN.full[e])
                    if tiles_of(L).index(e[2]) >= 2:
                        act.wait_ge(ylo_ready, q - 1)
                    flat = rb[:, b, :, :].rearrange("p (q r) t -> p q (r t)", q=2)
                    link(act.activation(flat, o_all(b, 1), ACT.Ln, bias=eps[:, 0:1]))
                    act.activation(flat, flat, ACT.Exp, scale=-0.5).then_inc(orstd_ready, 1)
                    act.wait_ge(yg_ready, q + 1)
                    act.activation(y_all(h_hi, e[2]), rb[:, b, :, :].rearrange("p (q r) t -> p q r t", q=2), ACT.Copy).then_inc(yhi_ready, 1)
                elif kind == "wout":
                    act.wait_ge(mod_turned, 3 + 2 * L)
                    act.wait_ge(ylo_ready, 6 * L + len(tiles_of(L)))
                    for k in range(0, KT, 4):
                        act.dma_start(x[:, k:k + 4, :], x_keep[:, k:k + 4, :]).then_inc(x_back, 16)
                    with act.Fori(0, KT // 4, 1) as i:
                        for j in range(4):
                            high(n0 + j + RING, i)
                elif kind == "ffn_in":
                    T, nb = tokens(L), BLOCKS[e[2]]
                    p0 = HID * L + e[3]
                    if e[2] == 0:
                        act.preload_act_table_set("silu_and_others")
                    with act.Fori(0, nb // 2, 1) as i:
                        for q in range(2):
                            c = n0 + 2 * q
                            high(c + RING, i)
                            act.wait_ge(chunk_used, 4 * i + (c + 1))
                            act.wait_ge(g_ready, 2 * i + (p0 + q + 1))
                            act.activation(sil[:, 0:T], A[0][:, 0:T], ACT.Silu).then_inc(free["A0"], 1)
                            high(c + 1 + RING, i)
                            act.wait_ge(free["A1"], 2 * i + (PLAN.acc[e][1] + q + 1))
                            act.activation(g_hi[:, bass.ds(2 * i + q, 1), 0:T], sqb[:, 0:1, 0:T], ACT.Copy).then_inc(ghi_ready, 1)
                elif kind == "ffn_out" and n0 + KT + RING > N_CHUNKS:
                    for j in range(KT):
                        high(n0 + j + RING)
                elif kind == "ffn_out":
                    with act.Fori(0, KT // 4, 1) as i:
                        for j in range(4):
                            high(n0 + j + RING, i, width=WIDTH[n0] if e[2] == 2 else None)
                elif kind == "ahead":
                    high(PLAN.n0[("late",) + e[1:]] + RING)
                elif kind == "mean":
                    if e[2] and e[3] == 0:
                        act.preload_act_table_set(LN_SET)
                    act.wait_ge(full["mean"], PLAN.full[e])
                    normalise(e, e)
                elif kind == "sq":
                    s, k = e[3:]
                    t0, t1, _ = span(e)
                    first = e[1] == 0 and e[2] == 0
                    if first and s:
                        act.wait_ge(ctx_in, 16)
                    act.wait_ge(xnew_ready, k + 1 if first else KT + RES[before_pre(e)])
                    if SQ[e] > 2:
                        act.wait_ge(sq_used, SQ[e] - 2)
                    act.activation(sqs[k % 2][:, t0:t1], x[:, k, t0:t1], ACT.Square).then_inc(sq_ready, 1)
                elif kind == "rstd":
                    act.wait_ge(sq_used, SQ[("sq",) + e[1:] + (KT - 1,)])
                    normalise(e, ("sq",) + e[1:] + (0,))
                elif kind == "nrm":
                    k, (t0, t1, v) = e[4], span(e)
                    act.wait_ge(haff_ready, NRM[e])
                    dst = h_hi if k in LOW_V else y
                    m = act.activation(dst[:, k, t0:t1], y[:, k, t0:t1], ACT.Identity, bias=coef[:, L, 3 * e[2], k, v:v + 1])
                    if k not in LOW_V:
                        link(m)
                        m = act.activation(h_hi[:, k, t0:t1], y[:, k, t0:t1], ACT.Copy)
                    m.then_inc(hhi_ready, 1)
                elif e == ("head", -1, 1, 0, 0):
                    for j in range(RAW, RING):
                        high(N_MOD0 + j)
                elif kind == "keep":
                    s = e[2]
                    t0, t1, _ = parts(("nrm", L, 0))[s]
                    if L:
                        act.wait_ge(xnew_ready, KT + RES[("res", 0, 1, s, KT - 1)])
                    for k in range(0, KT, 4):
                        act.dma_start(x_keep[:, k:k + 4, t0:t1], x[:, k:k + 4, t0:t1]).then_inc(x_kept, 16)
                elif kind == "send":
                    for k in range(0, KT, 2):
                        act.wait_ge(xnew_ready, KT + RES[("res", 1, 1, 0, k + 1)])
                        act.dma_start(out[:, k:k + 2, :], x[:, k:k + 2, 0:SEQ]).then_inc(out_sent, 16)
                    act.wait_ge(out_sent, 16 * (KT // 2))

        @block.vector
        def _(dve):
            steps = [0]

            def link(ins):
                steps[0] += 1
                ins.then_inc(dve_step, 1)
                dve.wait_ge(dve_step, steps[0])

            dve.memset(eps[:, :], EPS).then_inc(eps_set, 1)
            dve.memset(c4[:, :, :].bitcast(F32), 0.0).then_inc(c4_zero, 1)
            dve.memset(coef[:, 0, 0, 0, :], 0.0).then_inc(g_ready, 1)
            dve.wait_ge(c4hi_ready, 1)
            dve.tensor_tensor(c4[:, :, 2:4], csil[:, :, :], c4[:, :, 0:2].bitcast(F32), ALU.subtract).then_inc(c_ready, 1)

            def gather(L, a, b, src):
                src = src.rearrange("p (m v) -> p m v", v=2)
                for v in range(2):
                    m = dve.tensor_tensor(modT[:, a:b, v], src[:, :, v], col(L, PB + a, b - a), ALU.add)
                return m

            def coefficients(L, a, b):
                for w in range(a // KT, b // KT):
                    src = modT[:, w * KT:(w + 1) * KT, :]
                    for v in range(2):
                        if w % 3 == 0:
                            m = dve.tensor_copy(coef[:, L, w, :, v], src[:, :, v])
                        else:
                            gain = col(L, PG + KT * {1: 0, 2: 1, 4: 2, 5: 3}[w], KT)
                            m = dve.scalar_tensor_tensor(coef[:, L, w, :, v], src[:, :, v], 1.0 if w % 3 == 1 else 0.0,
                                                         gain, ALU.add, ALU.mult)
                m.then_inc(coef_step, 1)

            for e in ORDER:
                kind, L = e[0], e[1]
                n0 = PLAN.n0[e]
                if kind == "start" and e[2] == 0:
                    dve.wait_ge(x_in, 48)
                    for k in range(KT):
                        p = posr[:, k, :].rearrange("p (r c) -> p r c", c=1).to_broadcast([P, 8, 64]) if k < 4 else \
                            posc[:, k - 4:k - 3, :].to_broadcast([P, 8, 64])
                        xk = x[:, k, 0:SEQ].rearrange("p (r c) -> p r c", r=8)
                        dve.tensor_tensor(xk, xk, p, ALU.add).then_inc(xnew_ready, 1)
                elif kind == "start":
                    dve.wait_ge(mod_turned, 1)
                    gather(0, 0, 16, G[0][:, 0:32]).then_inc(free["G0"], 1)
                    dve.wait_ge(free["G0"], 1)
                    coefficients(0, 0, 16)
                    dve.wait_ge(coef_step, 1)
                elif kind == "modend":
                    dve.wait_ge(mod_turned, 2 + 2 * L)
                    a, b = MOD_BETWEEN[L]
                    gather(L, a, b, N[:, 2 * a:2 * b]).then_inc(free["N0"], 1)
                    dve.wait_ge(free["N0"], PLAN.before[("mod", L, a, 1)][0][1] + 1)
                    coefficients(L, 16, 32 if L else 48)
                    dve.wait_ge(coef_step, 2 + 2 * L)
                elif kind == "fill":
                    m, n = fill_of(L, e[2])
                    dve.wait_ge(mrow_ready, ROWS[e])
                    if e[2] != tiles_of(L)[0]:
                        p = before_fill(L, e[2])
                        gather(1, m - p, m, A[turn(L, e[2])][:, 896:896 + 2 * p]).then_inc(mod_read, 1)
                elif kind == "coef":
                    m, n = fill_of(L, tiles_of(L)[-1])
                    dve.wait_ge(mod_turned, 3 + 2 * L)
                    gather(1, m, m + n, N[:, 0:2 * n]).then_inc(mod_read, 1)
                    dve.wait_ge(mod_read, 6 * L + len(tiles_of(L)))
                    coefficients(1, *COEFS[L])
                    dve.wait_ge(coef_step, 3 + 2 * L)
                elif kind == "proj":
                    name, j, _ = W_IN[e[2]]
                    T = tokens(L, name)
                    if e[2] == 0:
                        dve.wait_ge(x_kept, 64 * (L + 1))
                        dve.memset(lrT[32:33, :], 1.0).then_inc(lr_ones, 1)
                        dve.memset(S[:, 0, 8, :, :], 0.0)
                        link(dve.memset(S[:, 1, 11, :, :], 0.0))
                    if name == "u":
                        read_out(dve, proj(L, "c", j))
                        dve.wait_ge(chunk_used, n0 + 1)
                        m = dve.tensor_tensor(cgz[:, j, 0:T], cgz[:, j, 0:T], A[PLAN.acc[e]][:, 0:T], ALU.mult)
                        m.then_inc(free[f"A{PLAN.acc[e]}"], 1)
                    if name == "b":
                        read_out(dve, proj(L, "u", j))
                        for t0, t1, _ in segments(T):
                            tap = [col(L, PCW + 2 * w + j) for w in range(3)]
                            link(dve.tensor_scalar(cv[:, t0:t1], cgz[:, j, t0:t1], tap[1], col(L, PCB + j), ALU.mult, ALU.add))
                            link(dve.scalar_tensor_tensor(cv[:, t0 + 1:t1], cgz[:, j, t0:t1 - 1], tap[0], cv[:, t0 + 1:t1],
                                                          ALU.mult, ALU.add))
                            link(dve.scalar_tensor_tensor(cv[:, t0:t1 - 1], cgz[:, j, t0 + 1:t1], tap[2], cv[:, t0:t1 - 1],
                                                          ALU.mult, ALU.add))
                        read_out(dve, proj(L, "b", j))
                        dve.tensor_tensor(bg[:, j, 0:T], bg[:, j, 0:T], cv[:, 0:T], ALU.mult).then_inc(conv_f, 1)
                elif kind == "z":
                    tt = e[2]
                    b, q = tt % 2, TT_ALL * L + tt
                    dve.wait_ge(full["z"], PLAN.full[e])
                    link(dve.tensor_scalar(zs[:, b, :], unit_of(e), -1.0, None, ALU.mult))
                    dve.tensor_tensor(zs[:, b, :], zs[:, b, :], unit_of(e), ALU.min).then_inc(zneg_ready, 1)
                    dve.wait_ge(zln_ready, q + 1)
                    m = dve.scalar_tensor_tensor(ls[:, tt, :], unit_of(e), 0.0, zs[:, b, :], ALU.min, ALU.subtract)
                    m.then_inc(free[PLAN.before[e][0][0]], 1)
                elif kind == "suffix":
                    g, tt = STEPS[e[2]]
                    if e[2] == 0:
                        read_out(dve, ("turn", L, 1))
                    read_out(dve, e)
                    dve.tensor_tensor(eu[:, g, :], eu[:, g, :], ktok[:, tt, :], ALU.mult).then_inc(ku_ready, 1)
                elif kind == "dstate":
                    g, tt = STEPS[e[2]]
                    dve.wait_ge(full["dstate"], PLAN.full[e])
                    order = (0, 1) if g == 0 else (1, 0)
                    for c in order:
                        at = 2 * tt + c
                        after = {11: 0, 7: None}.get(at, at + 1) if g == 0 else {8: 7, 0: None}.get(at, at - 1)
                        if after is None:
                            continue
                        final = (g, at) in ((0, 6), (1, 1))
                        for pr in range(2):
                            m = dve.scalar_tensor_tensor(S[:, g, after, pr, :], S[:, g, at, pr, :],
                                                         dec[:, e[2], 2 * pr + c:2 * pr + c + 1],
                                                         G[c][:, pr * DV:(pr + 1) * DV], ALU.mult, ALU.add)
                            if pr == 1:
                                m.then_inc(free[f"G{c}"], 1)
                            elif final:
                                m.then_inc(free[f"G{1 - c}"], 1)
                        dve.wait_ge(free[f"G{c}"], PLAN.before[e][c][1] + 1)
                elif kind == "four":
                    tt = e[2]
                    q = 6 * L + tiles_of(L).index(tt)
                    ab = [t[:, 0:4, :].rearrange("p a b -> p (a b)")[:, tt * 512:(tt + 1) * 512] for t in (h_hi, h_lo)]
                    dve.wait_ge(ab_hi, q + 1)
                    m = dve.tensor_tensor(ab[1], unit_of(e), ab[0].bitcast(F32), ALU.subtract)
                    m.then_inc(free[PLAN.before[e][0][0]], 1)
                elif kind == "dft":
                    T = tokens(L)
                    if e[2] == 0:
                        for j in range(2):
                            dve.wait_ge(conv_hi, 2 * L + j + 1)
                            dve.tensor_tensor(h_lo[:, 6 + j, 0:T], bg[:, j, 0:T], h_hi[:, 6 + j, 0:T].bitcast(F32),
                                              ALU.subtract).then_inc(conv_ready, 1)
                    if e[2] == (3 if L else 4):
                        for ch in range(2):
                            dve.wait_ge(four_hi, 2 * L + ch + 1)
                            m = dve.tensor_tensor(h_lo[:, 4 + ch, 0:T], A[ch][:, 0:T], h_hi[:, 4 + ch, 0:T].bitcast(F32),
                                                  ALU.subtract)
                            m.then_inc(free[f"A{ch}"], 1)
                elif kind == "gate":
                    tt, g = e[2], e[3]
                    b = turn(L, tt)
                    if tiles_of(L).index(tt) == 0 and g == 0:
                        link(dve.memset(Pm[:, :, :, :, :, :], 0.0))
                    read_out(dve, e)
                    q_, k_ = qT[:, :, tt * P:(tt + 1) * P], kT[:, :, tt * P:(tt + 1) * P]
                    dve.tensor_tensor(E[:, b, g, 0, :, :], E[:, b, g, 0, :, :], q_, ALU.mult)
                    dve.tensor_tensor(E[:, b, g, 1, :, :], E[:, b, g, 1, :, :], k_, ALU.mult)
                    dve.tensor_tensor(E[:, b, g, 2, :, :], E[:, b, g, 2, :, :], q_, ALU.mult).then_inc(qk_ready, 1)
                elif kind == "score":
                    b = turn(L, e[2])
                    dve.wait_ge(full["score"], PLAN.full[e])
                    if tiles_of(L).index(e[2]) >= 2:
                        dve.wait_ge(full["o"], nth(L, e[2]) - 1)
                    for hp in range(2):
                        for g in range(2):
                            m = dve.copy_predicated(Pm[:, b, hp, g, :, :],
                                                    mask[:, g:g + 1, :].to_broadcast([P, 2, P]),
                                                    N[:, hp * 512 + g * 256:hp * 512 + (g + 1) * 256].rearrange("p (r t) -> p r t", r=2))
                        m.then_inc(free[f"N{hp}"], 1)
                elif kind == "msq":
                    tt = e[2]
                    b, q = turn(L, tt), nth(L, tt)
                    dve.wait_ge(orstd_ready, q + 1)
                    flat = rb[:, b, :, :].rearrange("p (q r) t -> p q (r t)", q=2)
                    m = dve.tensor_tensor(flat, o_all(b, 0), flat, ALU.mult)
                    m.then_inc(free[f"A{b}"], 1)
                    read_out(dve, ("o", L, tt))
                    for h in range(HEADS):
                        at = (h % 2) * 2 + h // 2
                        m = dve.scalar_tensor_tensor(rb[:, b, at, :], rb[:, b, at, :], col(L, PGN + h),
                                                     r_s[:, h, tt * P:(tt + 1) * P], ALU.mult, ALU.mult)
                    m.then_inc(yg_ready, 1)
                    dve.wait_ge(yhi_ready, q + 1)
                    dve.tensor_tensor(y_all(h_lo, tt), rb[:, b, :, :].rearrange("p (q r) t -> p q r t", q=2),
                                      y_all(h_hi, tt).bitcast(F32), ALU.subtract).then_inc(ylo_ready, 1)
                elif kind in ("wout", "ffn_out"):
                    last = kind == "wout" or e[2] == 2
                    add = kind == "ffn_out" and e[2] > 0
                    t0, t1, _ = parts(e)[0] if last else (0, tokens(L), 0)
                    if last:
                        link(dve.memset(ssq[:, 0:tokens(L)], 0.0))
                    for j in range(2):
                        dve.wait_ge(free[f"A{j}"], PLAN.acc[e][j])
                    base = steps[0]
                    sums = sums_before(L, int(kind == "ffn_out"))
                    with dve.Fori(0, KT // 4, 1) as i:
                        for j in range(4):
                            ym = y[:, bass.ds(4 * i + j, 1), t0:t1]
                            src = A[j % 2][:, t0:t1].rearrange("p (a t) -> p a t", a=1)
                            dve.wait_ge(chunk_used, 4 * i + (n0 + j + 1))
                            m = dve.tensor_tensor(ym, src, ym, ALU.add) if add else dve.tensor_copy(ym, src)
                            m.then_inc(free[f"A{j % 2}"], 1)
                            if last:
                                dve.wait_ge(free[f"A{j % 2}"], 2 * i + (PLAN.acc[e][j % 2] + j // 2 + 1))
                                s3 = sqb[:, 0:1, t0:t1]
                                dve.tensor_tensor(s3, ym, ym, ALU.mult).then_inc(dve_step, 1)
                                dve.wait_ge(dve_step, 4 * i + (base + j + 1))
                                q3 = sqb[:, 1:2, t0:t1]
                                dve.tensor_tensor(q3, q3, s3, ALU.add).then_inc(ssq_ready, 1)
                                dve.wait_ge(ssq_ready, 4 * i + (sums + j + 1))
                    steps[0] += KT if last else 0
                elif kind == "take":
                    w, m = e[2:]
                    t0, t1, _ = parts(e)[1]
                    late = ("late", L, w, m)
                    ym, src = y[:, m, t0:t1], A[m % 2][:, t0:t1]
                    dve.wait_ge(chunk_used, PLAN.n0[late] + 1)
                    q = dve.tensor_tensor(ym, src, ym, ALU.add) if w else dve.tensor_copy(ym, src)
                    q.then_inc(free[f"A{m % 2}"], 1)
                    read_out(dve, late)
                    link(dve.tensor_tensor(sil[:, t0:t1], ym, ym, ALU.mult))
                    dve.wait_ge(ssq_ready, sums_before(L, w) + KT + m)
                    dve.tensor_tensor(ssq[:, t0:t1], ssq[:, t0:t1], sil[:, t0:t1], ALU.add).then_inc(ssq_ready, 1)
                elif kind == "ffn_in":
                    T, nb = tokens(L), BLOCKS[e[2]]
                    p0 = HID * L + e[3]
                    with dve.Fori(0, nb // 2, 1) as i:
                        for q in range(2):
                            dve.wait_ge(free["A0"], 2 * i + (PLAN.acc[e][0] + q + 1))
                            dve.wait_ge(chunk_used, 4 * i + (n0 + 2 * q + 2))
                            dve.tensor_tensor(sil[:, 0:T], sil[:, 0:T], A[1][:, 0:T], ALU.mult).then_inc(free["A1"], 1)
                            dve.wait_ge(ghi_ready, 2 * i + (p0 + q + 1))
                            gp = bass.ds(2 * i + q, 1)
                            dve.tensor_tensor(g_lo[:, gp, 0:T], sqb[:, 0:1, 0:T], g_hi[:, gp, 0:T].bitcast(F32),
                                              ALU.subtract).then_inc(g_ready, 1)
                elif kind == "res":
                    w, s, k = e[2:]
                    t0, t1, v = span(e)
                    if k == 0:
                        if w == 0:
                            dve.wait_ge(x_back, 32 * (L + 1))
                        dve.wait_ge(rstd_ready, RSTD[("mean", L, w, s)])
                    if e in YN:
                        dve.wait_ge(yn_ready, YN[e])
                    else:
                        link(dve.tensor_tensor(y[:, k, t0:t1], y[:, k, t0:t1], rstd[:, t0:t1], ALU.mult))
                    dve.scalar_tensor_tensor(x[:, k, t0:t1], y[:, k, t0:t1], coef[:, L, 3 * w + 2, k, v:v + 1],
                                             x[:, k, t0:t1], ALU.mult, ALU.add).then_inc(xnew_ready, 1)
                elif kind == "nrm":
                    w, s, k = e[2:]
                    t0, t1, v = span(e)
                    if k == 0:
                        dve.wait_ge(rstd_ready, RSTD[("rstd", L, w, s)])
                    dve.scalar_tensor_tensor(y[:, k, t0:t1], x[:, k, t0:t1], coef[:, L, 3 * w + 1, k, v:v + 1],
                                             rstd[:, t0:t1], ALU.mult, ALU.mult).then_inc(haff_ready, 1)
                    for j in ((k - 1, k) if k == KT - 1 else (k - 1,)):
                        if j in LOW_V:
                            dve.wait_ge(hhi_ready, NRM[("nrm", L, w, s, j)])
                            dve.scalar_tensor_tensor(h_lo[:, j, t0:t1], y[:, j, t0:t1], coef[:, L, 3 * w, j, v:v + 1],
                                                     h_hi[:, j, t0:t1].bitcast(F32), ALU.add,
                                                     ALU.subtract).then_inc(hlo_ready_v, 1)


def stream_layout(a):
    out = np.zeros((N_CHUNKS, P, 1024), np.float32)
    ang = lambda n: 2 * np.pi * (np.outer(np.arange(n), np.arange(n)) % n) / n
    dft = {}
    for n in (SEQ, CTX):
        s = 1.0 / np.sqrt(n * 64.0)
        dft[n] = (np.cos(ang(n)) * s, -np.sin(ang(n)) * s)

    def tile(w, k0, K, m):
        return w[k0 * P:(k0 + K) * P, m:m + P].reshape(K, P, -1).transpose(1, 0, 2)

    for e in ORDER:
        for i, c in enumerate(chunks_of(e)):
            dst = out[PLAN.n0[e] + i]
            if c[0] == "dft":
                if c[1] < 4:
                    dst[:, 0:512], dst[:, 512:] = (t[c[1] * P:(c[1] + 1) * P] for t in dft[SEQ])
                else:
                    for s in range(2):
                        for q in range(2):
                            dst[:, (2 * s + q) * CTX:(2 * s + q + 1) * CTX] = dft[CTX][q][s * P:(s + 1) * P]
                continue
            name = {"mod": "w_mod", "in": "w_in", "out": "w_out", "fin": "w_ffn_in", "fout": "w_ffn_out"}[c[0]]
            w = a[name][c[1]]
            k0, K = (c[3], c[4]) if c[0] == "fout" else (0, KT)
            m = c[2] if c[0] == "in" else c[2] * P
            dst[:, 0:K * P] = tile(w, k0, K, m).reshape(P, K * P)
    return out


def constants():
    t = np.arange(P)
    same = (t[:, None] // CHUNK) == (t[None, :] // CHUNK)
    s_, t_ = t[:, None] % CHUNK, t[None, :] % CHUNK
    half = CHUNK // 2
    before, after = same & (s_ <= t_), same & (s_ >= t_)
    mats = [before, before * 1.0 - (same & (s_ < half)), after, after * 1.0 - (same & (s_ >= half)),
            same & (s_ > t_), same & (s_ < t_), np.stack([t < CHUNK, t >= CHUNK], 1)]
    mats = np.concatenate([m.astype(np.float32) for m in mats], 1) / 16.0
    masks = np.stack([before, after], 1).astype(np.int32)
    a = 2 * np.pi * (np.outer(np.arange(64), np.arange(64)) % 64) / 64
    chan = np.zeros((P, 2 * P))
    for g in range(2):
        r = slice(g * 64, g * 64 + 64)
        chan[r, g * 64:g * 64 + 64] = np.cos(a)
        chan[r, P + g * 64:P + g * 64 + 64] = np.sin(a)
    wide = np.concatenate([chan, np.full((P, P), 1.0 / D), np.full((P, P), 1.0 / DV), np.eye(P),
                           np.tile(np.eye(2), (64, 1))], 1)
    rows = SEQ // 64
    row, c = np.repeat(np.arange(rows, dtype=np.float32), 64), np.tile(np.arange(64, dtype=np.float32), rows)
    quarter = D // 4
    f = (1.0 / (np.float32(10000.0) ** (np.arange(quarter, dtype=np.float32) / np.float32(quarter)))).astype(np.float32)
    enc = lambda p: np.concatenate([np.sin(p[:, None] * f[None]), np.cos(p[:, None] * f[None])], -1)
    pos = np.concatenate([enc(row), enc(c)], -1).astype(np.float32)
    return masks, mats.astype(np.float32), wide.astype(np.float32), pos


def feature_major(a):
    return np.ascontiguousarray(a.T.reshape(-1, P, a.shape[0]).transpose(1, 0, 2))


def kernel(**inputs):
    import numpy as _np
    import concourse.bacc as _bacc
    from concourse import mybir as _mybir
    from concourse.bass_utils import run_bass_kernel_spmd as _run

    a = {k: _np.asarray(v) for k, v in inputs.items()}
    masks, mats, wide, pos = constants()
    column = lambda v: v.reshape(-1, P).T
    cols = []
    for L in range(DEPTH):
        cols += [column(a[k][L]) for k in ("b_mod", "g_mix_pre", "g_mix_post", "g_ffn_pre", "g_ffn_post", "conv_w",
                                           "conv_b", "gla_norm_w")]
    cols += [column(a["c"][0]), column(a["c_ctx"])]
    wdec = _np.zeros((33, DEPTH, 512), _np.float32)
    for L in range(DEPTH):
        wdec[0:16, L, 0:256], wdec[32, L, 0:256] = a["w_dec_f"][L], a["b_dec_f"][L]
        wdec[16:32, L, 256:512], wdec[32, L, 256:512] = a["w_dec_b"][L], a["b_dec_b"][L]
    arrays = {
        "stream": stream_layout(a),
        "xT": _np.concatenate([feature_major(a["x"][0]), feature_major(a["ctx"][0])], 2),
        "pos_row": feature_major(pos[::64, 0:D // 2]),
        "pos_col": feature_major(pos[0:64, D // 2:]),
        "cols": _np.concatenate(cols, 1),
        "wdec": wdec,
        "masks": masks,
        "mats": mats,
        "wide": wide,
    }
    arrays = {k: _np.ascontiguousarray(v) for k, v in arrays.items()}
    nc = _bacc.Bacc("TRN2", target_bir_lowering=False, num_devices=1)
    args = [nc.dram_tensor(k, v.shape, _mybir.dt.from_np(v.dtype), kind="ExternalInput").ap() for k, v in arrays.items()]
    args.append(nc.dram_tensor("x_keep", (P, KT, TOK), F32, kind="Internal").ap())
    args.append(nc.dram_tensor("out_0_dram", (P, KT, SEQ), F32, kind="ExternalOutput").ap())
    bass_hybrid_block(nc, *args)
    r = _run(nc, [arrays], core_ids=[0])
    got = r.results[0]["out_0_dram"]
    return _np.ascontiguousarray(got.transpose(1, 0, 2).reshape(D, SEQ).T)[None]
```
